# Optimizing a Trainium2 kernel written in Bass

```python
import math
import jax
import jax.numpy as jnp
from jax import lax
import numpy as np

D_MODEL = 1024
BATCH = 1
SEQ = 256
DEPTH = 2

CHUNK = 64
HEAD_DIM = 64
BLOCK_Q = 128
EPS = 1e-6

A_HEADS = 8
A_KV_HEADS = 2
WINDOW = 128
WINDOW_CHUNKS = WINDOW // CHUNK
B_HEADS = 8
C_HEADS = 8
N_BRANCHES = 3

A_Q = A_HEADS * HEAD_DIM
A_KV = A_KV_HEADS * HEAD_DIM
B_W = B_HEADS * HEAD_DIM
C_W = C_HEADS * HEAD_DIM
IN_SIZES = (A_Q, A_KV, A_KV, B_W, B_W, B_W, B_HEADS, C_W, C_W, C_W, N_BRANCHES * D_MODEL)
IN_COLS = sum(IN_SIZES)
FORGET_OFF = A_Q + 2 * A_KV + 3 * B_W

PEER_HEADS = 8
PEER_NKEYS = 128
PEER_EXPERTS = PEER_NKEYS * PEER_NKEYS
PEER_DKEY = 128
PEER_TOPK = 16
PEER_BLOCK = 128
ADA_PARTS = 6

kernel_name = "chunk_causal_hybrid_gated_mixers_peer"

def rms_norm(x, g):
    xf = x.astype(jnp.float32)
    y = xf * lax.rsqrt(jnp.mean(xf * xf, axis=-1, keepdims=True) + EPS)
    return (y * g.astype(jnp.float32)).astype(x.dtype)

def alibi_slopes(n_heads):
    return jnp.exp2(-8.0 * (jnp.arange(n_heads, dtype=jnp.float32) + 1.0) / n_heads)

def split_points():
    pts, acc = [], 0
    for s in IN_SIZES[:-1]:
        acc += s
        pts.append(acc)
    return pts

def window_sink_attention(q, k, v, sinks):
    bsz, seq, hq, d = q.shape
    hkv = k.shape[2]
    grp = hq // hkv
    nb = seq // BLOCK_Q
    qb = q.reshape(bsz, nb, BLOCK_Q, hkv, grp, d)
    kb = k.reshape(bsz, nb, BLOCK_Q, hkv, d)
    vb = v.reshape(bsz, nb, BLOCK_Q, hkv, d)

    def band(t):
        prev = jnp.concatenate([jnp.zeros_like(t[:, :1]), t[:, :-1]], axis=1)
        return jnp.concatenate([prev, t], axis=2)

    kband, vband = band(kb), band(vb)
    s = jnp.einsum('bnqhgd,bnkhd->bnhgqk', qb, kband,
                   preferred_element_type=jnp.float32) * (1.0 / math.sqrt(d))
    blk = jnp.arange(nb)[:, None, None]
    qpos = jnp.arange(BLOCK_Q)[None, :, None]
    kpos = jnp.arange(2 * BLOCK_Q)[None, None, :] - BLOCK_Q
    chunk_diff = qpos // CHUNK - ((kpos + BLOCK_Q) // CHUNK - BLOCK_Q // CHUNK)
    mask = (chunk_diff >= 0) & (chunk_diff < WINDOW_CHUNKS) & (blk * BLOCK_Q + kpos >= 0)
    dist = jnp.abs(qpos - kpos)[0].astype(jnp.float32)
    slopes = alibi_slopes(hq).reshape(hkv, grp)
    s = s - slopes[:, :, None, None] * dist
    s = jnp.where(mask[None, :, None, None], s, -jnp.inf)
    sink = sinks.astype(jnp.float32).reshape(hkv, grp)[:, :, None, None]
    m = jnp.maximum(jnp.max(s, axis=-1, keepdims=True), sink)
    p = jnp.exp(s - m)
    p = p / (jnp.sum(p, axis=-1, keepdims=True) + jnp.exp(sink - m))
    o = jnp.einsum('bnhgqk,bnkhd->bnqhgd', p.astype(v.dtype), vband)
    return o.reshape(bsz, seq, hq * d)

def forgetting_attention(q, k, v, log_f):
    bsz, seq, h, d = q.shape
    nb = seq // BLOCK_Q
    cum = jnp.cumsum(log_f, axis=1).transpose(0, 2, 1)
    kpos = jnp.arange(seq)
    scale = 1.0 / math.sqrt(d)

    def block(i):
        start = i * BLOCK_Q
        qi = lax.dynamic_slice_in_dim(q, start, BLOCK_Q, axis=1)
        ci = lax.dynamic_slice_in_dim(cum, start, BLOCK_Q, axis=2)
        s = jnp.einsum('bqhd,bkhd->bhqk', qi, k, preferred_element_type=jnp.float32) * scale
        s = s + ci[..., :, None] - cum[..., None, :]
        qpos = start + jnp.arange(BLOCK_Q)
        s = jnp.where(kpos[None, :] <= qpos[:, None], s, -jnp.inf)
        p = jax.nn.softmax(s, axis=-1)
        return jnp.einsum('bhqk,bkhd->bqhd', p.astype(v.dtype), v)

    o = lax.map(block, jnp.arange(nb))
    return o.transpose(1, 0, 2, 3, 4).reshape(bsz, seq, h * d)

def stick_breaking_attention(q, k, v):
    bsz, seq, h, d = q.shape
    nb = seq // BLOCK_Q
    kpos = jnp.arange(seq)
    scale = 1.0 / math.sqrt(d)

    def block(i):
        start = i * BLOCK_Q
        qi = lax.dynamic_slice_in_dim(q, start, BLOCK_Q, axis=1)
        z = jnp.einsum('bqhd,bkhd->bhqk', qi, k, preferred_element_type=jnp.float32) * scale
        qpos = start + jnp.arange(BLOCK_Q)
        causal = kpos[None, :] < qpos[:, None]
        log_beta = jax.nn.log_sigmoid(z)
        log_rest = jnp.where(causal, jax.nn.log_sigmoid(-z), 0.0)
        tail = lax.cumsum(log_rest, axis=3, reverse=True) - log_rest
        a = jnp.where(causal, jnp.exp(log_beta + tail), 0.0)
        return jnp.einsum('bhqk,bkhd->bqhd', a.astype(v.dtype), v)

    o = lax.map(block, jnp.arange(nb))
    return o.transpose(1, 0, 2, 3, 4).reshape(bsz, seq, h * d)

def parallel_mixers(h, w_in, b_gate, q_norm_a, k_norm_a, sinks, q_norm_b, k_norm_b,
                    b_forget, w_out_a, w_out_b, w_out_c, w_out):
    bsz, seq, _ = h.shape
    proj = h @ w_in
    qa, ka, va, qb, kb, vb, fb, qc, kc, vc, gl = jnp.split(proj, split_points(), axis=-1)

    def heads(t, n):
        return t.reshape(bsz, seq, n, HEAD_DIM)

    ya = window_sink_attention(rms_norm(heads(qa, A_HEADS), q_norm_a),
                               rms_norm(heads(ka, A_KV_HEADS), k_norm_a),
                               heads(va, A_KV_HEADS), sinks)
    log_f = jax.nn.log_sigmoid((fb + b_forget).astype(jnp.float32))
    yb = forgetting_attention(rms_norm(heads(qb, B_HEADS), q_norm_b),
                              rms_norm(heads(kb, B_HEADS), k_norm_b),
                              heads(vb, B_HEADS), log_f)
    yc = stick_breaking_attention(heads(qc, C_HEADS), heads(kc, C_HEADS), heads(vc, C_HEADS))
    gates = jax.nn.sigmoid(gl.reshape(bsz, seq, N_BRANCHES, D_MODEL) + b_gate)
    merged = (gates[:, :, 0] * (ya @ w_out_a)
              + gates[:, :, 1] * (yb @ w_out_b)
              + gates[:, :, 2] * (yc @ w_out_c))
    return merged @ w_out

def peer_ffn(h, w_query, q_norm_peer, sub_keys_1, sub_keys_2, expert_u, expert_v):
    bsz, seq, dm = h.shape
    half = PEER_DKEY // 2
    qr = rms_norm((h @ w_query).reshape(bsz, seq, PEER_HEADS, PEER_DKEY), q_norm_peer)
    s1 = jnp.einsum('bshd,hnd->bshn', qr[..., :half], sub_keys_1, preferred_element_type=jnp.float32)
    s2 = jnp.einsum('bshd,hnd->bshn', qr[..., half:], sub_keys_2, preferred_element_type=jnp.float32)
    v1, i1 = lax.top_k(s1, PEER_TOPK)
    v2, i2 = lax.top_k(s2, PEER_TOPK)
    n_cand = PEER_TOPK * PEER_TOPK
    cand_s = (v1[..., :, None] + v2[..., None, :]).reshape(bsz, seq, PEER_HEADS, n_cand)
    cand_i = (i1[..., :, None] * PEER_NKEYS + i2[..., None, :]).reshape(bsz, seq, PEER_HEADS, n_cand)
    top_s, top_pos = lax.top_k(cand_s, PEER_TOPK)
    idx = jnp.take_along_axis(cand_i, top_pos, axis=-1)
    g = jax.nn.softmax(top_s, axis=-1)
    nb = (bsz * seq) // PEER_BLOCK
    n_sel = PEER_HEADS * PEER_TOPK
    hb = h.reshape(nb, PEER_BLOCK, dm)
    ib = idx.reshape(nb, PEER_BLOCK, n_sel)
    gb = g.reshape(nb, PEER_BLOCK, n_sel)

    def block(args):
        hx, ix, gx = args
        u = jnp.take(expert_u, ix, axis=0)
        act = jax.nn.gelu(jnp.einsum('td,ted->te', hx, u, preferred_element_type=jnp.float32))
        vv = jnp.take(expert_v, ix, axis=0)
        return jnp.einsum('te,ted->td', (gx * act).astype(vv.dtype), vv)

    out = lax.map(block, (hb, ib, gb))
    return out.reshape(bsz, seq, dm).astype(h.dtype)

def setup_inputs(seed: int = 0) -> dict:
    key = jax.random.key(seed)
    ks = jax.random.split(key, 24)
    f32 = jnp.float32
    D, L = D_MODEL, DEPTH

    def nrm(k, shape, scale):
        return jax.random.normal(k, shape, f32) * scale

    col_scale = jnp.ones((IN_COLS,), f32).at[FORGET_OFF:FORGET_OFF + B_HEADS].set(0.1)
    return {
        'x': nrm(ks[0], (BATCH, SEQ, D), 1.0),
        'c': nrm(ks[1], (BATCH, D), 1.0),
        'w_ada': nrm(ks[2], (L, D, ADA_PARTS * D), 0.5 * D ** -0.5),
        'b_ada': nrm(ks[3], (L, ADA_PARTS * D), 0.02),
        'norm1_g': 1.0 + nrm(ks[4], (L, D), 0.02),
        'w_in': nrm(ks[5], (L, D, IN_COLS), D ** -0.5) * col_scale,
        'b_gate': nrm(ks[6], (L, N_BRANCHES, D), 0.02),
        'q_norm_a': 1.0 + nrm(ks[7], (L, HEAD_DIM), 0.02),
        'k_norm_a': 1.0 + nrm(ks[8], (L, HEAD_DIM), 0.02),
        'sinks': nrm(ks[9], (L, A_HEADS), 0.5),
        'q_norm_b': 1.0 + nrm(ks[10], (L, HEAD_DIM), 0.02),
        'k_norm_b': 1.0 + nrm(ks[11], (L, HEAD_DIM), 0.02),
        'b_forget': 2.0 + 4.0 * jax.random.uniform(ks[12], (L, B_HEADS), f32),
        'w_out_a': nrm(ks[13], (L, A_Q, D), A_Q ** -0.5),
        'w_out_b': nrm(ks[14], (L, B_W, D), B_W ** -0.5),
        'w_out_c': nrm(ks[15], (L, C_W, D), C_W ** -0.5),
        'w_out': nrm(ks[16], (L, D, D), D ** -0.5),
        'norm2_g': 1.0 + nrm(ks[17], (L, D), 0.02),
        'w_query': nrm(ks[18], (L, D, PEER_HEADS * PEER_DKEY), D ** -0.5),
        'q_norm_peer': 1.0 + nrm(ks[19], (L, PEER_DKEY), 0.02),
        'sub_keys_1': nrm(ks[20], (L, PEER_HEADS, PEER_NKEYS, PEER_DKEY // 2), (PEER_DKEY // 2) ** -0.5),
        'sub_keys_2': nrm(ks[21], (L, PEER_HEADS, PEER_NKEYS, PEER_DKEY // 2), (PEER_DKEY // 2) ** -0.5),
        'expert_u': nrm(ks[22], (L, PEER_EXPERTS, D), D ** -0.5),
        'expert_v': nrm(ks[23], (L, PEER_EXPERTS, D), 0.5),
    }

def reference(x, c, w_ada, b_ada, norm1_g, w_in, b_gate, q_norm_a, k_norm_a, sinks,
              q_norm_b, k_norm_b, b_forget, w_out_a, w_out_b, w_out_c, w_out, norm2_g,
              w_query, q_norm_peer, sub_keys_1, sub_keys_2, expert_u, expert_v):
    for l in range(DEPTH):
        mod = jax.nn.silu(c) @ w_ada[l] + b_ada[l]
        sh1, sc1, g1, sh2, sc2, g2 = jnp.split(mod[:, None, :], ADA_PARTS, axis=-1)
        h = rms_norm(x, norm1_g[l]) * (1.0 + sc1) + sh1
        x = x + g1 * parallel_mixers(h, w_in[l], b_gate[l], q_norm_a[l], k_norm_a[l], sinks[l],
                                     q_norm_b[l], k_norm_b[l], b_forget[l], w_out_a[l],
                                     w_out_b[l], w_out_c[l], w_out[l])
        h = rms_norm(x, norm2_g[l]) * (1.0 + sc2) + sh2
        x = x + g2 * peer_ffn(h, w_query[l], q_norm_peer[l], sub_keys_1[l], sub_keys_2[l],
                              expert_u[l], expert_v[l])
    return x


_drawn_inputs = setup_inputs


def setup_inputs(seed=0):
    import zlib

    import numpy as np

    out = dict(_drawn_inputs(seed))
    spreads = {}
    factors = {'norm1_g': 5.408,
     'b_gate': 8.0,
     'q_norm_a': 8.0,
     'k_norm_a': 8.0,
     'sinks': 7.264,
     'q_norm_b': 8.0,
     'k_norm_b': 8.0,
     'norm2_g': 3.197,
     'q_norm_peer': 3.22}
    for name, (base, spread) in spreads.items():
        noise = np.random.default_rng([zlib.crc32(name.encode()), seed]).standard_normal(out[name].shape)
        drawn = base * np.exp(spread * noise) if base else spread * noise
        out[name] = jnp.asarray(drawn.astype(out[name].dtype))
    for name, factor in factors.items():
        out[name] = (out[name] * factor).astype(out[name].dtype)
    return out
```

```python
import concourse.bass as bass
from concourse import mybir
from contextlib import ExitStack

DEPTH, SEQ, D = 2, 256, 1024
P = 128
KC = D // P
HD = 64
HEADS = 8
EPS = 1e-6
PEER_HEADS, TOPK, NKEYS = 8, 16, 128
NEG = -1e30

N_ADA = 6 * KC
N_QKV = 32
N_GATE = 3 * KC
N_BR = 12
N_OUT = KC
N_QUERY = KC
N_PEER = 2 * NKEYS
T_QKV = N_ADA
T_GATE = T_QKV + N_QKV
T_BR = T_GATE + N_GATE
T_OUT = T_BR + N_BR
T_QUERY = T_OUT + N_OUT
T_PEER = T_QUERY + N_QUERY
TILES = T_PEER + N_PEER
RAW = 4
SPLIT = 2
O_GATE = N_QKV
O_BR = O_GATE + N_GATE
O_OUT = O_BR + N_BR
O_QUERY = O_OUT + N_OUT
O_PEER = O_QUERY + N_QUERY
OUTS = O_PEER + NKEYS

QA, KA, VA, QB, KB, VB, FG, QC, KCT, VC = 0, 4, 5, 6, 10, 14, 18, 19, 23, 27
V_TILES = [VA] + [VB + i for i in range(4)] + [VC + i for i in range(4)]

PB_ADA, PG1, PG2, PBG = 0, 48, 56, 64
PQA, PKA, PQB, PKB, PQP, PSINK, PBF = 88, 89, 90, 91, 92, 93, 101
NPAR = 102
C_ID, C_ONE, C_BLK, C_TRI, C_IOTA, C_ZERO, C_CM, C_BT, C_EPS = 0, 128, 256, 384, 512, 640, 768, 1152, 1536
NCONST = 1540


def trunk(nc, stream, par_dram, const_dram, taba_dram, keys_dram, x_dram, c_dram, out_dram):
    f32, f32r, u32 = mybir.dt.float32, mybir.dt.float32r, mybir.dt.uint32
    ALU, ACT, AX = mybir.AluOpType, mybir.ActivationFunctionType, mybir.AxisListType

    ctx = ExitStack()
    with ctx:
        def sb(name, shape, dt=f32):
            return ctx.enter_context(nc.sbuf_tensor(name, shape, dt))

        def sem(name):
            return ctx.enter_context(nc.semaphore(name))

        raw = [sb(f"raw{i}", [P, 1024]) for i in range(RAW)]
        hi = [sb(f"hi{i}", [P, 1024], f32r) for i in range(SPLIT)]
        lo = [sb(f"lo{i}", [P, 1024], f32r) for i in range(SPLIT)]
        x = sb("x", [P, KC, SEQ])
        mov_hi = sb("mov_hi", [P, 12, SEQ], f32r)
        mov_lo = sb("mov_lo", [P, 12, SEQ], f32r)
        w_hi = mov_hi[:, KC:KC + 2, :]
        w_lo = mov_lo[:, KC:KC + 2, :]
        const = sb("const", [P, NCONST])
        par_all = sb("par_all", [P, DEPTH, NPAR])
        par = sb("par", [P, NPAR])
        c_in = sb("c_in", [P, KC])
        c_tmp = sb("c_tmp", [P, KC])
        c_hi = sb("c_hi", [P, KC, 2], f32r)
        c_lo = sb("c_lo", [P, KC, 2], f32r)
        mod = sb("mod", [P, N_ADA])
        amp = sb("amp", [P, 2, KC])
        gain = sb("gain", [P, 2])
        small = sb("small", [P, 96])
        idx1T = sb("idx1T", [P, SEQ])
        idx2T = sb("idx2T", [P, SEQ])
        gateT = sb("gateT", [P, SEQ])
        act_g = sb("act_g", [P, 2, SEQ])
        w_f = sb("w_f", [P, 2, SEQ])
        onehot_a = act_g[:, :, :].rearrange("p a b -> p (a b)").rearrange("p (r i) -> p r i", r=4)
        onehot_b = w_f[:, :, :].rearrange("p a b -> p (a b)").rearrange("p (r i) -> p r i", r=4)
        rstd = act_g[:, 0, :]

        ident = const[:, C_ID:C_ID + P]
        ones = const[:, C_ONE:C_ONE + P]
        blk = const[:, C_BLK:C_BLK + P]
        tri = const[:, C_TRI:C_TRI + P]
        iota = const[:, C_IOTA:C_IOTA + P]
        zero = const[:, C_ZERO:C_ZERO + P]
        cmask = const[:, C_CM:C_CM + 384]
        btab = const[:, C_BT:C_BT + 384]
        eps = const[:, C_EPS:C_EPS + 1]
        mx, negm, den, sinkd = small[:, 0:16], small[:, 16:32], small[:, 32:48], small[:, 48:64]
        rden = small[:, 64:80]

        arena = sb("arena", [P, NKEYS, SEQ])
        flat = arena[:, :, :].rearrange("p a b -> p (a b)")
        used = [0]

        def part(n):
            a = flat[:, used[0]:used[0] + n]
            used[0] += n
            return a

        projT = part(56 * SEQ).rearrange("p (t s) -> p t s", s=SEQ)
        vtok = part(2 * 1152).rearrange("p (b c) -> p b c", b=2)
        taba = part(HEADS * 384).rearrange("p (h c) -> p h c", h=HEADS)
        prob = part(HEADS * 384).rearrange("p (h c) -> p h c", h=HEADS)
        probT = part(2 * 384).rearrange("p (r c) -> p r c", r=2)
        ytok = part(2 * 3 * 512).rearrange("p (b r c) -> p b r c", b=2, r=3)
        merged = part(KC * SEQ).rearrange("p (k s) -> p k s", s=SEQ)
        gated = part(2 * 512).rearrange("p (r c) -> p r c", r=2)
        sq = part(KC * SEQ).rearrange("p (k s) -> p k s", s=SEQ)
        assert used[0] <= NKEYS * SEQ, used
        stick = prob.rearrange("p h c -> p (h c)")[:, 0:8 * 384].rearrange("p (r n c) -> p r n c", r=2, n=4)
        used[0] = 0
        skeys = taba.rearrange("p h c -> p (h c)")[:, 0:PEER_HEADS * 256].rearrange("p (h c) -> p h c", h=PEER_HEADS)
        queryT = part(KC * SEQ).rearrange("p (k s) -> p k s", s=SEQ)
        score = part(16 * 256).rearrange("p (u c) -> p u c", u=16)
        rest = part(2 * 256).rearrange("p (r c) -> p r c", r=2)
        cand = part(2 * 256).rearrange("p (r c) -> p r c", r=2)
        candr = part(256)
        sel_v = part(2 * 16).rearrange("p (n k) -> p n k", n=2)
        sel_i = part(16 * 32).rearrange("p (u n k) -> p u n k", u=16, n=2).bitcast(u32)
        sel_if = part(16 * 32).rearrange("p (u n k) -> p u n k", u=16, n=2)
        top_s = part(16 * 16).rearrange("p (u k) -> p u k", u=16)
        top_p = part(16 * 16).rearrange("p (u k) -> p u k", u=16).bitcast(u32)
        pos_i = part(2 * 256).rearrange("p (n c) -> p n c", n=2).bitcast(u32)
        pos_f = part(2 * 256).rearrange("p (n c) -> p n c", n=2)
        gsum = part(2 * 16).rearrange("p (n c) -> p n c", n=2)
        pick = part(8 * 256)
        idx_tok = part(2 * 256).rearrange("p (n c) -> p n c", n=2)
        ftok = arena[:, 0:8, :].rearrange("p a b -> p (a b)").rearrange("p (b c) -> p b c", b=2)
        fl = sq[0:HEADS, 0:4, :]

        pj = [ctx.enter_context(nc.psum_tensor(f"pj{i}", [P, 512], f32)) for i in range(2)]
        wk = ctx.enter_context(nc.psum_tensor("wk", [P, 6, 512], f32))
        wkf = wk[:, :, :].rearrange("p b c -> p (b c)")

        setup_loaded = sem("setup_loaded")
        setup_step = sem("setup_step")
        c_exp = sem("c_exp")
        c_ready = sem("c_ready")
        raw_loaded = [sem(f"raw_loaded{i}") for i in range(RAW)]
        hi_done = sem("hi_done")
        lo_done = sem("lo_done")
        tile_done = sem("tile_done")
        out_free = sem("out_free")
        x_ready = sem("x_ready")
        sq_ready = sem("sq_ready")
        ss_ready = sem("ss_ready")
        rstd_ready = sem("rstd_ready")
        h_ready = sem("h_ready")
        h_hi = sem("h_hi")
        mov_ready = sem("mov_ready")
        tables = sem("tables")
        arena_free = sem("arena_free")
        keys_free = sem("keys_free")
        keys_in = sem("keys_in")
        vtr = sem("vtr")
        vtok_in = sem("vtok_in")
        qk_sq = sem("qk_sq")
        qk_ss = sem("qk_ss")
        qk_rr = sem("qk_rr")
        qk_done = sem("qk_done")
        f_sum = sem("f_sum")
        f_log = sem("f_log")
        f_ready = sem("f_ready")
        score_ready = sem("score_ready")
        score_read = sem("score_read")
        negmax = sem("negmax")
        sinkd_exp = sem("sinkd_exp")
        prob_ready = sem("prob_ready")
        ptr_ready = sem("ptr_ready")
        pt_copied = sem("pt_copied")
        pv_done = sem("pv_done")
        y_read = sem("y_read")
        z_ready = sem("z_ready")
        z_log = sem("z_log")
        z_read = sem("z_read")
        tail_ready = sem("tail_ready")
        stick_arg = sem("stick_arg")
        stick_exp = sem("stick_exp")
        stick_ready = sem("stick_ready")
        ytr = sem("ytr")
        y_hi = sem("y_hi")
        br_mul = sem("br_mul")
        br_add = sem("br_add")
        q_sq = sem("q_sq")
        q_ss = sem("q_ss")
        q_rr = sem("q_rr")
        q_norm = sem("q_norm")
        s_ready = sem("s_ready")
        s_copied = sem("s_copied")
        g_arg = sem("g_arg")
        g_exp = sem("g_exp")
        route_ready = sem("route_ready")
        route_tr = sem("route_tr")
        route_in = sem("route_in")
        hot_a = sem("hot_a")
        hot_b = sem("hot_b")
        hot_diff = sem("hot_diff")
        hot_used = sem("hot_used")
        g_free = sem("g_free")
        w_made = sem("w_made")
        w_head = sem("w_head")
        w_rest = sem("w_rest")
        f_tok = sem("f_tok")
        f_tr = sem("f_tr")
        stored = sem("stored")
        waits_met = sem("waits_met")
        act_step = sem("act_step")
        dve_step = sem("dve_step")

        def wait_alone(eng, s, value):
            eng.wait_ge(s, value)
            eng.sem_inc(waits_met, 1)

        block = ctx.enter_context(nc.Block())

        @block.sync
        def _(sp):
            sp.dma_start(const[:, :], const_dram).then_inc(setup_loaded, 16)
            sp.dma_start(par_all[:, :, :], par_dram).then_inc(setup_loaded, 16)
            sp.dma_start(c_in[:, :], c_dram).then_inc(setup_loaded, 16)
            for j in range(RAW):
                sp.dma_start(raw[j][:, :], stream[j]).then_inc(raw_loaded[j], 16)
                if j == 1:
                    sp.dma_start(x[:, :, :], x_dram).then_inc(setup_loaded, 16)
            with sp.Fori(0, DEPTH * TILES // RAW - 1) as i:
                for j in range(RAW):
                    sp.wait_ge(lo_done, i * RAW + j + 1)
                    sp.dma_start(raw[j][:, :], stream[i * RAW + RAW + j]).then_inc(raw_loaded[j], 16)
            sp.wait_ge(x_ready, 2 * DEPTH + 1)
            sp.dma_start(out_dram, x[:, :, :]).then_inc(stored, 16)
            sp.wait_ge(stored, 16)

        @block.gpsimd
        def _(pool):
            with pool.Fori(0, DEPTH) as l:
                wait_alone(pool, arena_free, l + 1)
                pool.dma_start(taba, taba_dram).then_inc(tables, 16)
                wait_alone(pool, keys_free, l + 1)
                pool.dma_start(skeys, keys_dram[l]).then_inc(keys_in, 16)
                wait_alone(pool, route_in, 6 * l + 6)
                with pool.Fori(0, SEQ // 4) as i:
                    wait_alone(pool, hot_used, l * SEQ + i * 4 + 4)
                    nc.gpsimd.tensor_tensor(onehot_b, iota.unsqueeze(1).to_broadcast([P, 4, NKEYS]),
                                            idx2T[:, bass.ds(i * 4, 4)].unsqueeze(2).to_broadcast([P, 4, NKEYS]),
                                            ALU.subtract).then_inc(hot_diff, 1)
                    wait_alone(pool, hot_diff, l * (SEQ // 4) + i + 1)
                    nc.gpsimd.tensor_scalar(onehot_b, onehot_b, 0.0, None, ALU.is_equal).then_inc(hot_b, 4)

        @block.scalar
        def _(act):
            def head(t, j):
                act.wait_ge(raw_loaded[j % RAW], 16 + load_count(t, j))
                act.wait_ge(tile_done, t + 1)
                nc.scalar.activation(hi[j % SPLIT][:, :], raw[j % RAW][:, :], ACT.Copy).then_inc(hi_done, 1)

            def load_count(t, j):
                return (t - (j % RAW)) * (16 // RAW)

            act.wait_ge(setup_loaded, 64)
            nc.scalar.activation(c_tmp[:, :], c_in[:, :], ACT.Exp, scale=-1.0).then_inc(c_exp, 1)
            with act.Fori(0, DEPTH) as l:
                act.sem_clear(act_step)
                n_link = [0]
                L0 = l * TILES

                def link(ins):
                    ins.then_inc(act_step, 1)
                    n_link[0] += 1
                    act.wait_ge(act_step, n_link[0])

                def norm(n):
                    act.wait_ge(x_ready, 2 * l + n + 1)
                    nc.scalar.activation(sq, x[:, :, :], ACT.Square).then_inc(sq_ready, 1)
                    act.wait_ge(ss_ready, 2 * l + n + 1)
                    link(nc.scalar.activation(rstd, wk[:, 0, 0:SEQ], ACT.Ln, bias=eps, scale=1.0 / D))
                    nc.scalar.activation(rstd, rstd, ACT.Exp, scale=-0.5).then_inc(rstd_ready, 1)
                    act.wait_ge(h_ready, 3 * l + (1 if n == 0 else 3))
                    nc.scalar.activation(mov_hi[:, 0:KC, :], sq, ACT.Copy).then_inc(h_hi, 1)

                head(L0, 0)
                with act.Fori(0, N_ADA // 4) as i:
                    for j in range(4):
                        head(L0 + i * 4 + (j + 1), j + 1)
                norm(0)
                with act.Fori(0, N_QKV // 4) as i:
                    for j in range(4):
                        t = L0 + i * 4 + (T_QKV + j)
                        head(t + 1, j + 1)
                        act.wait_ge(tile_done, t + 3)
                        nc.scalar.activation(projT[:, bass.ds(i * 4 + j, 1), :].squeeze(1), pj[j % 2][:, 0:SEQ],
                                             ACT.Copy).then_inc(out_free, 1)
                with act.Fori(0, N_GATE // 4) as i:
                    for j in range(4):
                        t = L0 + i * 4 + (T_GATE + j)
                        head(t + 1, j + 1)
                        act.wait_ge(tile_done, t + 3)
                        nc.scalar.activation(projT[:, bass.ds(i * 4 + (N_QKV + j), 1), :].squeeze(1),
                                             pj[j % 2][:, 0:SEQ], ACT.Sigmoid,
                                             bias=par[:, bass.ds(i * 4 + (PBG + j), 1)]).then_inc(out_free, 1)
                for b in range(2):
                    act.wait_ge(vtr, 2 * l + b + 1)
                    nc.scalar.activation(vtok[:, b, :], wkf[:, b * 1536:b * 1536 + 1152], ACT.Copy)\
                        .then_inc(vtok_in, 1)
                act.wait_ge(out_free, l * OUTS + (O_BR + 2))
                for g, (t0, n) in enumerate(((QA, 5), (QB, 8))):
                    if g:
                        act.wait_ge(qk_done, 2 * l + 1)
                    nc.scalar.activation(sq[:, 0:n, :], projT[:, t0:t0 + n, :], ACT.Square).then_inc(qk_sq, 1)
                    act.wait_ge(qk_ss, 2 * l + g + 1)
                    sqf = sq.rearrange("p k s -> p (k s)")[:, 0:n * SEQ]
                    link(nc.scalar.activation(sqf, wkf[:, 0:n * SEQ], ACT.Ln, bias=eps, scale=1.0 / HD))
                    nc.scalar.activation(sqf, sqf, ACT.Exp, scale=-0.5).then_inc(qk_rr, 1)
                act.wait_ge(f_sum, l + 1)
                link(nc.scalar.activation(fl[:, 1, :], fl[:, 0, :], ACT.Abs))
                link(nc.scalar.activation(fl[:, 1, :], fl[:, 1, :], ACT.Exp, scale=-1.0))
                nc.scalar.activation(fl[:, 1, :], fl[:, 1, :], ACT.Ln, bias=1.0).then_inc(f_log, 1)
                for br in range(2):
                    act.wait_ge(negmax, 2 * l + br + 1)
                    for h in range(HEADS):
                        for b, (c0, c1) in enumerate(((0, 128), (128, 384))):
                            e = nc.scalar.activation(prob[:, h, c0:c1], prob[:, h, c0:c1], ACT.Exp,
                                                     bias=negm[:, b * 8 + h:b * 8 + h + 1],
                                                     accum_out=den[:, b * 8 + h:b * 8 + h + 1])
                        e.then_inc(prob_ready, 1)
                    if br == 0:
                        nc.scalar.activation(sinkd, sinkd, ACT.Exp).then_inc(sinkd_exp, 1)
                def stick_tail(h):
                    act.wait_ge(stick_arg, 8 * l + h + 1)
                    nc.scalar.activation(stick[:, h % 2, 2, :], stick[:, h % 2, 2, :], ACT.Exp)\
                        .then_inc(stick_exp, 1)

                act.wait_ge(ptr_ready, 16 * l + 16)
                for h in range(HEADS):
                    act.wait_ge(z_ready, 8 * l + h + 1)
                    if h >= 2:
                        act.wait_ge(stick_ready, 8 * l + h - 1)
                    link(nc.scalar.activation(stick[:, h % 2, 0, :], wk[:, 2 + h % 2, 0:384], ACT.Abs))
                    link(nc.scalar.activation(stick[:, h % 2, 0, :], stick[:, h % 2, 0, :], ACT.Exp, scale=-1.0))
                    nc.scalar.activation(stick[:, h % 2, 0, :], stick[:, h % 2, 0, :], ACT.Ln, bias=1.0)\
                        .then_inc(z_log, 1)
                    if h:
                        stick_tail(h - 1)
                stick_tail(HEADS - 1)
                for n in range(6):
                    br, b = n // 2, n % 2
                    act.wait_ge(ytr, 6 * l + n + 1)
                    nc.scalar.activation(mov_hi[:, 4 * br:4 * br + 4, b * P:(b + 1) * P],
                                         wk[:, n, :].rearrange("p (c t) -> p c t", c=4), ACT.Copy)\
                        .then_inc(y_hi, 1)
                with act.Fori(0, N_BR // 4) as i:
                    for j in range(4):
                        head(L0 + i * 4 + (T_BR + 1 + j), j + 1)
                act.wait_ge(h_ready, 3 * l + 2)
                nc.scalar.activation(mov_hi[:, 0:KC, :], merged, ACT.Copy).then_inc(h_hi, 1)
                with act.Fori(0, N_OUT // 4) as i:
                    for j in range(4):
                        head(L0 + i * 4 + (T_OUT + 1 + j), j + 1)
                norm(1)
                with act.Fori(0, N_QUERY // 4) as i:
                    for j in range(4):
                        t = L0 + i * 4 + (T_QUERY + j)
                        head(t + 1, j + 1)
                        act.wait_ge(tile_done, t + 3)
                        nc.scalar.activation(queryT[:, bass.ds(i * 4 + j, 1), :].squeeze(1), pj[j % 2][:, 0:SEQ],
                                             ACT.Copy).then_inc(out_free, 1)
                act.wait_ge(out_free, l * OUTS + (O_PEER + 2))
                nc.scalar.activation(sq, queryT, ACT.Square).then_inc(q_sq, 1)
                act.wait_ge(q_ss, l + 1)
                sqf = sq.rearrange("p k s -> p (k s)")
                link(nc.scalar.activation(sqf, wkf[:, 0:2048], ACT.Ln, bias=eps, scale=1.0 / P))
                nc.scalar.activation(sqf, sqf, ACT.Exp, scale=-0.5).then_inc(q_rr, 1)
                for u in range(0, 16, 2):
                    act.wait_ge(s_ready, 16 * l + u + 2)
                    nc.scalar.activation(score[:, u:u + 2, :],
                                         wk[:, (u // 2) % 6, :].rearrange("p (u c) -> p u c", u=2), ACT.Copy)\
                        .then_inc(s_copied, 1)
                act.wait_ge(g_arg, l + 1)
                nc.scalar.activation(top_s, top_s, ACT.Exp).then_inc(g_exp, 1)
                act.wait_ge(route_in, 6 * l + 6)
                with act.Fori(0, SEQ // 8) as i:
                    for j in range(2):
                        act.wait_ge(hot_used, l * SEQ + i * 8 + (4 * j + 8))
                        nc.scalar.activation(
                            arena[:, :, bass.ds(i * 8 + 4 * j, 4)].rearrange("p i t -> p t i"),
                            wk[:, j, :].rearrange("p (t i) -> p t i", t=4), ACT.Copy).then_inc(g_free, 1)

                def gelu(n, s, t):
                    act.wait_ge(tile_done, t + 3)
                    nc.scalar.activation(act_g[:, s, :], pj[s][:, 0:SEQ], ACT.Gelu_apprx_tanh)\
                        .then_inc(out_free, 1)

                def w_heads(n, s):
                    act.wait_ge(w_made, l * NKEYS + n + 1)
                    nc.scalar.activation(w_hi[:, s, :], w_f[:, s, :], ACT.Copy).then_inc(w_head, 1)

                E0 = L0 + T_PEER
                head(E0 + 1, 1)
                gelu(0, 0, E0)
                w_heads(0, 0)
                with act.Fori(0, NKEYS // 2 - 1) as i:
                    head(E0 + i * 4 + 2, 2)
                    gelu(i * 2 + 1, 1, E0 + i * 4 + 1)
                    head(E0 + i * 4 + 3, 3)
                    w_heads(i * 2 + 1, 1)
                    head(E0 + i * 4 + 4, 0)
                    gelu(i * 2 + 2, 0, E0 + i * 4 + 3)
                    head(E0 + i * 4 + 5, 1)
                    w_heads(i * 2 + 2, 0)
                head(E0 + 254, 2)
                gelu(NKEYS - 1, 1, E0 + 253)
                head(E0 + 255, 3)
                w_heads(NKEYS - 1, 1)

        @block.vector
        def _(dve):
            setup = [0]

            def slink(ins):
                ins.then_inc(setup_step, 1)
                setup[0] += 1
                dve.wait_ge(setup_step, setup[0])

            def rest_of(t, j):
                dve.wait_ge(hi_done, t + 1)
                nc.vector.tensor_tensor(lo[j % SPLIT][:, :], raw[j % RAW][:, :], hi[j % SPLIT][:, :].bitcast(f32),
                                        ALU.subtract).then_inc(lo_done, 1)

            dve.wait_ge(setup_loaded, 64)
            dve.wait_ge(c_exp, 1)
            slink(nc.vector.tensor_scalar(c_tmp[:, :], c_tmp[:, :], 1.0, None, ALU.add))
            slink(nc.vector.reciprocal(c_tmp[:, :], c_tmp[:, :]))
            slink(nc.vector.tensor_tensor(c_tmp[:, :], c_tmp[:, :], c_in[:, :], ALU.mult))
            cb = c_tmp[:, :].unsqueeze(2).to_broadcast([P, KC, 2])
            slink(nc.vector.tensor_copy(c_hi[:, :, :], cb))
            nc.vector.tensor_tensor(c_lo[:, :, :], cb, c_hi[:, :, :].bitcast(f32), ALU.subtract).then_inc(c_ready, 1)
            dve.sem_inc(x_ready, 1)
            dve.sem_inc(arena_free, 1)

            with dve.Fori(0, DEPTH) as l:
                dve.sem_clear(dve_step)
                n_link = [0]
                L0 = l * TILES

                def link(ins):
                    ins.then_inc(dve_step, 1)
                    n_link[0] += 1
                    dve.wait_ge(dve_step, n_link[0])

                def norm(n):
                    dve.wait_ge(rstd_ready, 2 * l + n + 1)
                    link(nc.vector.tensor_tensor(sq, x[:, :, :], rstd.unsqueeze(1).to_broadcast([P, KC, SEQ]),
                                                 ALU.mult))
                    for k in range(KC):
                        last = nc.vector.tensor_scalar(sq[:, k, :], sq[:, k, :], amp[:, n, k:k + 1],
                                                       mod[:, 24 * n + k:24 * n + k + 1], ALU.mult, ALU.add)
                    last.then_inc(h_ready, 1)
                    dve.wait_ge(h_ready, 3 * l + (1 if n == 0 else 3))
                    dve.wait_ge(h_hi, 3 * l + (1 if n == 0 else 3))
                    nc.vector.tensor_tensor(mov_lo[:, 0:KC, :], sq, mov_hi[:, 0:KC, :].bitcast(f32),
                                            ALU.subtract).then_inc(mov_ready, 1)

                link(nc.vector.tensor_copy(par[:, :], par_all[:, bass.ds(l, 1), :].squeeze(1)))
                rest_of(L0, 0)
                with dve.Fori(0, N_ADA // 4) as i:
                    for j in range(4):
                        rest_of(L0 + i * 4 + (j + 1), j + 1)
                dve.wait_ge(tile_done, L0 + N_ADA + 2)
                link(nc.vector.tensor_tensor(mod[:, :], wk[:, 1, 0:2 * N_ADA:2], par[:, 0:N_ADA], ALU.add))
                for n, g in ((0, PG1), (1, PG2)):
                    link(nc.vector.scalar_tensor_tensor(amp[:, n, :], mod[:, 24 * n + 8:24 * n + 16], 1.0,
                                                        par[:, g:g + KC], ALU.add, ALU.mult))
                for n, g in ((0, PQA), (1, PQB)):
                    link(nc.vector.tensor_scalar(gain[:, n:n + 1], par[:, g:g + 1], HD ** -0.5, None, ALU.mult))
                norm(0)
                with dve.Fori(0, (N_QKV + N_GATE) // 4) as i:
                    for j in range(4):
                        rest_of(L0 + i * 4 + (T_QKV + 1 + j), j + 1)
                dve.wait_ge(out_free, l * OUTS + (O_BR + 2))
                nc.vector.tensor_scalar(projT[:, QC:QC + 4, :], projT[:, QC:QC + 4, :], HD ** -0.5, None, ALU.mult)
                for g, (q0, k0, nk, gk) in enumerate(((QA, KA, 1, PKA), (QB, KB, 4, PKB))):
                    dve.wait_ge(qk_rr, 2 * l + g + 1)
                    nc.vector.scalar_tensor_tensor(projT[:, q0:q0 + 4, :], projT[:, q0:q0 + 4, :], gain[:, g:g + 1],
                                                   sq[:, 0:4, :], ALU.mult, ALU.mult)
                    nc.vector.scalar_tensor_tensor(projT[:, k0:k0 + nk, :], projT[:, k0:k0 + nk, :],
                                                   par[:, gk:gk + 1], sq[:, 4:4 + nk, :], ALU.mult,
                                                   ALU.mult).then_inc(qk_done, 1)
                dve.wait_ge(qk_done, 2 * l + 2)
                nc.vector.tensor_scalar(fl[:, 0, :], projT[0:HEADS, FG, :], par[0:HEADS, PBF:PBF + 1], None,
                                        ALU.add).then_inc(f_sum, 1)
                dve.wait_ge(f_log, l + 1)
                link(nc.vector.scalar_tensor_tensor(fl[:, 0, :], fl[:, 0, :], 0.0, fl[:, 1, :], ALU.min,
                                                    ALU.subtract))
                link(nc.vector.tensor_tensor_scan(fl[:, 2, :], const[0:HEADS, C_ONE:C_ONE + 1].to_broadcast([HEADS, SEQ]),
                                                  fl[:, 0, :], 0.0, ALU.mult, ALU.add))
                nc.vector.tensor_scalar(fl[:, 3, :], fl[:, 2, :], -1.0, None, ALU.mult).then_inc(f_ready, 1)
                dve.wait_ge(tables, 16 * l + 16)
                for br in range(2):
                    if br:
                        dve.wait_ge(ptr_ready, 16 * l + 8)
                    for h in range(HEADS):
                        wait_alone(dve, score_ready, 16 * l + 8 * br + h + 1)
                        for b, (c0, c1) in enumerate(((0, 128), (128, 384))):
                            tab = taba[:, h, c0:c1] if br == 0 else btab[:, c0:c1]
                            e = nc.vector.tensor_tensor_reduce(
                                out=prob[:, h, c0:c1], in0=wk[:, 2 + h % 4, c0:c1], in1=tab, scale=1.0,
                                scalar=-3e38, op0=ALU.add, op1=ALU.max, accum_out=mx[:, b * 8 + h:b * 8 + h + 1])
                        e.then_inc(score_read, 1)
                    dve.wait_ge(score_read, 16 * l + 8 * br + 8)
                    if br == 0:
                        sink = par[:, PSINK:PSINK + 8].unsqueeze(1).to_broadcast([P, 2, 8])
                        mx2, sk2 = mx.rearrange("p (b h) -> p b h", b=2), sinkd.rearrange("p (b h) -> p b h", b=2)
                        link(nc.vector.tensor_tensor(mx2, mx2, sink, ALU.max))
                        link(nc.vector.tensor_tensor(sk2, sink, mx2, ALU.subtract))
                    nc.vector.tensor_scalar(negm, mx, -1.0, None, ALU.mult).then_inc(negmax, 1)
                    for h in range(HEADS):
                        n = 8 * br + h
                        dve.wait_ge(ptr_ready, 16 * l + n + 1)
                        if n >= 2:
                            dve.wait_ge(pv_done, 24 * l + n - 1)
                        nc.vector.tensor_copy(probT[:, h % 2, :], wk[:, h % 2, 0:384]).then_inc(pt_copied, 1)
                    dve.wait_ge(prob_ready, 16 * l + 8 * br + 8)
                    if br == 0:
                        dve.wait_ge(sinkd_exp, l + 1)
                        link(nc.vector.tensor_tensor(den, den, sinkd, ALU.add))
                    link(nc.vector.reciprocal(rden, den))
                    dve.wait_ge(pv_done, 24 * l + 8 * br + 8)
                    for b in range(2):
                        e = nc.vector.tensor_tensor(
                            ytok[:, b, br, :].rearrange("p (h c) -> p h c", h=8),
                            pj[b][:, :].rearrange("p (h c) -> p h c", h=8),
                            rden[:, b * 8:b * 8 + 8].unsqueeze(2).to_broadcast([P, 8, HD]), ALU.mult)
                    e.then_inc(y_read, 1)
                def stick_tail(h):
                    s = h % 2
                    dve.wait_ge(tail_ready, 8 * l + h + 1)
                    nc.vector.tensor_tensor(stick[:, s, 2, :], stick[:, s, 2, :], wk[:, 4 + s, 0:384],
                                            ALU.subtract).then_inc(stick_arg, 1)
                    dve.wait_ge(stick_exp, 8 * l + h + 1)
                    if h >= 2:
                        dve.wait_ge(pv_done, 24 * l + 16 + h - 1)
                    nc.vector.tensor_tensor(stick[:, s, 3, :], stick[:, s, 2, :], cmask,
                                            ALU.mult).then_inc(stick_ready, 1)

                for h in range(HEADS):
                    s = h % 2
                    z = wk[:, 2 + s, 0:384]
                    dve.wait_ge(z_log, 8 * l + h + 1)
                    link(nc.vector.scalar_tensor_tensor(stick[:, s, 1, :], z, 0.0, stick[:, s, 0, :], ALU.max,
                                                        ALU.add))
                    nc.vector.tensor_tensor(stick[:, s, 1, :], stick[:, s, 1, :], cmask, ALU.mult)
                    nc.vector.scalar_tensor_tensor(stick[:, s, 2, :], z, 0.0, stick[:, s, 0, :], ALU.min,
                                                   ALU.subtract).then_inc(z_read, 1)
                    if h:
                        stick_tail(h - 1)
                    else:
                        dve.wait_ge(z_read, 8 * l + 1)
                stick_tail(HEADS - 1)
                dve.wait_ge(pv_done, 24 * l + 24)
                for b in range(2):
                    e = nc.vector.tensor_copy(ytok[:, b, 2, :], pj[b][:, :])
                e.then_inc(y_read, 1)
                link(nc.vector.memset(merged, 0.0))
                dve.sem_inc(keys_free, 1)
                for n in range(6):
                    br, b = n // 2, n % 2
                    dve.wait_ge(y_hi, 6 * l + n + 1)
                    nc.vector.tensor_tensor(mov_lo[:, 4 * br:4 * br + 4, b * P:(b + 1) * P],
                                            wk[:, n, :].rearrange("p (c t) -> p c t", c=4),
                                            mov_hi[:, 4 * br:4 * br + 4, b * P:(b + 1) * P].bitcast(f32),
                                            ALU.subtract).then_inc(mov_ready, 1)
                with dve.Fori(0, 3) as br:
                    for j in range(4):
                        t = L0 + br * 4 + (T_BR + j)
                        rest_of(t + 1, j + 1)
                        dve.wait_ge(tile_done, t + 3)
                        n = l * N_BR + br * 4 + j
                        nc.vector.tensor_tensor(
                            gated[:, j % 2, :].rearrange("p (o s) -> p o s", o=2),
                            pj[j % 2][:, :].rearrange("p (o s) -> p o s", o=2),
                            projT[:, bass.ds(br * 8 + (N_QKV + 2 * j), 2), :], ALU.mult).then_inc(out_free, 1)
                        dve.wait_ge(out_free, l * OUTS + br * 4 + (O_BR + j + 3))
                        nc.vector.tensor_tensor(merged[:, 2 * j:2 * j + 2, :], merged[:, 2 * j:2 * j + 2, :],
                                                gated[:, j % 2, :].rearrange("p (o s) -> p o s", o=2),
                                                ALU.add).then_inc(br_add, 1)
                        dve.wait_ge(br_add, n + 1)
                dve.sem_inc(h_ready, 1)
                dve.wait_ge(h_hi, 3 * l + 2)
                nc.vector.tensor_tensor(mov_lo[:, 0:KC, :], merged, mov_hi[:, 0:KC, :].bitcast(f32),
                                        ALU.subtract).then_inc(mov_ready, 1)
                with dve.Fori(0, N_OUT // 4) as i:
                    for j in range(4):
                        t = L0 + i * 4 + (T_OUT + j)
                        rest_of(t + 1, j + 1)
                        dve.wait_ge(tile_done, t + 3)
                        xk = x[:, bass.ds(i * 4 + j, 1), :].squeeze(1)
                        nc.vector.scalar_tensor_tensor(xk, pj[j % 2][:, 0:SEQ], mod[:, bass.ds(i * 4 + (16 + j), 1)],
                                                       xk, ALU.mult, ALU.add).then_inc(out_free, 1)
                dve.wait_ge(out_free, l * OUTS + (O_QUERY + 2))
                dve.sem_inc(x_ready, 1)
                norm(1)
                with dve.Fori(0, N_QUERY // 4) as i:
                    for j in range(4):
                        rest_of(L0 + i * 4 + (T_QUERY + 1 + j), j + 1)
                dve.wait_ge(q_rr, l + 1)
                nc.vector.scalar_tensor_tensor(queryT, queryT, par[:, PQP:PQP + 1], sq, ALU.mult,
                                               ALU.mult).then_inc(q_norm, 1)
                for u in range(16):
                    if u % 2 == 0:
                        wait_alone(dve, s_copied, 8 * l + u // 2 + 1)
                    for n in range(2):
                        s = score[:, u, n * 128:(n + 1) * 128]
                        r = rest[:, n, 0:128]
                        link(nc.vector.max(sel_v[:, n, 0:8], s))
                        nc.vector.max_index(sel_i[:, u, n, 0:8], sel_v[:, n, 0:8], s)
                        link(nc.vector.match_replace(r, sel_v[:, n, 0:8], s, -3e38))
                        link(nc.vector.max(sel_v[:, n, 8:16], r))
                        nc.vector.max_index(sel_i[:, u, n, 8:16], sel_v[:, n, 8:16], r)
                    c = cand[:, 0, :]
                    link(nc.vector.tensor_tensor(c.rearrange("p (a b) -> p a b", a=16),
                                                 sel_v[:, 0, :].unsqueeze(2).to_broadcast([P, 16, 16]),
                                                 sel_v[:, 1, :].unsqueeze(1).to_broadcast([P, 16, 16]), ALU.add))
                    link(nc.vector.max(top_s[:, u, 0:8], c))
                    nc.vector.max_index(top_p[:, u, 0:8], top_s[:, u, 0:8], c)
                    link(nc.vector.match_replace(candr, top_s[:, u, 0:8], c, -3e38))
                    link(nc.vector.max(top_s[:, u, 8:16], candr))
                    link(nc.vector.max_index(top_p[:, u, 8:16], top_s[:, u, 8:16], candr))
                gs, gr = gsum[:, 0, :], gsum[:, 1, :]
                link(nc.vector.tensor_copy(gs, top_s[:, :, 0:1].squeeze(2)))
                nc.vector.tensor_tensor(top_s, top_s, gs.unsqueeze(2).to_broadcast([P, 16, 16]),
                                        ALU.subtract).then_inc(g_arg, 1)
                tp = top_p.rearrange("p u k -> p (u k)")
                nc.vector.tensor_scalar(pos_i[:, 0, :], tp, 4, None, ALU.logical_shift_right)
                link(nc.vector.tensor_scalar(pos_i[:, 1, :], tp, 15, None, ALU.bitwise_and))
                nc.vector.tensor_copy(sel_if, sel_i)
                link(nc.vector.tensor_copy(pos_f, pos_i))
                for n in range(2):
                    for b in range(2):
                        hot = pick.rearrange("p (c j) -> p c j", j=16)
                        pf = pos_f[:, n, b * 128:(b + 1) * 128]
                        link(nc.vector.tensor_tensor(hot, pf.unsqueeze(2).to_broadcast([P, 128, 16]),
                                                     iota[:, 0:16].unsqueeze(1).to_broadcast([P, 128, 16]),
                                                     ALU.is_equal))
                        hot4 = pick.rearrange("p (u k j) -> p u k j", u=8, k=16)
                        link(nc.vector.tensor_tensor(
                            hot4, hot4, sel_if[:, b * 8:b * 8 + 8, n, :].unsqueeze(2).to_broadcast([P, 8, 16, 16]),
                            ALU.mult))
                        link(nc.vector.tensor_reduce(idx_tok[:, n, b * 128:(b + 1) * 128], hot, AX.X, ALU.add))
                dve.wait_ge(g_exp, l + 1)
                link(nc.vector.tensor_reduce(gs, top_s, AX.X, ALU.add))
                link(nc.vector.reciprocal(gr, gs))
                nc.vector.tensor_tensor(top_s, top_s, gr.unsqueeze(2).to_broadcast([P, 16, 16]),
                                        ALU.mult).then_inc(route_ready, 1)
                for n, (dst) in enumerate((idx1T, idx2T, gateT)):
                    for b in range(2):
                        dve.wait_ge(route_tr, 6 * l + 2 * n + b + 1)
                        nc.vector.tensor_copy(dst[:, b * P:(b + 1) * P], wk[:, 2 * n + b, 0:P]).then_inc(route_in, 1)
                wait_alone(dve, route_in, 6 * l + 6)
                with dve.Fori(0, SEQ // 4) as i:
                    for r in range(4):
                        dve.wait_ge(hot_used, l * SEQ + i * 4 + (r + 1))
                        nc.vector.tensor_scalar(onehot_a[:, r, :], iota, idx1T[:, bass.ds(i * 4 + r, 1)],
                                                gateT[:, bass.ds(i * 4 + r, 1)], ALU.is_equal,
                                                ALU.mult).then_inc(hot_a, 1)
                dve.wait_ge(g_free, l * (SEQ // 4) + (SEQ // 4 + 2))

                def weigh(n, s):
                    dve.wait_ge(out_free, l * OUTS + n + (O_PEER + 3))
                    g = arena[:, bass.ds(n, 1), :].squeeze(1) if not isinstance(n, int) else arena[:, n, :]
                    nc.vector.tensor_tensor(w_f[:, s, :], act_g[:, s, :], g, ALU.mult).then_inc(w_made, 1)

                def w_rests(n, s):
                    dve.wait_ge(w_head, l * NKEYS + n + 1)
                    nc.vector.tensor_tensor(w_lo[:, s, :], w_f[:, s, :], w_hi[:, s, :].bitcast(f32),
                                            ALU.subtract).then_inc(w_rest, 1)

                E0 = L0 + T_PEER
                rest_of(E0 + 1, 1)
                weigh(0, 0)
                w_rests(0, 0)
                with dve.Fori(0, NKEYS // 2 - 1) as i:
                    rest_of(E0 + i * 4 + 2, 2)
                    weigh(i * 2 + 1, 1)
                    rest_of(E0 + i * 4 + 3, 3)
                    w_rests(i * 2 + 1, 1)
                    rest_of(E0 + i * 4 + 4, 0)
                    weigh(i * 2 + 2, 0)
                    rest_of(E0 + i * 4 + 5, 1)
                    w_rests(i * 2 + 2, 0)
                rest_of(E0 + 254, 2)
                weigh(NKEYS - 1, 1)
                rest_of(E0 + 255, 3)
                w_rests(NKEYS - 1, 1)
                dve.wait_ge(tile_done, L0 + TILES + 2)
                nc.vector.tensor_copy(ftok, wk[:, 2:6, :].rearrange("p (b e) c -> p b (e c)", b=2)).then_inc(f_tok, 1)
                for k in range(KC):
                    if k % 2 == 0:
                        dve.wait_ge(f_tr, 4 * l + k // 2 + 1)
                    e = nc.vector.scalar_tensor_tensor(
                        x[:, k, :], wk[:, 2 + k // 2, (k % 2) * SEQ:(k % 2 + 1) * SEQ], mod[:, 40 + k:41 + k],
                        x[:, k, :], ALU.mult, ALU.add)
                e.then_inc(x_ready, 1)
                dve.wait_ge(x_ready, 2 * l + 3)
                dve.sem_inc(arena_free, 1)

        @block.tensor
        def _(pe):
            def product(out, w_h, w_l, m_h, m_l, first, last):
                pe.matmul(out, w_h, m_h, start=first, stop=False)
                pe.matmul(out, w_h, m_l, start=False, stop=False)
                return pe.matmul(out, w_l, m_h, start=False, stop=last)

            def chunk(j, k):
                return hi[j % SPLIT][:, k * P:(k + 1) * P], lo[j % SPLIT][:, k * P:(k + 1) * P]

            pe.sem_inc(tile_done, 2)
            pe.sem_inc(out_free, 2)
            pe.sem_inc(hot_used, 4)
            pe.sem_inc(g_free, 2)
            pe.wait_ge(c_ready, 1)
            with pe.Fori(0, DEPTH) as l:
                L0 = l * TILES

                def norm(n):
                    pe.wait_ge(sq_ready, 2 * l + n + 1)
                    for k in range(KC):
                        last = pe.matmul(wk[:, 0, 0:SEQ], ones, sq[:, k, :], start=k == 0, stop=k == KC - 1)
                    last.then_inc(ss_ready, 1)

                def project(t, j, o):
                    pe.wait_ge(lo_done, t + 1)
                    pe.wait_ge(out_free, l * OUTS + o + 1)
                    for k in range(KC):
                        last = product(pj[j % 2][:, 0:SEQ], *chunk(j, k), mov_hi[:, k, :], mov_lo[:, k, :],
                                       k == 0, k == KC - 1)
                    return last

                with pe.Fori(0, N_ADA // 4) as i:
                    for j in range(4):
                        pe.wait_ge(lo_done, L0 + i * 4 + (j + 1))
                        for k in range(KC):
                            last = product(wk[:, 1, bass.ds(i * 8 + 2 * j, 2)], *chunk(j, k), c_hi[:, k, :],
                                           c_lo[:, k, :], k == 0, k == KC - 1)
                        last.then_inc(tile_done, 1)
                norm(0)
                wait_alone(pe, mov_ready, 9 * l + 1)
                with pe.Fori(0, (N_QKV + N_GATE) // 4) as i:
                    for j in range(4):
                        project(L0 + i * 4 + (T_QKV + j), j, i * 4 + j).then_inc(tile_done, 1)
                pe.wait_ge(out_free, l * OUTS + (O_BR + 2))
                for b in range(2):
                    for n, t in enumerate(V_TILES):
                        c = b * 1536 + n * P
                        last = pe.transpose(wkf[:, c:c + P], projT[:, t, b * P:(b + 1) * P], ident)
                    last.then_inc(vtr, 1)
                for g, (t0, n) in enumerate(((QA, 5), (QB, 8))):
                    pe.wait_ge(qk_sq, 2 * l + g + 1)
                    if g == 0:
                        pe.wait_ge(vtok_in, 2 * l + 2)
                    else:
                        pe.wait_ge(qk_rr, 2 * l + 1)
                    for k in range(n):
                        last = pe.matmul(wkf[:, k * SEQ:(k + 1) * SEQ], blk, sq[:, k, :], start=True, stop=True)
                    last.then_inc(qk_ss, 1)
                pe.wait_ge(qk_done, 2 * l + 2)
                for br in range(2):
                    if br:
                        pe.wait_ge(f_ready, l + 1)

                    def scores(h):
                        n = 8 * br + h
                        if n >= 4:
                            pe.wait_ge(score_read, 16 * l + n - 3)
                        if br == 0:
                            o = (h // 4) * HD
                            q, k = projT[o:o + HD, QA + h % 4, :], projT[o:o + HD, KA, :]
                        else:
                            o = (h % 2) * HD
                            q, k = projT[o:o + HD, QB + h // 2, :], projT[o:o + HD, KB + h // 2, :]
                        s = wk[:, 2 + h % 4, :]
                        hot = ident[0:HEADS, h:h + 1].to_broadcast([HEADS, P])
                        for q0, nk, c0 in ((0, P, 0), (P, 2 * P, P)):
                            last = pe.matmul(s[:, c0:c0 + nk], q[:, q0:q0 + P], k[:, 0:nk], start=True, stop=br == 0)
                            if br:
                                last = pe.matmul(s[:, c0:c0 + nk], hot, fl[:, 3, 0:nk], start=False, stop=True)
                        last.then_inc(score_ready, 1)

                    def turn(h):
                        n = 8 * br + h
                        pe.wait_ge(prob_ready, 16 * l + n + 1)
                        if n >= 2:
                            pe.wait_ge(pt_copied, 16 * l + n - 1)
                        for c in range(3):
                            last = pe.transpose(wk[:, h % 2, c * P:(c + 1) * P], prob[:, h, c * P:(c + 1) * P], ident)
                        last.then_inc(ptr_ready, 1)

                    def values(h):
                        n = 8 * br + h
                        pe.wait_ge(pt_copied, 16 * l + n + 1)
                        if h == 0 and br:
                            pe.wait_ge(y_read, 3 * l + 1)
                        v = (h // 4) * HD if br == 0 else P + h * HD
                        o = slice(h * HD, (h + 1) * HD)
                        pt = probT[:, h % 2, :]
                        pe.matmul(pj[0][:, o], pt[:, 0:P], vtok[:, 0, v:v + HD], start=True, stop=True)
                        pe.matmul(pj[1][:, o], pt[:, P:2 * P], vtok[:, 0, v:v + HD], start=True, stop=False)
                        pe.matmul(pj[1][:, o], pt[:, 2 * P:3 * P], vtok[:, 1, v:v + HD], start=False,
                                  stop=True).then_inc(pv_done, 1)

                    for h in range(HEADS):
                        scores(h)
                    turn(0)
                    for h in range(HEADS):
                        if h + 1 < HEADS:
                            turn(h + 1)
                        values(h)
                def logits(h):
                    if h >= 2:
                        pe.wait_ge(z_read, 8 * l + h - 1)
                    else:
                        pe.wait_ge(score_read, 16 * l + 16)
                    o = (h % 2) * HD
                    q, k = projT[o:o + HD, QC + h // 2, :], projT[o:o + HD, KCT + h // 2, :]
                    z = wk[:, 2 + h % 2, :]
                    pe.matmul(z[:, 0:SEQ], k[:, 0:P], q, start=True, stop=True)
                    pe.matmul(z[:, SEQ:SEQ + P], k[:, P:2 * P], q[:, P:2 * P], start=True,
                              stop=True).then_inc(z_ready, 1)

                def tails(h):
                    pe.wait_ge(z_read, 8 * l + h + 1)
                    if h >= 2:
                        pe.wait_ge(stick_arg, 8 * l + h - 1)
                    t = wk[:, 4 + h % 2, :]
                    sp_ = stick[:, h % 2, 1, :]
                    pe.matmul(t[:, 0:P], tri, sp_[:, 0:P], start=True, stop=True)
                    pe.matmul(t[:, P:2 * P], tri, sp_[:, P:2 * P], start=True, stop=False)
                    pe.matmul(t[:, P:2 * P], ones, sp_[:, 2 * P:3 * P], start=False, stop=True)
                    pe.matmul(t[:, 2 * P:3 * P], tri, sp_[:, 2 * P:3 * P], start=True,
                              stop=True).then_inc(tail_ready, 1)

                def stick_values(h):
                    pe.wait_ge(stick_ready, 8 * l + h + 1)
                    if h == 0:
                        pe.wait_ge(y_read, 3 * l + 2)
                    v = P + 512 + h * HD
                    o = slice(h * HD, (h + 1) * HD)
                    a = stick[:, h % 2, 3, :]
                    pe.matmul(pj[0][:, o], a[:, 0:P], vtok[:, 0, v:v + HD], start=True, stop=True)
                    pe.matmul(pj[1][:, o], a[:, P:2 * P], vtok[:, 0, v:v + HD], start=True, stop=False)
                    pe.matmul(pj[1][:, o], a[:, 2 * P:3 * P], vtok[:, 1, v:v + HD], start=False,
                              stop=True).then_inc(pv_done, 1)

                logits(0)
                for h in range(HEADS):
                    if h + 1 < HEADS:
                        logits(h + 1)
                    tails(h)
                    if h:
                        stick_values(h - 1)
                stick_values(HEADS - 1)
                pe.wait_ge(y_read, 3 * l + 3)
                for n in range(6):
                    br, b = n // 2, n % 2
                    for c in range(4):
                        last = pe.transpose(wk[:, n, c * P:(c + 1) * P], ytok[:, b, br, c * P:(c + 1) * P], ident)
                    last.then_inc(ytr, 1)
                wait_alone(pe, mov_ready, 9 * l + 7)
                with pe.Fori(0, 3) as br:
                    for j in range(4):
                        pe.wait_ge(lo_done, L0 + br * 4 + (T_BR + j + 1))
                        pe.wait_ge(out_free, l * OUTS + br * 4 + (O_BR + j + 1))
                        for o in range(2):
                            for k in range(4):
                                last = product(pj[j % 2][:, o * SEQ:(o + 1) * SEQ], *chunk(j, 4 * o + k),
                                               mov_hi[:, bass.ds(br * 4 + k, 1), :].squeeze(1),
                                               mov_lo[:, bass.ds(br * 4 + k, 1), :].squeeze(1), k == 0, k == 3)
                        last.then_inc(tile_done, 1)
                wait_alone(pe, mov_ready, 9 * l + 8)
                with pe.Fori(0, N_OUT // 4) as i:
                    for j in range(4):
                        project(L0 + i * 4 + (T_OUT + j), j, i * 4 + (O_OUT + j)).then_inc(tile_done, 1)
                norm(1)
                wait_alone(pe, mov_ready, 9 * l + 9)
                with pe.Fori(0, N_QUERY // 4) as i:
                    for j in range(4):
                        project(L0 + i * 4 + (T_QUERY + j), j, i * 4 + (O_QUERY + j)).then_inc(tile_done, 1)
                pe.wait_ge(q_sq, l + 1)
                pe.wait_ge(rstd_ready, 2 * l + 2)
                for k in range(KC):
                    last = pe.matmul(wkf[:, k * SEQ:(k + 1) * SEQ], ones, sq[:, k, :], start=True, stop=True)
                last.then_inc(q_ss, 1)
                pe.wait_ge(q_norm, l + 1)
                pe.wait_ge(keys_in, 16 * l + 16)
                for u in range(16):
                    b, h = u // 8, u % 8
                    if u >= 12 and u % 2 == 0:
                        pe.wait_ge(s_copied, 8 * l + u // 2 - 5)
                    pe.matmul(wk[:, (u // 2) % 6, (u % 2) * 256:(u % 2 + 1) * 256], queryT[:, h, b * P:(b + 1) * P],
                              skeys[:, h, :], start=True, stop=True).then_inc(s_ready, 1)
                pe.wait_ge(route_ready, l + 1)
                pe.wait_ge(s_copied, 8 * l + 8)
                tsf = top_s.rearrange("p u k -> p (u k)")
                for n, src in enumerate((idx_tok[:, 0, :], idx_tok[:, 1, :], tsf)):
                    for b in range(2):
                        pe.transpose(wk[:, 2 * n + b, 0:P], src[:, b * P:(b + 1) * P], ident).then_inc(route_tr, 1)
                wait_alone(pe, route_in, 6 * l + 6)
                with pe.Fori(0, SEQ // 8) as i:
                    for r in range(8):
                        pe.wait_ge(hot_a, l * SEQ + i * 8 + (r + 1))
                        pe.wait_ge(hot_b, l * SEQ + i * 8 + (r + 1))
                        if r % 4 == 0:
                            pe.wait_ge(g_free, l * (SEQ // 4) + i * 2 + (r // 4 + 1))
                        pe.matmul(wk[:, r // 4, (r % 4) * P:(r % 4 + 1) * P], onehot_a[:, r % 4, :],
                                  onehot_b[:, r % 4, :], start=True, stop=True).then_inc(hot_used, 1)

                def up(t, j, n):
                    project(t, j, n + O_PEER, ).then_inc(tile_done, 1)

                def down(t, j, n, s, last_group=False):
                    pe.wait_ge(lo_done, t + 1)
                    pe.wait_ge(w_rest, l * NKEYS + n + 1)
                    vh, vl = hi[j % SPLIT], lo[j % SPLIT]
                    for b in range(2):
                        wh, wl = w_hi[:, s, b * P:(b + 1) * P], w_lo[:, s, b * P:(b + 1) * P]
                        for e in range(2):
                            last = product(wk[:, 2 + 2 * b + e, :], wh, wl, vh[:, e * 512:(e + 1) * 512],
                                           vl[:, e * 512:(e + 1) * 512], False, last_group)
                    last.then_inc(tile_done, 1)

                E0 = L0 + T_PEER
                for c in range(4):
                    pe.matmul(wk[:, 2 + c, :], zero, const[:, 0:512], start=True, stop=False)
                up_bank = 0
                project(E0, 0, O_PEER).then_inc(tile_done, 1)
                with pe.Fori(0, NKEYS // 2 - 1) as i:
                    for q in range(2):
                        t = E0 + i * 4 + (1 + 2 * q)
                        pe.wait_ge(lo_done, t + 1)
                        pe.wait_ge(out_free, l * OUTS + i * 2 + (O_PEER + 2 + q))
                        for k in range(KC):
                            last = product(pj[(1 + q) % 2][:, 0:SEQ], *chunk(1 + 2 * q, k), mov_hi[:, k, :],
                                           mov_lo[:, k, :], k == 0, k == KC - 1)
                        last.then_inc(tile_done, 1)
                        down(t + 1, 2 + 2 * q, i * 2 + q, q)
                t = E0 + 253
                pe.wait_ge(lo_done, t + 1)
                pe.wait_ge(out_free, l * OUTS + (O_PEER + NKEYS))
                for k in range(KC):
                    last = product(pj[1][:, 0:SEQ], *chunk(1, k), mov_hi[:, k, :], mov_lo[:, k, :], k == 0,
                                   k == KC - 1)
                last.then_inc(tile_done, 1)
                down(E0 + 254, 2, NKEYS - 2, 0)
                down(E0 + 255, 3, NKEYS - 1, 1, True)
                pe.wait_ge(f_tok, l + 1)
                for k in range(KC):
                    for b in range(2):
                        c = (k % 2) * SEQ + b * P
                        last = pe.transpose(wk[:, 2 + k // 2, c:c + P], ftok[:, b, k * P:(k + 1) * P], ident)
                    if k % 2:
                        last.then_inc(f_tr, 1)


def _rows(w):
    k, n = w.shape[0] // P, w.shape[1] // P
    return w.reshape(k, P, n, P).transpose(2, 1, 0, 3).reshape(n, P, k * P)


def _lay_out(np, i):
    qh = [h for t in range(4) for h in (t, t + 4)]
    tiles = []
    for l in range(DEPTH):
        w = i["w_in"][l]
        cut = np.split(w, [512, 640, 768, 1280, 1792, 2304, 2312, 2824, 3336, 3848], axis=1)
        qa, ka, va, qb, kb, vb, fb, qc, kc, vc, gates = cut
        qa = qa.reshape(D, 8, HD)[:, qh].reshape(D, 512)
        fb = np.concatenate([fb, np.zeros((D, P - 8), fb.dtype)], 1)
        blank = np.zeros((D, P), w.dtype)
        tiles.append(_rows(i["w_ada"][l]))
        tiles.append(_rows(np.concatenate([qa, ka, va, qb, kb, vb, fb, qc, kc, vc, blank, gates], 1)))
        for b in "abc":
            wo = i["w_out_" + b][l]
            t = wo.reshape(4, P, 4, 2, P).transpose(2, 1, 3, 0, 4)
            tiles.append(t.reshape(4, P, 1024))
        tiles.append(_rows(i["w_out"][l]))
        tiles.append(_rows(i["w_query"][l]))
        u = i["expert_u"][l].reshape(NKEYS, NKEYS, KC, P).transpose(1, 3, 2, 0).reshape(NKEYS, P, 1024)
        v = i["expert_v"][l].reshape(NKEYS, NKEYS, D).transpose(1, 0, 2)
        mix = np.empty((N_PEER, P, 1024), u.dtype)
        mix[0] = u[0]
        mix[1:254:2] = u[1:]
        mix[2:255:2] = v[:127]
        mix[255] = v[127]
        tiles.append(mix)
    stream = np.concatenate(tiles)
    par = np.zeros((P, DEPTH, NPAR), np.float32)
    for l in range(DEPTH):
        q = par[:, l]
        q[:, PB_ADA:PB_ADA + 48] = i["b_ada"][l].reshape(48, P).T
        q[:, PG1:PG1 + 8] = i["norm1_g"][l].reshape(8, P).T
        q[:, PG2:PG2 + 8] = i["norm2_g"][l].reshape(8, P).T
        q[:, PBG:PBG + 24] = i["b_gate"][l].reshape(24, P).T
        for c, n in ((PQA, "q_norm_a"), (PKA, "k_norm_a"), (PQB, "q_norm_b"), (PKB, "k_norm_b")):
            q[:, c] = np.concatenate([i[n][l], i[n][l]])
        q[:, PQP] = i["q_norm_peer"][l]
        q[:, PSINK:PSINK + 8] = i["sinks"][l]
        q[0:8, PBF] = i["b_forget"][l]
    r = np.arange(P)
    const = np.zeros((P, NCONST), np.float32)
    const[:, C_ID:C_ID + P] = np.eye(P)
    const[:, C_ONE:C_ONE + P] = 1
    const[:, C_BLK:C_BLK + P] = (r[:, None] // HD) == (r[None] // HD)
    const[:, C_TRI:C_TRI + P] = r[:, None] > r[None]
    const[:, C_IOTA:C_IOTA + P] = r[None]
    before = (r[:, None] < r[None]).astype(np.float32)
    const[:, C_CM:C_CM + 384] = np.concatenate([before, np.ones((P, P)), before], 1)
    late = np.where(r[None] <= r[:, None], 0, NEG)
    const[:, C_BT:C_BT + 384] = np.concatenate([late, np.zeros((P, P)), late], 1)
    const[:, C_EPS] = EPS
    chunk = r // 64
    own = np.where(chunk[:, None] >= chunk[None], 0, NEG)
    prev = np.where((chunk[:, None] + 2 - chunk[None]) < 2, 0, NEG)
    d_own, d_prev = np.abs(r[:, None] - r[None]), r[:, None] - (r[None] - P)
    taba = np.zeros((P, HEADS, 384), np.float32)
    for h in range(HEADS):
        s = 2.0 ** -(h + 1)
        a, b = own - s * d_own, prev - s * d_prev
        taba[:, h] = np.concatenate([a, b, a], 1)
    keys = np.zeros((DEPTH, P, PEER_HEADS, 256), np.float32)
    keys[:, 0:64, :, 0:128] = i["sub_keys_1"].transpose(0, 3, 1, 2)
    keys[:, 64:128, :, 128:256] = i["sub_keys_2"].transpose(0, 3, 1, 2)
    xT = i["x"][0].reshape(SEQ, KC, P).transpose(2, 1, 0)
    cT = i["c"][0].reshape(KC, P).T
    return {"stream": stream, "par": par, "const": const, "taba": taba, "keys": keys,
            "xT": xT, "cT": cT}


def kernel(**inputs):
    import numpy as np
    import concourse.bacc as bacc
    from concourse.bass_utils import run_bass_kernel_spmd

    arrays = {k: np.ascontiguousarray(v) for k, v in _lay_out(np, {k: np.asarray(v) for k, v in inputs.items()}).items()}
    nc = bacc.Bacc("TRN2", target_bir_lowering=False, num_devices=1)
    args = [nc.dram_tensor("in_" + n, a.shape, mybir.dt.float32, kind="ExternalInput").ap() for n, a in arrays.items()]
    out = nc.dram_tensor("out", (P, KC, SEQ), mybir.dt.float32, kind="ExternalOutput").ap()
    trunk(nc, *args, out)
    r = run_bass_kernel_spmd(nc, [{"in_" + n: a for n, a in arrays.items()}], core_ids=[0])
    got = r.results[0]["out"]
    return got.transpose(2, 1, 0).reshape(1, SEQ, D)
```

```python
import concourse.bass as bass
from concourse import mybir
from contextlib import ExitStack

DEPTH, SEQ, D = 2, 256, 1024
P = 128
KC = D // P
HD = 64
HEADS = 8
EPS = 1e-6
PEER_HEADS, TOPK, NKEYS = 8, 16, 128
NEG = -1e30

N_ADA = 6 * KC
N_QKV = 32
N_GATE = 3 * KC
N_BR = 12
N_OUT = KC
N_QUERY = KC
N_PEER = 2 * NKEYS
ADA_FIRST = 2 * KC
EARLY = 88
BOTH = NKEYS - EARLY
T_QKV = ADA_FIRST
T_GATE = T_QKV + 2 * N_QKV
T_BR = T_GATE + N_GATE
T_OUT = T_BR + N_BR
T_QUERY = T_OUT + N_OUT
T_PEER = T_QUERY + N_QUERY
T_BOTH = T_PEER + EARLY
T_DOWN = T_BOTH + 2 * BOTH
TILES = T_PEER + N_PEER
assert N_ADA == ADA_FIRST + N_QKV and TILES == T_DOWN + EARLY
RAW = 4
SPLIT = 2
O_GATE = N_QKV
O_BR = O_GATE + N_GATE
O_OUT = O_BR + N_BR
O_QUERY = O_OUT + N_OUT
O_PEER = O_QUERY + N_QUERY
OUTS = O_PEER + NKEYS

QA, KA, VA, QB, KB, VB, FG, QC, KCT, VC = 0, 4, 5, 6, 10, 14, 18, 19, 23, 27
V_TILES = [VA] + [VB + i for i in range(4)] + [VC + i for i in range(4)]

PB_ADA, PG1, PG2, PBG = 0, 48, 56, 64
PQA, PKA, PQB, PKB, PQP, PSINK, PBF = 88, 89, 90, 91, 92, 93, 101
NPAR = 102
C_ID, C_ONE, C_BLK, C_TRI, C_IOTA, C_ZERO, C_CM, C_BT, C_EPS = 0, 128, 256, 384, 512, 640, 768, 1152, 1536
NCONST = 1540


def trunk(nc, stream, par_dram, const_dram, taba_dram, keys_dram, x_dram, c_dram, out_dram):
    f32, f32r, u32 = mybir.dt.float32, mybir.dt.float32r, mybir.dt.uint32
    ALU, ACT, AX = mybir.AluOpType, mybir.ActivationFunctionType, mybir.AxisListType

    ctx = ExitStack()
    with ctx:
        def sb(name, shape, dt=f32):
            return ctx.enter_context(nc.sbuf_tensor(name, shape, dt))

        def sem(name):
            return ctx.enter_context(nc.semaphore(name))

        raw = [sb(f"raw{i}", [P, 1024]) for i in range(RAW)]
        hi = [sb(f"hi{i}", [P, 1024], f32r) for i in range(SPLIT)]
        lo = [sb(f"lo{i}", [P, 1024], f32r) for i in range(SPLIT)]
        x = sb("x", [P, KC, SEQ])
        mov_hi = sb("mov_hi", [P, 12, SEQ], f32r)
        mov_lo = sb("mov_lo", [P, 12, SEQ], f32r)
        w_hi = mov_hi[:, KC:KC + 4, :]
        w_lo = mov_lo[:, KC:KC + 4, :]
        const = sb("const", [P, NCONST])
        par_all = sb("par_all", [P, DEPTH, NPAR])
        par = sb("par", [P, NPAR])
        c_in = sb("c_in", [P, KC])
        c_tmp = sb("c_tmp", [P, KC])
        c_hi = sb("c_hi", [P, KC], f32r)
        c_lo = sb("c_lo", [P, KC], f32r)
        mod = sb("mod", [P, N_ADA])
        amp = sb("amp", [P, 2, KC])
        gain = sb("gain", [P, 2])
        small = sb("small", [P, 96])
        idx1T = sb("idx1T", [P, SEQ])
        idx2T = sb("idx2T", [P, SEQ])
        gateT = sb("gateT", [P, SEQ])
        onehot_a = sb("onehot_a", [P, 8, NKEYS])
        onehot_b = w_hi.rearrange("p a b -> p (a b)").rearrange("p (r i) -> p r i", r=8)
        act_g = onehot_a[:, 0:4, :].rearrange("p a b -> p (a b)").rearrange("p (r s) -> p r s", r=2)
        rstd = act_g[:, 0, :]

        ident = const[:, C_ID:C_ID + P]
        ones = const[:, C_ONE:C_ONE + P]
        blk = const[:, C_BLK:C_BLK + P]
        tri = const[:, C_TRI:C_TRI + P]
        iota = const[:, C_IOTA:C_IOTA + P]
        zero = const[:, C_ZERO:C_ZERO + P]
        cmask = const[:, C_CM:C_CM + 384]
        btab = const[:, C_BT:C_BT + 384]
        eps = const[:, C_EPS:C_EPS + 1]
        mx, negm, den, sinkd = small[:, 0:16], small[:, 16:32], small[:, 32:48], small[:, 48:64]
        rden = small[:, 64:80]

        arena = sb("arena", [P, NKEYS, SEQ])
        flat = arena[:, :, :].rearrange("p a b -> p (a b)")
        used = [0]

        def part(n):
            a = flat[:, used[0]:used[0] + n]
            used[0] += n
            return a

        projT = part(56 * SEQ).rearrange("p (t s) -> p t s", s=SEQ)
        vtok = part(2 * 1152).rearrange("p (b c) -> p b c", b=2)
        taba = part(HEADS * 384).rearrange("p (h c) -> p h c", h=HEADS)
        prob = part(HEADS * 384).rearrange("p (h c) -> p h c", h=HEADS)
        probT = part(2 * 384).rearrange("p (r c) -> p r c", r=2)
        ytok = part(2 * 3 * 512).rearrange("p (b r c) -> p b r c", b=2, r=3)
        merged = part(KC * SEQ).rearrange("p (k s) -> p k s", s=SEQ)
        gated = part(2 * 512).rearrange("p (r c) -> p r c", r=2)
        sq = part(KC * SEQ).rearrange("p (k s) -> p k s", s=SEQ)
        assert used[0] <= NKEYS * SEQ, used
        stick = prob.rearrange("p h c -> p (h c)")[:, 0:8 * 384].rearrange("p (r n c) -> p r n c", r=2, n=4)
        used[0] = EARLY * SEQ
        keys_at = used[0]
        skeys = part(PEER_HEADS * 256).rearrange("p (h c) -> p h c", h=PEER_HEADS)
        query_at = used[0]
        queryT = part(KC * SEQ).rearrange("p (k s) -> p k s", s=SEQ)
        score_at = used[0]
        score = part(16 * 256).rearrange("p (u c) -> p u c", u=16)
        rest = part(2 * 128).rearrange("p (r c) -> p r c", r=2)
        cand = part(256)
        candr = part(256)
        sel_v = part(2 * 16).rearrange("p (n k) -> p n k", n=2)
        sel_i = part(16 * 32).rearrange("p (u n k) -> p u n k", u=16, n=2).bitcast(u32)
        top_s = part(16 * 16).rearrange("p (u k) -> p u k", u=16)
        top_p = part(16 * 16).rearrange("p (u k) -> p u k", u=16).bitcast(u32)
        gsum = part(2 * 16).rearrange("p (n c) -> p n c", n=2)
        assert used[0] <= NKEYS * SEQ, used
        used[0] = score_at
        sq2 = part(KC * SEQ).rearrange("p (k s) -> p k s", s=SEQ)
        used[0] = keys_at
        sel_if = part(16 * 32).rearrange("p (u n k) -> p u n k", u=16, n=2)
        pos_i = part(2 * 256).rearrange("p (n c) -> p n c", n=2).bitcast(u32)
        pos_f = part(2 * 256).rearrange("p (n c) -> p n c", n=2)
        idx_tok = part(2 * 256).rearrange("p (n c) -> p n c", n=2)
        assert used[0] <= query_at
        used[0] = query_at
        pick = part(8 * 256)
        ftok = arena[:, 0:8, :].rearrange("p a b -> p (a b)").rearrange("p (b c) -> p b c", b=2)
        fl = sq[0:HEADS, 0:4, :]

        pj = [ctx.enter_context(nc.psum_tensor(f"pj{i}", [P, 512], f32)) for i in range(2)]
        wk = ctx.enter_context(nc.psum_tensor("wk", [P, 6, 512], f32))
        wkf = wk[:, :, :].rearrange("p b c -> p (b c)")

        def group_of(n):
            return arena[:, n, :] if isinstance(n, int) else arena[:, bass.ds(n, 1), :].squeeze(1)

        setup_loaded = sem("setup_loaded")
        setup_step = sem("setup_step")
        c_exp = sem("c_exp")
        c_ready = sem("c_ready")
        raw_loaded = [sem(f"raw_loaded{i}") for i in range(RAW)]
        hi_done = sem("hi_done")
        lo_done = sem("lo_done")
        tile_done = sem("tile_done")
        out_free = sem("out_free")
        x_ready = sem("x_ready")
        sq_ready = sem("sq_ready")
        ss_ready = sem("ss_ready")
        rstd_ready = sem("rstd_ready")
        h_ready = sem("h_ready")
        h_hi = sem("h_hi")
        mov_ready = sem("mov_ready")
        tables = sem("tables")
        arena_free = sem("arena_free")
        keys_free = sem("keys_free")
        keys_in = sem("keys_in")
        vtr = sem("vtr")
        vtok_in = sem("vtok_in")
        qk_sq = sem("qk_sq")
        qk_ss = sem("qk_ss")
        qk_rr = sem("qk_rr")
        qk_done = sem("qk_done")
        f_sum = sem("f_sum")
        f_log = sem("f_log")
        f_ready = sem("f_ready")
        score_ready = sem("score_ready")
        score_read = sem("score_read")
        negmax = sem("negmax")
        sinkd_exp = sem("sinkd_exp")
        prob_ready = sem("prob_ready")
        ptr_ready = sem("ptr_ready")
        pt_copied = sem("pt_copied")
        pv_done = sem("pv_done")
        y_read = sem("y_read")
        z_ready = sem("z_ready")
        z_log = sem("z_log")
        z_read = sem("z_read")
        tail_ready = sem("tail_ready")
        stick_arg = sem("stick_arg")
        stick_exp = sem("stick_exp")
        stick_ready = sem("stick_ready")
        ytr = sem("ytr")
        y_hi = sem("y_hi")
        br_mul = sem("br_mul")
        br_add = sem("br_add")
        q_sq = sem("q_sq")
        q_ss = sem("q_ss")
        q_rr = sem("q_rr")
        q_norm = sem("q_norm")
        s_ready = sem("s_ready")
        s_copied = sem("s_copied")
        g_arg = sem("g_arg")
        g_exp = sem("g_exp")
        route_ready = sem("route_ready")
        route_tr = sem("route_tr")
        route_in = sem("route_in")
        hot_a = sem("hot_a")
        hot_b = sem("hot_b")
        hot_used = sem("hot_used")
        hot_dist = sem("hot_dist")
        g_times = sem("g_times")
        g_free = sem("g_free")
        mod_read = sem("mod_read")
        mod_sum = sem("mod_sum")
        w_made = sem("w_made")
        w_head = sem("w_head")
        w_rest = sem("w_rest")
        f_tok = sem("f_tok")
        f_tr = sem("f_tr")
        stored = sem("stored")
        waits_met = sem("waits_met")
        act_step = sem("act_step")
        dve_step = sem("dve_step")

        def wait_alone(eng, s, value):
            eng.wait_ge(s, value)
            eng.sem_inc(waits_met, 1)

        block = ctx.enter_context(nc.Block())

        @block.sync
        def _(sp):
            sp.dma_start(const[:, :], const_dram).then_inc(setup_loaded, 16)
            sp.dma_start(par_all[:, :, :], par_dram).then_inc(setup_loaded, 16)
            sp.dma_start(c_in[:, :], c_dram).then_inc(setup_loaded, 16)
            for j in range(RAW):
                sp.dma_start(raw[j][:, :], stream[j]).then_inc(raw_loaded[j], 16)
                if j == 1:
                    sp.dma_start(x[:, :, :], x_dram).then_inc(setup_loaded, 16)
            with sp.Fori(0, DEPTH * TILES // RAW - 1) as i:
                for j in range(RAW):
                    sp.wait_ge(lo_done, i * RAW + j + 1)
                    sp.dma_start(raw[j][:, :], stream[i * RAW + RAW + j]).then_inc(raw_loaded[j], 16)
            sp.wait_ge(x_ready, 2 * DEPTH + 1)
            sp.dma_start(out_dram, x[:, :, :]).then_inc(stored, 16)
            sp.wait_ge(stored, 16)

        @block.gpsimd
        def _(pool):
            with pool.Fori(0, DEPTH) as l:
                wait_alone(pool, arena_free, l + 1)
                pool.dma_start(taba, taba_dram).then_inc(tables, 16)
                wait_alone(pool, keys_free, l + 1)
                pool.dma_start(skeys, keys_dram[l]).then_inc(keys_in, 16)

        @block.scalar
        def _(act):
            def head(t, j):
                act.wait_ge(raw_loaded[j % RAW], 16 + load_count(t, j))
                act.wait_ge(tile_done, t + 1)
                nc.scalar.activation(hi[j % SPLIT][:, :], raw[j % RAW][:, :], ACT.Copy).then_inc(hi_done, 1)

            def load_count(t, j):
                return (t - (j % RAW)) * (16 // RAW)

            act.wait_ge(setup_loaded, 64)
            nc.scalar.activation(c_tmp[:, :], c_in[:, :], ACT.Exp, scale=-1.0).then_inc(c_exp, 1)
            with act.Fori(0, DEPTH) as l:
                act.sem_clear(act_step)
                n_link = [0]
                L0 = l * TILES

                def link(ins):
                    ins.then_inc(act_step, 1)
                    n_link[0] += 1
                    act.wait_ge(act_step, n_link[0])

                def norm(n, sq):
                    act.wait_ge(x_ready, 2 * l + n + 1)
                    nc.scalar.activation(sq, x[:, :, :], ACT.Square).then_inc(sq_ready, 1)
                    act.wait_ge(ss_ready, 2 * l + n + 1)
                    link(nc.scalar.activation(rstd, wk[:, 0, 0:SEQ], ACT.Ln, bias=eps, scale=1.0 / D))
                    nc.scalar.activation(rstd, rstd, ACT.Exp, scale=-0.5).then_inc(rstd_ready, 1)
                    act.wait_ge(h_ready, 3 * l + (1 if n == 0 else 3))
                    nc.scalar.activation(mov_hi[:, 0:KC, :], sq, ACT.Copy).then_inc(h_hi, 1)

                nc.scalar.preload_act_table_set("natural_log_exp_and_others")
                head(L0, 0)
                head(L0 + 1, 1)
                with act.Fori(0, ADA_FIRST // 4) as i:
                    for j in range(4):
                        head(L0 + i * 4 + (j + 2), j + 2)
                norm(0, sq)
                with act.Fori(0, N_QKV // 4) as i:
                    for j in range(4):
                        t = L0 + i * 8 + (T_QKV + 2 * j)
                        head(t + 2, 2 * j + 2)
                        act.wait_ge(tile_done, t + 3)
                        nc.scalar.activation(projT[:, bass.ds(i * 4 + j, 1), :].squeeze(1), pj[j % 2][:, 0:SEQ],
                                             ACT.Copy).then_inc(out_free, 1)
                        head(t + 3, 2 * j + 3)
                nc.scalar.preload_act_table_set("sigmoid_and_others")
                with act.Fori(0, N_GATE // 4) as i:
                    for j in range(4):
                        t = L0 + i * 4 + (T_GATE + j)
                        head(t + 2, j + 2)
                        act.wait_ge(tile_done, t + 3)
                        nc.scalar.activation(projT[:, bass.ds(i * 4 + (N_QKV + j), 1), :].squeeze(1),
                                             pj[j % 2][:, 0:SEQ], ACT.Sigmoid,
                                             bias=par[:, bass.ds(i * 4 + (PBG + j), 1)]).then_inc(out_free, 1)
                nc.scalar.preload_act_table_set("natural_log_exp_and_others")
                for b in range(2):
                    act.wait_ge(vtr, 2 * l + b + 1)
                    nc.scalar.activation(vtok[:, b, :], wkf[:, b * 1536:b * 1536 + 1152], ACT.Copy)\
                        .then_inc(vtok_in, 1)
                act.wait_ge(out_free, l * OUTS + (O_BR + 2))
                for g, (t0, n) in enumerate(((QA, 5), (QB, 8))):
                    if g:
                        act.wait_ge(qk_done, 2 * l + 1)
                    nc.scalar.activation(sq[:, 0:n, :], projT[:, t0:t0 + n, :], ACT.Square).then_inc(qk_sq, 1)
                    act.wait_ge(qk_ss, 2 * l + g + 1)
                    sqf = sq.rearrange("p k s -> p (k s)")[:, 0:n * SEQ]
                    link(nc.scalar.activation(sqf, wkf[:, 0:n * SEQ], ACT.Ln, bias=eps, scale=1.0 / HD))
                    nc.scalar.activation(sqf, sqf, ACT.Exp, scale=-0.5).then_inc(qk_rr, 1)
                act.wait_ge(f_sum, l + 1)
                link(nc.scalar.activation(fl[:, 1, :], fl[:, 0, :], ACT.Abs))
                link(nc.scalar.activation(fl[:, 1, :], fl[:, 1, :], ACT.Exp, scale=-1.0))
                nc.scalar.activation(fl[:, 1, :], fl[:, 1, :], ACT.Ln, bias=1.0).then_inc(f_log, 1)
                for br in range(2):
                    act.wait_ge(negmax, 2 * l + br + 1)
                    for h in range(HEADS):
                        for b, (c0, c1) in enumerate(((0, 128), (128, 384))):
                            e = nc.scalar.activation(prob[:, h, c0:c1], prob[:, h, c0:c1], ACT.Exp,
                                                     bias=negm[:, b * 8 + h:b * 8 + h + 1],
                                                     accum_out=den[:, b * 8 + h:b * 8 + h + 1])
                        e.then_inc(prob_ready, 1)
                    if br == 0:
                        nc.scalar.activation(sinkd, sinkd, ACT.Exp).then_inc(sinkd_exp, 1)
                def stick_tail(h):
                    act.wait_ge(stick_arg, 8 * l + h + 1)
                    nc.scalar.activation(stick[:, h % 2, 2, :], stick[:, h % 2, 2, :], ACT.Exp)\
                        .then_inc(stick_exp, 1)

                act.wait_ge(ptr_ready, 16 * l + 16)
                for h in range(HEADS):
                    act.wait_ge(z_ready, 8 * l + h + 1)
                    if h >= 2:
                        act.wait_ge(stick_ready, 8 * l + h - 1)
                    link(nc.scalar.activation(stick[:, h % 2, 0, :], wk[:, 2 + h % 2, 0:384], ACT.Abs))
                    link(nc.scalar.activation(stick[:, h % 2, 0, :], stick[:, h % 2, 0, :], ACT.Exp, scale=-1.0))
                    nc.scalar.activation(stick[:, h % 2, 0, :], stick[:, h % 2, 0, :], ACT.Ln, bias=1.0)\
                        .then_inc(z_log, 1)
                    if h:
                        stick_tail(h - 1)
                stick_tail(HEADS - 1)
                for n in range(6):
                    br, b = n // 2, n % 2
                    act.wait_ge(ytr, 6 * l + n + 1)
                    nc.scalar.activation(mov_hi[:, 4 * br:4 * br + 4, b * P:(b + 1) * P],
                                         wk[:, n, :].rearrange("p (c t) -> p c t", c=4), ACT.Copy)\
                        .then_inc(y_hi, 1)
                with act.Fori(0, N_BR // 4) as i:
                    for j in range(4):
                        head(L0 + i * 4 + (T_BR + 2 + j), j + 2)
                act.wait_ge(h_ready, 3 * l + 2)
                nc.scalar.activation(mov_hi[:, 0:KC, :], merged, ACT.Copy).then_inc(h_hi, 1)
                with act.Fori(0, N_OUT // 4) as i:
                    for j in range(4):
                        head(L0 + i * 4 + (T_OUT + 2 + j), j + 2)
                norm(1, sq2)
                with act.Fori(0, N_QUERY // 4) as i:
                    for j in range(4):
                        t = L0 + i * 4 + (T_QUERY + j)
                        head(t + 2, j + 2)
                        act.wait_ge(tile_done, t + 3)
                        nc.scalar.activation(queryT[:, bass.ds(i * 4 + j, 1), :].squeeze(1), pj[j % 2][:, 0:SEQ],
                                             ACT.Copy).then_inc(out_free, 1)
                act.wait_ge(out_free, l * OUTS + (O_PEER + 2))
                nc.scalar.activation(sq2, queryT, ACT.Square).then_inc(q_sq, 1)
                act.wait_ge(q_ss, l + 1)
                sqf = sq2.rearrange("p k s -> p (k s)")
                link(nc.scalar.activation(sqf, wkf[:, 0:2048], ACT.Ln, bias=eps, scale=1.0 / P))
                nc.scalar.activation(sqf, sqf, ACT.Exp, scale=-0.5).then_inc(q_rr, 1)
                for u in range(0, 16, 2):
                    act.wait_ge(s_ready, 16 * l + u + 2)
                    nc.scalar.activation(score[:, u:u + 2, :],
                                         wk[:, (u // 2) % 6, :].rearrange("p (u c) -> p u c", u=2), ACT.Copy)\
                        .then_inc(s_copied, 1)

                nc.scalar.preload_act_table(ACT.Gelu_apprx_tanh)
                with act.Fori(0, EARLY // 4) as i:
                    for j in range(4):
                        t = L0 + i * 4 + (T_PEER + j)
                        head(t + 2, j + 2)
                        act.wait_ge(tile_done, t + 3)
                        nc.scalar.activation(arena[:, bass.ds(i * 4 + j, 1), :].squeeze(1), pj[j % 2][:, 0:SEQ],
                                             ACT.Gelu_apprx_tanh).then_inc(out_free, 1)
                act.wait_ge(g_arg, l + 1)
                nc.scalar.activation(top_s, top_s, ACT.Exp).then_inc(g_exp, 1)
                nc.scalar.preload_act_table(ACT.Gelu_apprx_tanh)
                act.wait_ge(route_in, 6 * l + 6)

                def one_hot(pair):
                    act.wait_ge(hot_used, l * SEQ + pair * 8 + 4)
                    for r in range(4):
                        e = nc.scalar.activation(onehot_b[:, r, :], iota, ACT.Abs,
                                                 bias=idx2T[:, bass.ds(pair * 8 + r, 1)], scale=-1.0)
                    e.then_inc(hot_dist, 1)
                    act.wait_ge(hot_dist, l * (SEQ // 8) + pair + 1)
                    nc.scalar.activation(onehot_b[:, 0:4, :], onehot_b[:, 0:4, :].bitcast(f32),
                                         ACT.Relu, bias=1.0, scale=-1.0).then_inc(hot_b, 1)

                def copy_g(group, j):
                    act.wait_ge(g_times, l * (SEQ // 4) + group + 1)
                    nc.scalar.activation(
                        arena[:, EARLY:NKEYS, bass.ds(group * 4, 4)].rearrange("p i t -> p t i"),
                        wk[:, j, :].rearrange("p (t i) -> p t i", t=4)[:, :, EARLY:NKEYS],
                        ACT.Copy).then_inc(g_free, 1)

                one_hot(l * 0)
                with act.Fori(0, SEQ // 16 - 1) as i:
                    for q in range(4):
                        copy_g(i * 4 + q, q)
                        if q % 2 == 0:
                            one_hot(i * 2 + (q // 2 + 1))
                for q in range(4):
                    copy_g(l * 0 + (SEQ // 4 - 4 + q), q)
                    if q == 0:
                        one_hot(l * 0 + (SEQ // 8 - 1))

                def w_heads(n, s):
                    nc.scalar.activation(w_hi[:, s, :], group_of(n), ACT.Copy).then_inc(w_head, 1)

                act.wait_ge(g_free, l * (SEQ // 4) + (SEQ // 4 + 4))
                for n in range(3):
                    w_heads(n, n)
                with act.Fori(0, BOTH // 4) as i:
                    for j in range(4):
                        t = L0 + i * 8 + (T_BOTH + 2 * j)
                        head(t + 2, 2 * j + 2)
                        act.wait_ge(tile_done, t + 3)
                        nc.scalar.activation(act_g[:, j % 2, :], pj[j % 2][:, 0:SEQ], ACT.Gelu_apprx_tanh)\
                            .then_inc(out_free, 1)
                        w_heads(i * 4 + (j + 3), (j + 3) % 4)
                        head(t + 3, 2 * j + 3)
                act.wait_ge(w_made, (l + 1) * BOTH)
                with act.Fori(0, EARLY // 4 - 1) as i:
                    for j in range(4):
                        t = L0 + i * 4 + (T_DOWN + j)
                        head(t + 2, j + 2)
                        act.wait_ge(tile_done, t + 3)
                        w_heads(i * 4 + (BOTH + j + 3), (j + 3) % 4)
                t = L0 + TILES - 4
                head(t + 2, 2)
                act.wait_ge(tile_done, t + 3)
                w_heads(NKEYS - 1, 3)
                head(t + 3, 3)

        @block.vector
        def _(dve):
            setup = [0]

            def slink(ins):
                ins.then_inc(setup_step, 1)
                setup[0] += 1
                dve.wait_ge(setup_step, setup[0])

            def rest_of(t, j):
                dve.wait_ge(hi_done, t + 1)
                nc.vector.tensor_tensor(lo[j % SPLIT][:, :], raw[j % RAW][:, :], hi[j % SPLIT][:, :].bitcast(f32),
                                        ALU.subtract).then_inc(lo_done, 1)

            dve.wait_ge(setup_loaded, 64)
            dve.wait_ge(c_exp, 1)
            slink(nc.vector.tensor_scalar(c_tmp[:, :], c_tmp[:, :], 1.0, None, ALU.add))
            slink(nc.vector.reciprocal(c_tmp[:, :], c_tmp[:, :]))
            slink(nc.vector.tensor_tensor(c_tmp[:, :], c_tmp[:, :], c_in[:, :], ALU.mult))
            slink(nc.vector.tensor_copy(c_hi[:, :], c_tmp[:, :]))
            nc.vector.tensor_tensor(c_lo[:, :], c_tmp[:, :], c_hi[:, :].bitcast(f32), ALU.subtract).then_inc(c_ready, 1)
            dve.sem_inc(x_ready, 1)
            dve.sem_inc(arena_free, 1)

            with dve.Fori(0, DEPTH) as l:
                dve.sem_clear(dve_step)
                n_link = [0]
                L0 = l * TILES

                def link(ins):
                    ins.then_inc(dve_step, 1)
                    n_link[0] += 1
                    dve.wait_ge(dve_step, n_link[0])

                def norm(n, sq):
                    dve.wait_ge(rstd_ready, 2 * l + n + 1)
                    link(nc.vector.tensor_tensor(sq, x[:, :, :], rstd.unsqueeze(1).to_broadcast([P, KC, SEQ]),
                                                 ALU.mult))
                    for k in range(KC):
                        last = nc.vector.tensor_scalar(sq[:, k, :], sq[:, k, :], amp[:, n, k:k + 1],
                                                       mod[:, 24 * n + k:24 * n + k + 1], ALU.mult, ALU.add)
                    last.then_inc(h_ready, 1)
                    dve.wait_ge(h_ready, 3 * l + (1 if n == 0 else 3))
                    dve.wait_ge(h_hi, 3 * l + (1 if n == 0 else 3))
                    nc.vector.tensor_tensor(mov_lo[:, 0:KC, :], sq, mov_hi[:, 0:KC, :].bitcast(f32),
                                            ALU.subtract).then_inc(mov_ready, 1)

                link(nc.vector.tensor_copy(par[:, :], par_all[:, bass.ds(l, 1), :].squeeze(1)))
                def modulation(q, t):
                    dve.wait_ge(tile_done, t + 3)
                    own = gated[:, 0, :].rearrange("p (a b) -> p a b", a=4)
                    nc.vector.tensor_tensor(own, wk[:, 1, :].rearrange("p (a b) -> p a b", a=4),
                                            ident.unsqueeze(1).to_broadcast([P, 4, P]), ALU.mult).then_inc(mod_read, 1)
                    dve.wait_ge(mod_read, l * (N_ADA // 4) + q + 2)
                    nc.vector.tensor_reduce(mod[:, bass.ds(q * 4, 4)], own, AX.X, ALU.add).then_inc(mod_sum, 1)
                    dve.wait_ge(mod_sum, l * (N_ADA // 4) + q + 1)

                rest_of(L0, 0)
                rest_of(L0 + 1, 1)
                with dve.Fori(0, ADA_FIRST // 4) as i:
                    for j in range(4):
                        rest_of(L0 + i * 4 + (j + 2), j + 2)
                    modulation(i, L0 + i * 4 + 3)
                link(nc.vector.tensor_tensor(mod[:, 0:ADA_FIRST], mod[:, 0:ADA_FIRST], par[:, 0:ADA_FIRST], ALU.add))
                nc.vector.scalar_tensor_tensor(amp[:, 0, :], mod[:, KC:2 * KC], 1.0, par[:, PG1:PG1 + KC],
                                               ALU.add, ALU.mult)
                for n, g in ((0, PQA), (1, PQB)):
                    link(nc.vector.tensor_scalar(gain[:, n:n + 1], par[:, g:g + 1], HD ** -0.5, None, ALU.mult))
                norm(0, sq)
                with dve.Fori(0, N_QKV // 4) as i:
                    for j in range(8):
                        rest_of(L0 + i * 8 + (T_QKV + 2 + j), j + 2)
                    modulation(i + ADA_FIRST // 4, L0 + i * 8 + (T_QKV + 7))
                with dve.Fori(0, N_GATE // 4) as i:
                    for j in range(4):
                        rest_of(L0 + i * 4 + (T_GATE + 2 + j), j + 2)
                link(nc.vector.tensor_tensor(mod[:, ADA_FIRST:N_ADA], mod[:, ADA_FIRST:N_ADA],
                                             par[:, ADA_FIRST:N_ADA], ALU.add))
                nc.vector.scalar_tensor_tensor(amp[:, 1, :], mod[:, 4 * KC:5 * KC], 1.0, par[:, PG2:PG2 + KC],
                                               ALU.add, ALU.mult)
                dve.wait_ge(out_free, l * OUTS + (O_BR + 2))
                nc.vector.tensor_scalar(projT[:, QC:QC + 4, :], projT[:, QC:QC + 4, :], HD ** -0.5, None, ALU.mult)
                for g, (q0, k0, nk, gk) in enumerate(((QA, KA, 1, PKA), (QB, KB, 4, PKB))):
                    dve.wait_ge(qk_rr, 2 * l + g + 1)
                    nc.vector.scalar_tensor_tensor(projT[:, q0:q0 + 4, :], projT[:, q0:q0 + 4, :], gain[:, g:g + 1],
                                                   sq[:, 0:4, :], ALU.mult, ALU.mult)
                    nc.vector.scalar_tensor_tensor(projT[:, k0:k0 + nk, :], projT[:, k0:k0 + nk, :],
                                                   par[:, gk:gk + 1], sq[:, 4:4 + nk, :], ALU.mult,
                                                   ALU.mult).then_inc(qk_done, 1)
                dve.wait_ge(qk_done, 2 * l + 2)
                nc.vector.tensor_scalar(fl[:, 0, :], projT[0:HEADS, FG, :], par[0:HEADS, PBF:PBF + 1], None,
                                        ALU.add).then_inc(f_sum, 1)
                dve.wait_ge(f_log, l + 1)
                link(nc.vector.scalar_tensor_tensor(fl[:, 0, :], fl[:, 0, :], 0.0, fl[:, 1, :], ALU.min,
                                                    ALU.subtract))
                link(nc.vector.tensor_tensor_scan(fl[:, 2, :], const[0:HEADS, C_ONE:C_ONE + 1].to_broadcast([HEADS, SEQ]),
                                                  fl[:, 0, :], 0.0, ALU.mult, ALU.add))
                nc.vector.tensor_scalar(fl[:, 3, :], fl[:, 2, :], -1.0, None, ALU.mult).then_inc(f_ready, 1)
                dve.wait_ge(tables, 16 * l + 16)
                for br in range(2):
                    if br:
                        dve.wait_ge(ptr_ready, 16 * l + 8)
                    for h in range(HEADS):
                        wait_alone(dve, score_ready, 16 * l + 8 * br + h + 1)
                        for b, (c0, c1) in enumerate(((0, 128), (128, 384))):
                            tab = taba[:, h, c0:c1] if br == 0 else btab[:, c0:c1]
                            e = nc.vector.tensor_tensor_reduce(
                                out=prob[:, h, c0:c1], in0=wk[:, 2 + h % 4, c0:c1], in1=tab, scale=1.0,
                                scalar=-3e38, op0=ALU.add, op1=ALU.max, accum_out=mx[:, b * 8 + h:b * 8 + h + 1])
                        e.then_inc(score_read, 1)
                    dve.wait_ge(score_read, 16 * l + 8 * br + 8)
                    if br == 0:
                        sink = par[:, PSINK:PSINK + 8].unsqueeze(1).to_broadcast([P, 2, 8])
                        mx2, sk2 = mx.rearrange("p (b h) -> p b h", b=2), sinkd.rearrange("p (b h) -> p b h", b=2)
                        link(nc.vector.tensor_tensor(mx2, mx2, sink, ALU.max))
                        link(nc.vector.tensor_tensor(sk2, sink, mx2, ALU.subtract))
                    nc.vector.tensor_scalar(negm, mx, -1.0, None, ALU.mult).then_inc(negmax, 1)
                    for h in range(HEADS):
                        n = 8 * br + h
                        dve.wait_ge(ptr_ready, 16 * l + n + 1)
                        if n >= 2:
                            dve.wait_ge(pv_done, 24 * l + n - 1)
                        nc.vector.tensor_copy(probT[:, h % 2, :], wk[:, h % 2, 0:384]).then_inc(pt_copied, 1)
                    dve.wait_ge(prob_ready, 16 * l + 8 * br + 8)
                    if br == 0:
                        dve.wait_ge(sinkd_exp, l + 1)
                        link(nc.vector.tensor_tensor(den, den, sinkd, ALU.add))
                    link(nc.vector.reciprocal(rden, den))
                    dve.wait_ge(pv_done, 24 * l + 8 * br + 8)
                    for b in range(2):
                        e = nc.vector.tensor_tensor(
                            ytok[:, b, br, :].rearrange("p (h c) -> p h c", h=8),
                            pj[b][:, :].rearrange("p (h c) -> p h c", h=8),
                            rden[:, b * 8:b * 8 + 8].unsqueeze(2).to_broadcast([P, 8, HD]), ALU.mult)
                    e.then_inc(y_read, 1)
                def stick_tail(h):
                    s = h % 2
                    dve.wait_ge(tail_ready, 8 * l + h + 1)
                    nc.vector.tensor_tensor(stick[:, s, 2, :], stick[:, s, 2, :], wk[:, 4 + s, 0:384],
                                            ALU.subtract).then_inc(stick_arg, 1)
                    dve.wait_ge(stick_exp, 8 * l + h + 1)
                    if h >= 2:
                        dve.wait_ge(pv_done, 24 * l + 16 + h - 1)
                    nc.vector.tensor_tensor(stick[:, s, 3, :], stick[:, s, 2, :], cmask,
                                            ALU.mult).then_inc(stick_ready, 1)

                for h in range(HEADS):
                    s = h % 2
                    z = wk[:, 2 + s, 0:384]
                    dve.wait_ge(z_log, 8 * l + h + 1)
                    link(nc.vector.scalar_tensor_tensor(stick[:, s, 1, :], z, 0.0, stick[:, s, 0, :], ALU.max,
                                                        ALU.add))
                    nc.vector.tensor_tensor(stick[:, s, 1, :], stick[:, s, 1, :], cmask, ALU.mult)
                    nc.vector.scalar_tensor_tensor(stick[:, s, 2, :], z, 0.0, stick[:, s, 0, :], ALU.min,
                                                   ALU.subtract).then_inc(z_read, 1)
                    if h:
                        stick_tail(h - 1)
                    else:
                        dve.wait_ge(z_read, 8 * l + 1)
                stick_tail(HEADS - 1)
                dve.wait_ge(pv_done, 24 * l + 24)
                for b in range(2):
                    e = nc.vector.tensor_copy(ytok[:, b, 2, :], pj[b][:, :])
                e.then_inc(y_read, 1)
                link(nc.vector.memset(merged, 0.0))
                for n in range(6):
                    br, b = n // 2, n % 2
                    dve.wait_ge(y_hi, 6 * l + n + 1)
                    nc.vector.tensor_tensor(mov_lo[:, 4 * br:4 * br + 4, b * P:(b + 1) * P],
                                            wk[:, n, :].rearrange("p (c t) -> p c t", c=4),
                                            mov_hi[:, 4 * br:4 * br + 4, b * P:(b + 1) * P].bitcast(f32),
                                            ALU.subtract).then_inc(mov_ready, 1)
                with dve.Fori(0, 3) as br:
                    for j in range(4):
                        t = L0 + br * 4 + (T_BR + j)
                        rest_of(t + 2, j + 2)
                        dve.wait_ge(tile_done, t + 3)
                        n = l * N_BR + br * 4 + j
                        nc.vector.tensor_tensor(
                            gated[:, j % 2, :].rearrange("p (o s) -> p o s", o=2),
                            pj[j % 2][:, :].rearrange("p (o s) -> p o s", o=2),
                            projT[:, bass.ds(br * 8 + (N_QKV + 2 * j), 2), :], ALU.mult).then_inc(out_free, 1)
                        dve.wait_ge(out_free, l * OUTS + br * 4 + (O_BR + j + 3))
                        nc.vector.tensor_tensor(merged[:, 2 * j:2 * j + 2, :], merged[:, 2 * j:2 * j + 2, :],
                                                gated[:, j % 2, :].rearrange("p (o s) -> p o s", o=2),
                                                ALU.add).then_inc(br_add, 1)
                        dve.wait_ge(br_add, n + 1)
                dve.sem_inc(h_ready, 1)
                dve.wait_ge(h_hi, 3 * l + 2)
                link(nc.vector.tensor_tensor(mov_lo[:, 0:KC, :], merged, mov_hi[:, 0:KC, :].bitcast(f32),
                                             ALU.subtract))
                dve.sem_inc(mov_ready, 1)
                dve.sem_inc(keys_free, 1)
                with dve.Fori(0, N_OUT // 4) as i:
                    for j in range(4):
                        t = L0 + i * 4 + (T_OUT + j)
                        rest_of(t + 2, j + 2)
                        dve.wait_ge(tile_done, t + 3)
                        xk = x[:, bass.ds(i * 4 + j, 1), :].squeeze(1)
                        nc.vector.scalar_tensor_tensor(xk, pj[j % 2][:, 0:SEQ], mod[:, bass.ds(i * 4 + (16 + j), 1)],
                                                       xk, ALU.mult, ALU.add).then_inc(out_free, 1)
                dve.wait_ge(out_free, l * OUTS + (O_QUERY + 2))
                dve.sem_inc(x_ready, 1)
                norm(1, sq2)
                with dve.Fori(0, N_QUERY // 4) as i:
                    for j in range(4):
                        rest_of(L0 + i * 4 + (T_QUERY + 2 + j), j + 2)
                dve.wait_ge(q_rr, l + 1)
                nc.vector.scalar_tensor_tensor(queryT, queryT, par[:, PQP:PQP + 1], sq2, ALU.mult,
                                               ALU.mult).then_inc(q_norm, 1)
                early = [0]

                def split_early(n):
                    for _ in range(min(n, EARLY - early[0])):
                        j = early[0]
                        rest_of(L0 + (T_PEER + 2 + j), j + 2)
                        early[0] += 1

                for u in range(16):
                    if u % 2 == 0:
                        wait_alone(dve, s_copied, 8 * l + u // 2 + 1)
                    for n in range(2):
                        s = score[:, u, n * 128:(n + 1) * 128]
                        r = rest[:, n, 0:128]
                        link(nc.vector.max(sel_v[:, n, 0:8], s))
                        nc.vector.max_index(sel_i[:, u, n, 0:8], sel_v[:, n, 0:8], s)
                        link(nc.vector.match_replace(r, sel_v[:, n, 0:8], s, -3e38))
                        link(nc.vector.max(sel_v[:, n, 8:16], r))
                        nc.vector.max_index(sel_i[:, u, n, 8:16], sel_v[:, n, 8:16], r)
                        split_early(2 if n else 1)
                    c = cand
                    link(nc.vector.tensor_tensor(c.rearrange("p (a b) -> p a b", a=16),
                                                 sel_v[:, 0, :].unsqueeze(2).to_broadcast([P, 16, 16]),
                                                 sel_v[:, 1, :].unsqueeze(1).to_broadcast([P, 16, 16]), ALU.add))
                    link(nc.vector.max(top_s[:, u, 0:8], c))
                    nc.vector.max_index(top_p[:, u, 0:8], top_s[:, u, 0:8], c)
                    link(nc.vector.match_replace(candr, top_s[:, u, 0:8], c, -3e38))
                    link(nc.vector.max(top_s[:, u, 8:16], candr))
                    link(nc.vector.max_index(top_p[:, u, 8:16], top_s[:, u, 8:16], candr))
                    split_early(2 if u % 4 == 0 else 1)
                gs, gr = gsum[:, 0, :], gsum[:, 1, :]
                link(nc.vector.tensor_copy(gs, top_s[:, :, 0:1].squeeze(2)))
                nc.vector.tensor_tensor(top_s, top_s, gs.unsqueeze(2).to_broadcast([P, 16, 16]),
                                        ALU.subtract).then_inc(g_arg, 1)
                tp = top_p.rearrange("p u k -> p (u k)")
                nc.vector.tensor_scalar(pos_i[:, 0, :], tp, 4, None, ALU.logical_shift_right)
                link(nc.vector.tensor_scalar(pos_i[:, 1, :], tp, 15, None, ALU.bitwise_and))
                nc.vector.tensor_copy(sel_if, sel_i)
                link(nc.vector.tensor_copy(pos_f, pos_i))
                split_early(1)
                for n in range(2):
                    for b in range(2):
                        hot = pick.rearrange("p (c j) -> p c j", j=16)
                        pf = pos_f[:, n, b * 128:(b + 1) * 128]
                        split_early(5)
                        link(nc.vector.tensor_tensor(hot, pf.unsqueeze(2).to_broadcast([P, 128, 16]),
                                                     iota[:, 0:16].unsqueeze(1).to_broadcast([P, 128, 16]),
                                                     ALU.is_equal))
                        hot4 = pick.rearrange("p (u k j) -> p u k j", u=8, k=16)
                        link(nc.vector.tensor_tensor(
                            hot4, hot4, sel_if[:, b * 8:b * 8 + 8, n, :].unsqueeze(2).to_broadcast([P, 8, 16, 16]),
                            ALU.mult))
                        link(nc.vector.tensor_reduce(idx_tok[:, n, b * 128:(b + 1) * 128], hot, AX.X, ALU.add))
                split_early(EARLY)
                dve.wait_ge(g_exp, l + 1)
                link(nc.vector.tensor_reduce(gs, top_s, AX.X, ALU.add))
                link(nc.vector.reciprocal(gr, gs))
                nc.vector.tensor_tensor(top_s, top_s, gr.unsqueeze(2).to_broadcast([P, 16, 16]),
                                        ALU.mult).then_inc(route_ready, 1)
                for n, dst in enumerate((idx1T, idx2T, gateT)):
                    for b in range(2):
                        dve.wait_ge(route_tr, 6 * l + 2 * n + b + 1)
                        nc.vector.tensor_copy(dst[:, b * P:(b + 1) * P], wk[:, 2 * n + b, 0:P]).then_inc(route_in, 1)
                wait_alone(dve, route_in, 6 * l + 6)

                def one_hot(group, j):
                    dve.wait_ge(hot_used, l * SEQ + group * 4 + 4)
                    if j:
                        nc.vector.tensor_tensor(
                            onehot_b[:, 4:8, :], iota.unsqueeze(1).to_broadcast([P, 4, NKEYS]),
                            idx2T[:, bass.ds(group * 4, 4)].unsqueeze(2).to_broadcast([P, 4, NKEYS]),
                            ALU.is_equal)
                    for r in range(4):
                        nc.vector.tensor_scalar(onehot_a[:, 4 * j + r, :], iota, idx1T[:, bass.ds(group * 4 + r, 1)],
                                                gateT[:, bass.ds(group * 4 + r, 1)], ALU.is_equal,
                                                ALU.mult).then_inc(hot_a, 1)

                def times_g(group, j):
                    dve.wait_ge(hot_used, l * SEQ + group * 4 + 12)
                    a = arena[:, 0:EARLY, bass.ds(group * 4, 4)].rearrange("p i t -> p t i")
                    nc.vector.tensor_tensor(a, wk[:, j, :].rearrange("p (t i) -> p t i", t=4)[:, :, 0:EARLY], a,
                                            ALU.mult).then_inc(g_times, 1)

                dve.wait_ge(out_free, l * OUTS + (O_PEER + EARLY + 2))
                one_hot(l * 0, 0)
                with dve.Fori(0, SEQ // 16 - 1) as i:
                    for q in range(4):
                        one_hot(i * 4 + (q + 1), (q + 1) % 2)
                        times_g(i * 4 + q, q)
                for q in range(4):
                    if q < 3:
                        one_hot(l * 0 + (SEQ // 4 - 3 + q), (q + 1) % 2)
                    times_g(l * 0 + (SEQ // 4 - 4 + q), q)

                def w_rests(n, s, done):
                    dve.wait_ge(w_head, l * NKEYS + done)
                    nc.vector.tensor_tensor(w_lo[:, s, :], group_of(n), w_hi[:, s, :].bitcast(f32),
                                            ALU.subtract).then_inc(w_rest, 1)

                dve.wait_ge(g_free, l * (SEQ // 4) + (SEQ // 4 + 4))
                for n in range(3):
                    w_rests(n, n, n + 1)
                with dve.Fori(0, BOTH // 4) as i:
                    for j in range(4):
                        t = L0 + i * 8 + (T_BOTH + 2 * j)
                        rest_of(t + 2, 2 * j + 2)
                        dve.wait_ge(out_free, l * OUTS + i * 4 + (O_PEER + EARLY + j + 3))
                        g = group_of(i * 4 + (EARLY + j))
                        nc.vector.tensor_tensor(g, act_g[:, j % 2, :], g, ALU.mult).then_inc(w_made, 1)
                        w_rests(i * 4 + (j + 3), (j + 3) % 4, i * 4 + (j + 4))
                        rest_of(t + 3, 2 * j + 3)
                wait_alone(dve, w_made, (l + 1) * BOTH)
                with dve.Fori(0, EARLY // 4 - 1) as i:
                    for j in range(4):
                        t = L0 + i * 4 + (T_DOWN + j)
                        rest_of(t + 2, j + 2)
                        w_rests(i * 4 + (BOTH + j + 3), (j + 3) % 4, i * 4 + (BOTH + j + 4))
                t = L0 + TILES - 4
                rest_of(t + 2, 2)
                w_rests(NKEYS - 1, 3, NKEYS)
                rest_of(t + 3, 3)
                dve.wait_ge(tile_done, L0 + TILES + 2)
                nc.vector.tensor_copy(ftok, wk[:, 2:6, :].rearrange("p (b e) c -> p b (e c)", b=2)).then_inc(f_tok, 1)
                for k in range(KC):
                    if k % 2 == 0:
                        dve.wait_ge(f_tr, 4 * l + k // 2 + 1)
                    e = nc.vector.scalar_tensor_tensor(
                        x[:, k, :], wk[:, 2 + k // 2, (k % 2) * SEQ:(k % 2 + 1) * SEQ], mod[:, 40 + k:41 + k],
                        x[:, k, :], ALU.mult, ALU.add)
                e.then_inc(x_ready, 1)
                dve.wait_ge(x_ready, 2 * l + 3)
                dve.sem_inc(arena_free, 1)

        @block.tensor
        def _(pe):
            def product(out, w_h, w_l, m_h, m_l, first, last):
                pe.matmul(out, w_h, m_h, start=first, stop=False)
                pe.matmul(out, w_h, m_l, start=False, stop=False)
                return pe.matmul(out, w_l, m_h, start=False, stop=last)

            def chunk(j, k):
                return hi[j % SPLIT][:, k * P:(k + 1) * P], lo[j % SPLIT][:, k * P:(k + 1) * P]

            pe.sem_inc(tile_done, 2)
            pe.sem_inc(out_free, 2)
            pe.sem_inc(hot_used, 8)
            pe.sem_inc(g_free, 4)
            pe.sem_inc(mod_read, 1)
            pe.wait_ge(c_ready, 1)
            with pe.Fori(0, DEPTH) as l:
                L0 = l * TILES

                def norm(n, sq):
                    pe.wait_ge(sq_ready, 2 * l + n + 1)
                    for k in range(KC):
                        last = pe.matmul(wk[:, 0, 0:SEQ], ones, sq[:, k, :], start=k == 0, stop=k == KC - 1)
                    last.then_inc(ss_ready, 1)

                def project(t, j, o, bank):
                    pe.wait_ge(lo_done, t + 1)
                    pe.wait_ge(out_free, l * OUTS + o + 1)
                    for k in range(KC):
                        last = product(pj[bank][:, 0:SEQ], *chunk(j, k), mov_hi[:, k, :], mov_lo[:, k, :],
                                       k == 0, k == KC - 1)
                    return last

                def modulation(t, j, q, r):
                    pe.wait_ge(lo_done, t + 1)
                    if r == 0:
                        pe.wait_ge(mod_read, l * (N_ADA // 4) + q + 1)
                    for k in range(2):
                        c = 2 * r + k
                        ch, cl = c_hi[:, c:c + 1].to_broadcast([P, P]), c_lo[:, c:c + 1].to_broadcast([P, P])
                        w = slice(k * 512, (k + 1) * 512)
                        last = product(wk[:, 1, :], ch, cl, hi[j % SPLIT][:, w], lo[j % SPLIT][:, w], c == 0,
                                       c == KC - 1)
                    last.then_inc(tile_done, 1)

                with pe.Fori(0, ADA_FIRST // 4) as i:
                    for j in range(4):
                        modulation(L0 + i * 4 + j, j, i, j)
                norm(0, sq)
                wait_alone(pe, mov_ready, 9 * l + 1)
                with pe.Fori(0, N_QKV // 4) as i:
                    for j in range(4):
                        t = L0 + i * 8 + (T_QKV + 2 * j)
                        project(t, 2 * j, i * 4 + j, j % 2).then_inc(tile_done, 1)
                        modulation(t + 1, 2 * j + 1, i + ADA_FIRST // 4, j)
                with pe.Fori(0, N_GATE // 4) as i:
                    for j in range(4):
                        project(L0 + i * 4 + (T_GATE + j), j, i * 4 + (O_GATE + j), j % 2).then_inc(tile_done, 1)
                pe.wait_ge(out_free, l * OUTS + (O_BR + 2))
                for b in range(2):
                    for n, t in enumerate(V_TILES):
                        c = b * 1536 + n * P
                        last = pe.transpose(wkf[:, c:c + P], projT[:, t, b * P:(b + 1) * P], ident)
                    last.then_inc(vtr, 1)
                for g, (t0, n) in enumerate(((QA, 5), (QB, 8))):
                    pe.wait_ge(qk_sq, 2 * l + g + 1)
                    if g == 0:
                        pe.wait_ge(vtok_in, 2 * l + 2)
                    else:
                        pe.wait_ge(qk_rr, 2 * l + 1)
                    for k in range(n):
                        last = pe.matmul(wkf[:, k * SEQ:(k + 1) * SEQ], blk, sq[:, k, :], start=True, stop=True)
                    last.then_inc(qk_ss, 1)
                pe.wait_ge(qk_done, 2 * l + 2)
                for br in range(2):
                    if br:
                        pe.wait_ge(f_ready, l + 1)

                    def scores(h):
                        n = 8 * br + h
                        if n >= 4:
                            pe.wait_ge(score_read, 16 * l + n - 3)
                        if br == 0:
                            o = (h // 4) * HD
                            q, k = projT[o:o + HD, QA + h % 4, :], projT[o:o + HD, KA, :]
                        else:
                            o = (h % 2) * HD
                            q, k = projT[o:o + HD, QB + h // 2, :], projT[o:o + HD, KB + h // 2, :]
                        s = wk[:, 2 + h % 4, :]
                        hot = ident[0:HEADS, h:h + 1].to_broadcast([HEADS, P])
                        for q0, nk, c0 in ((0, P, 0), (P, 2 * P, P)):
                            last = pe.matmul(s[:, c0:c0 + nk], q[:, q0:q0 + P], k[:, 0:nk], start=True, stop=br == 0)
                            if br:
                                last = pe.matmul(s[:, c0:c0 + nk], hot, fl[:, 3, 0:nk], start=False, stop=True)
                        last.then_inc(score_ready, 1)

                    def turn(h):
                        n = 8 * br + h
                        pe.wait_ge(prob_ready, 16 * l + n + 1)
                        if n >= 2:
                            pe.wait_ge(pt_copied, 16 * l + n - 1)
                        for c in range(3):
                            last = pe.transpose(wk[:, h % 2, c * P:(c + 1) * P], prob[:, h, c * P:(c + 1) * P], ident)
                        last.then_inc(ptr_ready, 1)

                    def values(h):
                        n = 8 * br + h
                        pe.wait_ge(pt_copied, 16 * l + n + 1)
                        if h == 0 and br:
                            pe.wait_ge(y_read, 3 * l + 1)
                        v = (h // 4) * HD if br == 0 else P + h * HD
                        o = slice(h * HD, (h + 1) * HD)
                        pt = probT[:, h % 2, :]
                        pe.matmul(pj[0][:, o], pt[:, 0:P], vtok[:, 0, v:v + HD], start=True, stop=True)
                        pe.matmul(pj[1][:, o], pt[:, P:2 * P], vtok[:, 0, v:v + HD], start=True, stop=False)
                        pe.matmul(pj[1][:, o], pt[:, 2 * P:3 * P], vtok[:, 1, v:v + HD], start=False,
                                  stop=True).then_inc(pv_done, 1)

                    for h in range(HEADS):
                        scores(h)
                    turn(0)
                    for h in range(HEADS):
                        if h + 1 < HEADS:
                            turn(h + 1)
                        values(h)
                def logits(h):
                    if h >= 2:
                        pe.wait_ge(z_read, 8 * l + h - 1)
                    else:
                        pe.wait_ge(score_read, 16 * l + 16)
                    o = (h % 2) * HD
                    q, k = projT[o:o + HD, QC + h // 2, :], projT[o:o + HD, KCT + h // 2, :]
                    z = wk[:, 2 + h % 2, :]
                    pe.matmul(z[:, 0:SEQ], k[:, 0:P], q, start=True, stop=True)
                    pe.matmul(z[:, SEQ:SEQ + P], k[:, P:2 * P], q[:, P:2 * P], start=True,
                              stop=True).then_inc(z_ready, 1)

                def tails(h):
                    pe.wait_ge(z_read, 8 * l + h + 1)
                    if h >= 2:
                        pe.wait_ge(stick_arg, 8 * l + h - 1)
                    t = wk[:, 4 + h % 2, :]
                    sp_ = stick[:, h % 2, 1, :]
                    pe.matmul(t[:, 0:P], tri, sp_[:, 0:P], start=True, stop=True)
                    pe.matmul(t[:, P:2 * P], tri, sp_[:, P:2 * P], start=True, stop=False)
                    pe.matmul(t[:, P:2 * P], ones, sp_[:, 2 * P:3 * P], start=False, stop=True)
                    pe.matmul(t[:, 2 * P:3 * P], tri, sp_[:, 2 * P:3 * P], start=True,
                              stop=True).then_inc(tail_ready, 1)

                def stick_values(h):
                    pe.wait_ge(stick_ready, 8 * l + h + 1)
                    if h == 0:
                        pe.wait_ge(y_read, 3 * l + 2)
                    v = P + 512 + h * HD
                    o = slice(h * HD, (h + 1) * HD)
                    a = stick[:, h % 2, 3, :]
                    pe.matmul(pj[0][:, o], a[:, 0:P], vtok[:, 0, v:v + HD], start=True, stop=True)
                    pe.matmul(pj[1][:, o], a[:, P:2 * P], vtok[:, 0, v:v + HD], start=True, stop=False)
                    pe.matmul(pj[1][:, o], a[:, 2 * P:3 * P], vtok[:, 1, v:v + HD], start=False,
                              stop=True).then_inc(pv_done, 1)

                logits(0)
                for h in range(HEADS):
                    if h + 1 < HEADS:
                        logits(h + 1)
                    tails(h)
                    if h:
                        stick_values(h - 1)
                stick_values(HEADS - 1)
                pe.wait_ge(y_read, 3 * l + 3)
                for n in range(6):
                    br, b = n // 2, n % 2
                    for c in range(4):
                        last = pe.transpose(wk[:, n, c * P:(c + 1) * P], ytok[:, b, br, c * P:(c + 1) * P], ident)
                    last.then_inc(ytr, 1)
                wait_alone(pe, mov_ready, 9 * l + 7)
                for n in range(N_BR):
                    br, j = n // 4, n % 4
                    pe.wait_ge(lo_done, L0 + (T_BR + n + 1))
                    pe.wait_ge(out_free, l * OUTS + (O_BR + n + 1))
                    for o in range(2):
                        for k in range(4):
                            last = product(pj[j % 2][:, o * SEQ:(o + 1) * SEQ], *chunk(j, 4 * o + k),
                                           mov_hi[:, br * 4 + k, :], mov_lo[:, br * 4 + k, :], k == 0, k == 3)
                    last.then_inc(tile_done, 1)
                wait_alone(pe, mov_ready, 9 * l + 8)
                with pe.Fori(0, N_OUT // 4) as i:
                    for j in range(4):
                        project(L0 + i * 4 + (T_OUT + j), j, i * 4 + (O_OUT + j), j % 2).then_inc(tile_done, 1)
                norm(1, sq2)
                wait_alone(pe, mov_ready, 9 * l + 9)
                with pe.Fori(0, N_QUERY // 4) as i:
                    for j in range(4):
                        project(L0 + i * 4 + (T_QUERY + j), j, i * 4 + (O_QUERY + j), j % 2).then_inc(tile_done, 1)
                pe.wait_ge(q_sq, l + 1)
                pe.wait_ge(rstd_ready, 2 * l + 2)
                for k in range(KC):
                    last = pe.matmul(wkf[:, k * SEQ:(k + 1) * SEQ], ones, sq2[:, k, :], start=True, stop=True)
                last.then_inc(q_ss, 1)
                pe.wait_ge(q_norm, l + 1)
                pe.wait_ge(keys_in, 16 * l + 16)
                for u in range(16):
                    b, h = u // 8, u % 8
                    if u >= 12 and u % 2 == 0:
                        pe.wait_ge(s_copied, 8 * l + u // 2 - 5)
                    pe.matmul(wk[:, (u // 2) % 6, (u % 2) * 256:(u % 2 + 1) * 256], queryT[:, h, b * P:(b + 1) * P],
                              skeys[:, h, :], start=True, stop=True).then_inc(s_ready, 1)
                with pe.Fori(0, EARLY // 4) as i:
                    for j in range(4):
                        project(L0 + i * 4 + (T_PEER + j), j, i * 4 + (O_PEER + j), j % 2).then_inc(tile_done, 1)
                pe.wait_ge(route_ready, l + 1)
                pe.wait_ge(s_copied, 8 * l + 8)
                tsf = top_s.rearrange("p u k -> p (u k)")
                for n, src in enumerate((idx_tok[:, 0, :], idx_tok[:, 1, :], tsf)):
                    for b in range(2):
                        pe.transpose(wk[:, 2 * n + b, 0:P], src[:, b * P:(b + 1) * P], ident).then_inc(route_tr, 1)
                wait_alone(pe, route_in, 6 * l + 6)
                with pe.Fori(0, SEQ // 16) as i:
                    for r in range(16):
                        pe.wait_ge(hot_a, l * SEQ + i * 16 + (r + 1))
                        if r % 8 == 0:
                            pe.wait_ge(hot_b, l * (SEQ // 8) + i * 2 + (r // 8 + 1))
                        if r % 4 == 0:
                            pe.wait_ge(g_free, l * (SEQ // 4) + i * 4 + (r // 4 + 1))
                        pe.matmul(wk[:, r // 4, (r % 4) * P:(r % 4 + 1) * P], onehot_a[:, r % 8, :],
                                  onehot_b[:, r % 8, :].bitcast(f32), start=True, stop=True).then_inc(hot_used, 1)

                def down(t, j, n, s, last_group=False):
                    pe.wait_ge(lo_done, t + 1)
                    pe.wait_ge(w_rest, l * NKEYS + n + 1)
                    vh, vl = hi[j % SPLIT], lo[j % SPLIT]
                    for b in range(2):
                        wh, wl = w_hi[:, s, b * P:(b + 1) * P], w_lo[:, s, b * P:(b + 1) * P]
                        for e in range(2):
                            last = product(wk[:, 2 + 2 * b + e, :], wh, wl, vh[:, e * 512:(e + 1) * 512],
                                           vl[:, e * 512:(e + 1) * 512], False, last_group)
                    last.then_inc(tile_done, 1)

                pe.wait_ge(g_free, l * (SEQ // 4) + (SEQ // 4 + 4))
                for c in range(4):
                    pe.matmul(wk[:, 2 + c, :], zero, const[:, 0:512], start=True, stop=False)
                with pe.Fori(0, BOTH // 4) as i:
                    for j in range(4):
                        t = L0 + i * 8 + (T_BOTH + 2 * j)
                        project(t, 2 * j, i * 4 + (O_PEER + EARLY + j), j % 2).then_inc(tile_done, 1)
                        down(t + 1, 2 * j + 1, i * 4 + j, j)
                with pe.Fori(0, EARLY // 4 - 1) as i:
                    for j in range(4):
                        down(L0 + i * 4 + (T_DOWN + j), j, i * 4 + (BOTH + j), j)
                for j in range(4):
                    down(L0 + (TILES - 4 + j), j, NKEYS - 4 + j, j, j == 3)
                pe.wait_ge(f_tok, l + 1)
                for k in range(KC):
                    for b in range(2):
                        c = (k % 2) * SEQ + b * P
                        last = pe.transpose(wk[:, 2 + k // 2, c:c + P], ftok[:, b, k * P:(k + 1) * P], ident)
                    if k % 2:
                        last.then_inc(f_tr, 1)


def _rows(w):
    k, n = w.shape[0] // P, w.shape[1] // P
    return w.reshape(k, P, n, P).transpose(2, 1, 0, 3).reshape(n, P, k * P)


def _lay_out(np, i):
    qh = [h for t in range(4) for h in (t, t + 4)]
    tiles = []
    for l in range(DEPTH):
        w = i["w_in"][l]
        cut = np.split(w, [512, 640, 768, 1280, 1792, 2304, 2312, 2824, 3336, 3848], axis=1)
        qa, ka, va, qb, kb, vb, fb, qc, kc, vc, gates = cut
        qa = qa.reshape(D, 8, HD)[:, qh].reshape(D, 512)
        fb = np.concatenate([fb, np.zeros((D, P - 8), fb.dtype)], 1)
        blank = np.zeros((D, P), w.dtype)
        ada = i["w_ada"][l].reshape(4, 2, P, 12, 512).transpose(3, 0, 2, 1, 4).reshape(N_ADA, P, 1024)
        tiles.append(ada[:ADA_FIRST])
        both = np.empty((2 * N_QKV, P, 1024), w.dtype)
        both[0::2] = _rows(np.concatenate([qa, ka, va, qb, kb, vb, fb, qc, kc, vc, blank], 1))
        both[1::2] = ada[ADA_FIRST:]
        tiles.append(both)
        tiles.append(_rows(gates))
        for b in "abc":
            wo = i["w_out_" + b][l]
            t = wo.reshape(4, P, 4, 2, P).transpose(2, 1, 3, 0, 4)
            tiles.append(t.reshape(4, P, 1024))
        tiles.append(_rows(i["w_out"][l]))
        tiles.append(_rows(i["w_query"][l]))
        u = i["expert_u"][l].reshape(NKEYS, NKEYS, KC, P).transpose(1, 3, 2, 0).reshape(NKEYS, P, 1024)
        v = i["expert_v"][l].reshape(NKEYS, NKEYS, D).transpose(1, 0, 2)
        mix = np.empty((2 * BOTH, P, 1024), u.dtype)
        mix[0::2] = u[EARLY:]
        mix[1::2] = v[:BOTH]
        tiles += [u[:EARLY], mix, v[BOTH:]]
    stream = np.concatenate(tiles)
    par = np.zeros((P, DEPTH, NPAR), np.float32)
    for l in range(DEPTH):
        q = par[:, l]
        q[:, PB_ADA:PB_ADA + 48] = i["b_ada"][l].reshape(48, P).T
        q[:, PG1:PG1 + 8] = i["norm1_g"][l].reshape(8, P).T
        q[:, PG2:PG2 + 8] = i["norm2_g"][l].reshape(8, P).T
        q[:, PBG:PBG + 24] = i["b_gate"][l].reshape(24, P).T
        for c, n in ((PQA, "q_norm_a"), (PKA, "k_norm_a"), (PQB, "q_norm_b"), (PKB, "k_norm_b")):
            q[:, c] = np.concatenate([i[n][l], i[n][l]])
        q[:, PQP] = i["q_norm_peer"][l]
        q[:, PSINK:PSINK + 8] = i["sinks"][l]
        q[0:8, PBF] = i["b_forget"][l]
    r = np.arange(P)
    const = np.zeros((P, NCONST), np.float32)
    const[:, C_ID:C_ID + P] = np.eye(P)
    const[:, C_ONE:C_ONE + P] = 1
    const[:, C_BLK:C_BLK + P] = (r[:, None] // HD) == (r[None] // HD)
    const[:, C_TRI:C_TRI + P] = r[:, None] > r[None]
    const[:, C_IOTA:C_IOTA + P] = r[None]
    before = (r[:, None] < r[None]).astype(np.float32)
    const[:, C_CM:C_CM + 384] = np.concatenate([before, np.ones((P, P)), before], 1)
    late = np.where(r[None] <= r[:, None], 0, NEG)
    const[:, C_BT:C_BT + 384] = np.concatenate([late, np.zeros((P, P)), late], 1)
    const[:, C_EPS] = EPS
    chunk = r // 64
    own = np.where(chunk[:, None] >= chunk[None], 0, NEG)
    prev = np.where((chunk[:, None] + 2 - chunk[None]) < 2, 0, NEG)
    d_own, d_prev = np.abs(r[:, None] - r[None]), r[:, None] - (r[None] - P)
    taba = np.zeros((P, HEADS, 384), np.float32)
    for h in range(HEADS):
        s = 2.0 ** -(h + 1)
        a, b = own - s * d_own, prev - s * d_prev
        taba[:, h] = np.concatenate([a, b, a], 1)
    keys = np.zeros((DEPTH, P, PEER_HEADS, 256), np.float32)
    keys[:, 0:64, :, 0:128] = i["sub_keys_1"].transpose(0, 3, 1, 2)
    keys[:, 64:128, :, 128:256] = i["sub_keys_2"].transpose(0, 3, 1, 2)
    xT = i["x"][0].reshape(SEQ, KC, P).transpose(2, 1, 0)
    cT = i["c"][0].reshape(KC, P).T
    return {"stream": stream, "par": par, "const": const, "taba": taba, "keys": keys,
            "xT": xT, "cT": cT}


def kernel(**inputs):
    import numpy as np
    import concourse.bacc as bacc
    from concourse.bass_utils import run_bass_kernel_spmd

    arrays = {k: np.ascontiguousarray(v) for k, v in _lay_out(np, {k: np.asarray(v) for k, v in inputs.items()}).items()}
    nc = bacc.Bacc("TRN2", target_bir_lowering=False, num_devices=1)
    args = [nc.dram_tensor("in_" + n, a.shape, mybir.dt.float32, kind="ExternalInput").ap() for n, a in arrays.items()]
    out = nc.dram_tensor("out", (P, KC, SEQ), mybir.dt.float32, kind="ExternalOutput").ap()
    trunk(nc, *args, out)
    r = run_bass_kernel_spmd(nc, [{"in_" + n: a for n, a in arrays.items()}], core_ids=[0])
    got = r.results[0]["out"]
    return got.transpose(2, 1, 0).reshape(1, SEQ, D)
```

```python
import concourse.bass as bass
from concourse import mybir
from contextlib import ExitStack

DEPTH, SEQ, D = 2, 256, 1024
P = 128
KC = D // P
HD = 64
HEADS = 8
EPS = 1e-6
PEER_HEADS, TOPK, NKEYS = 8, 16, 128
NEG = -1e30

N_QKV = 32
N_GATE = 3 * KC
N_BR = 12
N_OUT = KC
N_QUERY = KC
N_PEER = 2 * NKEYS
EARLY = 88
EXP_AT = EARLY - 8
ROUTE_AT = EARLY - 4
BOTH = NKEYS - EARLY
T_GATE = N_QKV
T_BR = T_GATE + N_GATE
T_OUT = T_BR + N_BR
T_QUERY = T_OUT + N_OUT
T_PEER = T_QUERY + N_QUERY
T_BOTH = T_PEER + EARLY
T_DOWN = T_BOTH + 2 * BOTH
TILES = T_PEER + N_PEER
assert TILES == T_DOWN + EARLY
N_ADA = 6 * KC
ADA_FIRST = 2 * KC
ADA_QKV = 3 * KC
ADA_LATE = 3 * KC
ADA_GROUPS = N_ADA // 2
MG1, MS2, MC2, MG2, MS1, MC1 = (KC * n for n in range(6))
HOT_B = 3 * SEQ // 16
H_2, H_READY = KC, 2 * KC
HI_MERGED, HI_2, HI_READY = KC, 2 * KC, 3 * KC
M_MIX, M_MERGED, M_2, M_READY = KC, KC + 6, 2 * KC + 6, 3 * KC + 6
RAW = 4
SPLIT = 2
O_GATE = N_QKV
O_BR = O_GATE + N_GATE
O_OUT = O_BR + N_BR
O_QUERY = O_OUT + N_OUT
O_PEER = O_QUERY + N_QUERY
OUTS = O_PEER + NKEYS

QA, KA, VA, QB, KB, VB, FG, QC, KCT, VC = 0, 4, 5, 6, 10, 14, 18, 19, 23, 27
V_TILES = [VA] + [VB + i for i in range(4)] + [VC + i for i in range(4)]

PB_ADA, PG1, PG2, PBG = 0, 48, 56, 64
PQA, PKA, PQB, PKB, PQP, PSINK, PBF = 88, 89, 90, 91, 92, 93, 101
NPAR = 102
C_ID, C_ONE, C_IOTA, C_ZERO, C_EPS = 0, 128, 256, 384, 512
NCONST = 516
X_BLK, X_TRI, X_CM, X_BT = 0, 128, 256, 640
NMIX = 1024


def trunk(nc, stream, par_dram, const_dram, mix_dram, taba_dram, keys_dram, front_dram, ada_dram, x_dram, c_dram,
          out_dram):
    f32, f32r, u32 = mybir.dt.float32, mybir.dt.float32r, mybir.dt.uint32
    ALU, ACT, AX = mybir.AluOpType, mybir.ActivationFunctionType, mybir.AxisListType

    ctx = ExitStack()
    with ctx:
        def sb(name, shape, dt=f32):
            return ctx.enter_context(nc.sbuf_tensor(name, shape, dt))

        def sem(name):
            return ctx.enter_context(nc.semaphore(name))

        raw = [sb(f"raw{i}", [P, 1024]) for i in range(RAW)]
        hi = [sb(f"hi{i}", [P, 1024], f32r) for i in range(SPLIT)]
        lo = [sb(f"lo{i}", [P, 1024], f32r) for i in range(SPLIT)]
        x = sb("x", [P, KC, SEQ])
        mov_hi = sb("mov_hi", [P, 12, SEQ], f32r)
        mov_lo = sb("mov_lo", [P, 12, SEQ], f32r)
        w_hi = mov_hi[:, KC:KC + 4, :]
        w_lo = mov_lo[:, KC:KC + 4, :]
        const = sb("const", [P, NCONST])
        par_all = sb("par_all", [P, DEPTH, NPAR])
        par = sb("par", [P, NPAR])
        c_in = sb("c_in", [P, KC])
        c_tmp = sb("c_tmp", [P, KC])
        mod = sb("mod", [P, N_ADA])
        amp = sb("amp", [P, 2, KC])
        gain = sb("gain", [P, 2])
        small = sb("small", [P, 96])
        idx1T = sb("idx1T", [P, SEQ])
        idx2T = sb("idx2T", [P, SEQ])
        gateT = sb("gateT", [P, SEQ])
        ada_late = sb("ada_late", [P, 2, 512])
        onehot_a = sb("onehot_a", [P, 8, NKEYS])
        onehot_b = w_hi.rearrange("p a b -> p (a b)").rearrange("p (r i) -> p r i", r=8)
        act_g = onehot_a[:, 0:4, :].rearrange("p a b -> p (a b)").rearrange("p (r s) -> p r s", r=2)
        rstd = act_g[:, 0, :]

        ident = const[:, C_ID:C_ID + P]
        ones = const[:, C_ONE:C_ONE + P]
        iota = const[:, C_IOTA:C_IOTA + P]
        zero = const[:, C_ZERO:C_ZERO + P]
        eps = const[:, C_EPS:C_EPS + 1]
        mx, negm, den, sinkd = small[:, 0:16], small[:, 16:32], small[:, 32:48], small[:, 48:64]
        rden = small[:, 64:80]

        arena = sb("arena", [P, NKEYS, SEQ])
        flat = arena[:, :, :].rearrange("p a b -> p (a b)")
        used = [0]

        def part(n):
            a = flat[:, used[0]:used[0] + n]
            used[0] += n
            return a

        projT = part(56 * SEQ).rearrange("p (t s) -> p t s", s=SEQ)
        vtok = part(2 * 1152).rearrange("p (b c) -> p b c", b=2)
        taba = part(HEADS * 384).rearrange("p (h c) -> p h c", h=HEADS)
        prob = part(HEADS * 384).rearrange("p (h c) -> p h c", h=HEADS)
        probT = part(2 * 384).rearrange("p (r c) -> p r c", r=2)
        ytok = part(2 * 3 * 512).rearrange("p (b r c) -> p b r c", b=2, r=3)
        merged = part(KC * SEQ).rearrange("p (k s) -> p k s", s=SEQ)
        gated = part(2 * 512).rearrange("p (r c) -> p r c", r=2)
        sq = part(KC * SEQ).rearrange("p (k s) -> p k s", s=SEQ)
        mix = part(NMIX)
        blk, tri = mix[:, X_BLK:X_BLK + P], mix[:, X_TRI:X_TRI + P]
        cmask, btab = mix[:, X_CM:X_CM + 384], mix[:, X_BT:X_BT + 384]
        assert used[0] <= NKEYS * SEQ, used
        ada_front = flat[:, 0:ADA_FIRST * 1024].rearrange("p (t c) -> p t c", t=ADA_FIRST)
        ada_slot = prob.rearrange("p h c -> p (h c)")[:, 0:2048].rearrange("p (r c) -> p r c", r=2)
        stick = prob.rearrange("p h c -> p (h c)")[:, 0:8 * 384].rearrange("p (r n c) -> p r n c", r=2, n=4)
        used[0] = EARLY * SEQ
        keys_at = used[0]
        skeys = part(PEER_HEADS * 256).rearrange("p (h c) -> p h c", h=PEER_HEADS)
        query_at = used[0]
        queryT = part(KC * SEQ).rearrange("p (k s) -> p k s", s=SEQ)
        score_at = used[0]
        score = part(16 * 256).rearrange("p (u c) -> p u c", u=16)
        rest = part(2 * 128).rearrange("p (r c) -> p r c", r=2)
        cand = part(256)
        candr = part(256)
        sel_v = part(4 * 16).rearrange("p (r n k) -> p r n k", r=2, n=2)
        sel_i = part(16 * 32).rearrange("p (u n k) -> p u n k", u=16, n=2).bitcast(u32)
        top_s = part(16 * 16).rearrange("p (u k) -> p u k", u=16)
        top_p = part(16 * 16).rearrange("p (u k) -> p u k", u=16).bitcast(u32)
        gsum = part(2 * 16).rearrange("p (n c) -> p n c", n=2)
        assert used[0] <= NKEYS * SEQ, used
        used[0] = score_at
        sq2 = part(KC * SEQ).rearrange("p (k s) -> p k s", s=SEQ)
        used[0] = keys_at
        sel_if = part(16 * 32).rearrange("p (u n k) -> p u n k", u=16, n=2)
        pos_i = part(2 * 256).rearrange("p (n c) -> p n c", n=2).bitcast(u32)
        pos_f = part(2 * 256).rearrange("p (n c) -> p n c", n=2)
        idx_tok = part(2 * 256).rearrange("p (n c) -> p n c", n=2)
        assert used[0] <= query_at
        used[0] = query_at
        pick = part(8 * 256)
        ftok = arena[:, 0:8, :].rearrange("p a b -> p (a b)").rearrange("p (b c) -> p b c", b=2)
        fl = sq[0:HEADS, 0:4, :]

        pj = [ctx.enter_context(nc.psum_tensor(f"pj{i}", [P, 512], f32)) for i in range(2)]
        wk = ctx.enter_context(nc.psum_tensor("wk", [P, 6, 512], f32))
        wkf = wk[:, :, :].rearrange("p b c -> p (b c)")

        F_BANK = (2, 4, 3, 5)

        def group_of(n):
            return arena[:, n, :] if isinstance(n, int) else arena[:, bass.ds(n, 1), :].squeeze(1)

        setup_loaded = sem("setup_loaded")
        setup_step = sem("setup_step")
        c_exp = sem("c_exp")
        c_ready = sem("c_ready")
        front_loaded = [sem(f"front_loaded{i}") for i in range(4)]
        ada_loaded = [sem(f"ada_loaded{i}") for i in range(2)]
        late_loaded = [sem(f"late_loaded{i}") for i in range(2)]
        ada_used = sem("ada_used")
        late_used = sem("late_used")
        raw_loaded = [sem(f"raw_loaded{i}") for i in range(RAW)]
        hi_done = sem("hi_done")
        lo_done = sem("lo_done")
        tile_done = sem("tile_done")
        out_free = sem("out_free")
        x_ready = sem("x_ready")
        sq_ready = sem("sq_ready")
        ss_ready = sem("ss_ready")
        rstd_ready = sem("rstd_ready")
        h_ready = sem("h_ready")
        h_hi = sem("h_hi")
        mov_ready = sem("mov_ready")
        tables = sem("tables")
        arena_free = sem("arena_free")
        keys_free = sem("keys_free")
        keys_in = sem("keys_in")
        vtr = sem("vtr")
        vtok_in = sem("vtok_in")
        qk_sq = sem("qk_sq")
        qk_sq2 = sem("qk_sq2")
        qk_ss = sem("qk_ss")
        qk_rr = sem("qk_rr")
        qk_done = sem("qk_done")
        f_sum = sem("f_sum")
        f_log = sem("f_log")
        f_ready = sem("f_ready")
        score_ready = sem("score_ready")
        score_read = sem("score_read")
        negmax = sem("negmax")
        sinkd_exp = sem("sinkd_exp")
        prob_ready = sem("prob_ready")
        ptr_ready = sem("ptr_ready")
        pt_copied = sem("pt_copied")
        pv_done = sem("pv_done")
        sigmoids = sem("sigmoids")
        y_read = sem("y_read")
        z_ready = sem("z_ready")
        z_log = sem("z_log")
        z_read = sem("z_read")
        tail_ready = sem("tail_ready")
        stick_arg = sem("stick_arg")
        stick_exp = sem("stick_exp")
        stick_ready = sem("stick_ready")
        ytr = sem("ytr")
        y_hi = sem("y_hi")
        merged_zero = sem("merged_zero")
        br_add = sem("br_add")
        q_sq = sem("q_sq")
        q_ss = sem("q_ss")
        q_rr = sem("q_rr")
        q_norm = sem("q_norm")
        s_ready = sem("s_ready")
        s_copied = sem("s_copied")
        g_arg = sem("g_arg")
        g_exp = sem("g_exp")
        route_ready = sem("route_ready")
        route_tr = sem("route_tr")
        route_in = sem("route_in")
        hot_a = sem("hot_a")
        hot_b = sem("hot_b")
        hot_used = sem("hot_used")
        hot_dist = sem("hot_dist")
        g_times = sem("g_times")
        g_free = sem("g_free")
        front_used = sem("front_used")
        mod_own = sem("mod_own")
        mod_read = sem("mod_read")
        w_made = sem("w_made")
        w_head = sem("w_head")
        w_rest = sem("w_rest")
        f_tok = sem("f_tok")
        f_tok2 = sem("f_tok2")
        f_tr = sem("f_tr")
        stored = sem("stored")
        waits_met = sem("waits_met")
        act_step = sem("act_step")
        dve_step = sem("dve_step")

        def wait_alone(eng, s, value):
            eng.wait_ge(s, value)
            eng.sem_inc(waits_met, 1)

        block = ctx.enter_context(nc.Block())

        @block.sync
        def _(sp):
            sp.dma_start(c_in[:, :], c_dram).then_inc(setup_loaded, 16)
            sp.dma_start(par_all[:, :, :], par_dram).then_inc(setup_loaded, 16)
            sp.dma_start(const[:, :], const_dram).then_inc(setup_loaded, 16)
            sp.dma_start(x[:, :, :], x_dram).then_inc(setup_loaded, 16)
            for j in range(4):
                f = slice(j * ADA_FIRST // 4, (j + 1) * ADA_FIRST // 4)
                sp.dma_start(ada_front[:, f, :], front_dram[:, f, :]).then_inc(front_loaded[j], 16)
            for j in range(RAW):
                sp.dma_start(raw[j][:, :], stream[j]).then_inc(raw_loaded[j], 16)
            with sp.Fori(0, DEPTH * TILES // RAW - 1) as i:
                for j in range(RAW):
                    sp.wait_ge(lo_done, i * RAW + j + 1)
                    sp.dma_start(raw[j][:, :], stream[i * RAW + RAW + j]).then_inc(raw_loaded[j], 16)
            sp.wait_ge(x_ready, (DEPTH + 1) * KC)
            sp.dma_start(out_dram, x[:, :, :]).then_inc(stored, 16)
            sp.wait_ge(stored, 16)

        @block.gpsimd
        def _(pool):
            with pool.Fori(0, DEPTH) as l:
                wait_alone(pool, arena_free, l + 1)
                pool.dma_start(mix, mix_dram).then_inc(tables, 16)
                pool.dma_start(taba, taba_dram).then_inc(tables, 16)
                with pool.Fori(0, ADA_QKV // 2) as i:
                    for j in range(2):
                        wait_alone(pool, ada_used, l * ADA_QKV + i * 2 + (j + 1))
                        pool.dma_start(ada_slot[:, j, :], ada_dram[l * N_ADA + i * 2 + j])\
                            .then_inc(ada_loaded[j], 16)
                wait_alone(pool, qk_done, 2 * l + 2)
                nc.gpsimd.memset(merged, 0.0).then_inc(merged_zero, 1)
                wait_alone(pool, keys_free, l + 1)
                pool.dma_start(skeys, keys_dram[l]).then_inc(keys_in, 16)
                with pool.Fori(0, ADA_LATE // 2) as i:
                    for j in range(4):
                        wait_alone(pool, late_used, l * (2 * ADA_LATE) + i * 4 + (j + 1))
                        pool.dma_start(ada_late[:, j % 2, :],
                                       ada_dram[l * N_ADA + i * 2 + (ADA_QKV + j // 2)][:, j % 2 * 512:j % 2 * 512 + 512])\
                            .then_inc(late_loaded[j % 2], 16)

        @block.scalar
        def _(act):
            def head(t, j):
                act.wait_ge(raw_loaded[j % RAW], 16 + load_count(t, j))
                act.wait_ge(tile_done, t + 1)
                nc.scalar.activation(hi[j % SPLIT][:, :], raw[j % RAW][:, :], ACT.Copy).then_inc(hi_done, 1)

            def load_count(t, j):
                return (t - (j % RAW)) * (16 // RAW)

            act.wait_ge(setup_loaded, 64)
            nc.scalar.activation(c_tmp[:, :], c_in[:, :], ACT.Exp, scale=-1.0).then_inc(c_exp, 1)
            with act.Fori(0, DEPTH) as l:
                act.sem_clear(act_step)
                n_link = [0]
                L0 = l * TILES

                def link(ins):
                    ins.then_inc(act_step, 1)
                    n_link[0] += 1
                    act.wait_ge(act_step, n_link[0])

                def norm(n, sq):
                    act.wait_ge(ss_ready, 2 * l + n + 1)
                    link(nc.scalar.activation(rstd, wk[:, 0, 0:SEQ], ACT.Ln, bias=eps, scale=1.0 / D))
                    nc.scalar.activation(rstd, rstd, ACT.Exp, scale=-0.5).then_inc(rstd_ready, 1)
                    for k in range(KC):
                        shift = (MS1, MS2)[n] + k
                        act.wait_ge(h_ready, l * H_READY + ((0, H_2)[n] + k + 1))
                        nc.scalar.activation(mov_hi[:, k, :], sq[:, k, :], ACT.Identity,
                                             bias=mod[:, shift:shift + 1]).then_inc(h_hi, 1)

                nc.scalar.preload_act_table_set("natural_log_exp_and_others")
                head(L0, 0)
                head(L0 + 1, 1)
                for k in range(KC):
                    act.wait_ge(x_ready, l * KC + (k + 1))
                    nc.scalar.activation(sq[:, k, :], x[:, k, :], ACT.Square).then_inc(sq_ready, 1)
                norm(0, sq)
                with act.Fori(0, N_QKV // 4) as i:
                    for j in range(4):
                        t = L0 + i * 4 + j
                        head(t + 2, j + 2)
                        act.wait_ge(tile_done, t + 3)
                        nc.scalar.activation(projT[:, bass.ds(i * 4 + j, 1), :].squeeze(1), pj[j % 2][:, 0:SEQ],
                                             ACT.Copy).then_inc(out_free, 1)
                def gate(n):
                    t = L0 + (T_GATE + n)
                    head(t + 2, n + 2)
                    act.wait_ge(tile_done, t + 3)
                    nc.scalar.activation(projT[:, N_QKV + n, :], pj[n % 2][:, 0:SEQ], ACT.Identity,
                                         bias=par[:, PBG + n:PBG + n + 1]).then_inc(out_free, 1)

                for b in range(2):
                    act.wait_ge(vtr, 2 * l + b + 1)
                    nc.scalar.activation(vtok[:, b, :], wkf[:, b * 1536:b * 1536 + 1152], ACT.Copy)\
                        .then_inc(vtok_in, 1)
                act.wait_ge(out_free, l * OUTS + (O_GATE + 2))
                for g, (t0, n) in enumerate(((QA, 5), (QB, 8))):
                    if g == 0:
                        nc.scalar.activation(sq[:, 0:n, :], projT[:, t0:t0 + n, :], ACT.Square).then_inc(qk_sq, 1)
                    gate(g)
                    act.wait_ge(qk_ss, 2 * l + g + 1)
                    sqf = (sq, merged)[g].rearrange("p k s -> p (k s)")[:, 0:n * SEQ]
                    link(nc.scalar.activation(sqf, wkf[:, 0:n * SEQ], ACT.Ln, bias=eps, scale=1.0 / HD))
                    nc.scalar.activation(sqf, sqf, ACT.Exp, scale=-0.5).then_inc(qk_rr, 1)
                gate(2)
                act.wait_ge(f_sum, l + 1)
                link(nc.scalar.activation(fl[:, 1, :], fl[:, 0, :], ACT.Abs))
                link(nc.scalar.activation(fl[:, 1, :], fl[:, 1, :], ACT.Exp, scale=-1.0))
                nc.scalar.activation(fl[:, 1, :], fl[:, 1, :], ACT.Ln, bias=1.0).then_inc(f_log, 1)
                gate(3)
                for br, (first, between) in enumerate(((4, {1: [5], 5: [6], 7: [7]}),
                                                       (8, {1: [9], 3: [10], 5: [11], 7: [12, 13]}))):
                    gate(first)
                    act.wait_ge(negmax, 2 * l + br + 1)
                    for h in range(HEADS):
                        for b, (c0, c1) in enumerate(((0, 128), (128, 384))):
                            e = nc.scalar.activation(prob[:, h, c0:c1], prob[:, h, c0:c1], ACT.Exp,
                                                     bias=negm[:, b * 8 + h:b * 8 + h + 1],
                                                     accum_out=den[:, b * 8 + h:b * 8 + h + 1])
                        e.then_inc(prob_ready, 1)
                        if br == 0 and h == HEADS - 1:
                            nc.scalar.activation(sinkd, sinkd, ACT.Exp).then_inc(sinkd_exp, 1)
                        for n in between.get(h, ()):
                            gate(n)
                def stick_tail(h):
                    act.wait_ge(stick_arg, 8 * l + h + 1)
                    nc.scalar.activation(stick[:, h % 2, 2, :], stick[:, h % 2, 2, :], ACT.Exp)\
                        .then_inc(stick_exp, 1)

                act.wait_ge(ptr_ready, 16 * l + 16)
                for h in range(HEADS):
                    act.wait_ge(z_ready, 8 * l + h + 1)
                    if h >= 2:
                        act.wait_ge(stick_ready, 8 * l + h - 1)
                    link(nc.scalar.activation(stick[:, h % 2, 0, :], wk[:, 2 + h % 2, 0:384], ACT.Abs))
                    link(nc.scalar.activation(stick[:, h % 2, 0, :], stick[:, h % 2, 0, :], ACT.Exp, scale=-1.0))
                    nc.scalar.activation(stick[:, h % 2, 0, :], stick[:, h % 2, 0, :], ACT.Ln, bias=1.0)\
                        .then_inc(z_log, 1)
                    if h:
                        stick_tail(h - 1)
                        gate(13 + h)
                stick_tail(HEADS - 1)
                for n in (21, 22, 23):
                    gate(n)
                for n in range(6):
                    br, b = n // 2, n % 2
                    act.wait_ge(ytr, 6 * l + n + 1)
                    nc.scalar.activation(mov_hi[:, 4 * br:4 * br + 4, b * P:(b + 1) * P],
                                         wk[:, n, :].rearrange("p (c t) -> p c t", c=4), ACT.Copy)\
                        .then_inc(y_hi, 1)
                nc.scalar.preload_act_table_set("sigmoid_and_others")
                act.wait_ge(out_free, l * OUTS + (O_BR + 2))
                with act.Fori(0, N_BR // 4) as i:
                    gates = projT[:, bass.ds(i * KC + N_QKV, KC), :]
                    nc.scalar.activation(gates, gates, ACT.Sigmoid).then_inc(sigmoids, 1)
                    for j in range(4):
                        head(L0 + i * 4 + (T_BR + 2 + j), j + 2)
                for k in range(KC):
                    act.wait_ge(br_add, l * N_BR + (2 * N_BR // 3 + k // 2 + 1))
                    nc.scalar.activation(mov_hi[:, k, :], merged[:, k, :], ACT.Copy).then_inc(h_hi, 1)
                nc.scalar.preload_act_table_set("natural_log_exp_and_others")
                with act.Fori(0, N_OUT // 4) as i:
                    for j in range(4):
                        head(L0 + i * 4 + (T_OUT + 2 + j), j + 2)
                        act.wait_ge(out_free, l * OUTS + i * 4 + (O_OUT + 3 + j))
                        nc.scalar.activation(sq2[:, bass.ds(i * 4 + j, 1), :].squeeze(1),
                                             x[:, bass.ds(i * 4 + j, 1), :].squeeze(1), ACT.Square)\
                            .then_inc(sq_ready, 1)
                norm(1, sq2)
                with act.Fori(0, N_QUERY // 4) as i:
                    for j in range(4):
                        t = L0 + i * 4 + (T_QUERY + j)
                        head(t + 2, j + 2)
                        act.wait_ge(tile_done, t + 3)
                        nc.scalar.activation(queryT[:, bass.ds(i * 4 + j, 1), :].squeeze(1), pj[j % 2][:, 0:SEQ],
                                             ACT.Copy).then_inc(out_free, 1)
                act.wait_ge(out_free, l * OUTS + (O_PEER + 2))
                nc.scalar.activation(sq2, queryT, ACT.Square).then_inc(q_sq, 1)
                head(L0 + (T_PEER + 2), 2)
                act.wait_ge(q_ss, l + 1)
                sqf = sq2.rearrange("p k s -> p (k s)")
                link(nc.scalar.activation(sqf, wkf[:, 0:2048], ACT.Ln, bias=eps, scale=1.0 / P))
                nc.scalar.activation(sqf, sqf, ACT.Exp, scale=-0.5).then_inc(q_rr, 1)
                head(L0 + (T_PEER + 3), 3)
                for u in range(0, 16, 2):
                    act.wait_ge(s_ready, 16 * l + u + 2)
                    nc.scalar.activation(score[:, u:u + 2, :],
                                         wk[:, (u // 2) % 6, :].rearrange("p (u c) -> p u c", u=2), ACT.Copy)\
                        .then_inc(s_copied, 1)

                nc.scalar.preload_act_table(ACT.Gelu_apprx_tanh)
                def early_group(i, j, ahead=True):
                    t = L0 + i * 4 + (T_PEER + j)
                    if ahead:
                        head(t + 2, j + 2)
                    act.wait_ge(tile_done, t + 3)
                    nc.scalar.activation(arena[:, bass.ds(i * 4 + j, 1), :].squeeze(1), pj[j % 2][:, 0:SEQ],
                                         ACT.Gelu_apprx_tanh).then_inc(out_free, 1)

                for j in range(4):
                    early_group(l * 0, j, j >= 2)
                with act.Fori(1, EXP_AT // 4) as i:
                    for j in range(4):
                        early_group(i, j)
                nc.scalar.preload_act_table_set("natural_log_exp_and_others")
                act.wait_ge(g_arg, l + 1)
                nc.scalar.activation(top_s, top_s, ACT.Exp).then_inc(g_exp, 1)
                nc.scalar.preload_act_table(ACT.Gelu_apprx_tanh)
                with act.Fori(EXP_AT // 4, EARLY // 4) as i:
                    for j in range(4):
                        early_group(i, j)
                act.wait_ge(route_in, 6 * l + 6)

                def one_hot(group, q, i):
                    slot = q % 2 * 4
                    act.wait_ge(hot_used, l * SEQ + group * 4 + 4)
                    for r in range(4):
                        e = nc.scalar.activation(onehot_b[:, slot + r, :], iota, ACT.Abs,
                                                 bias=idx2T[:, bass.ds(group * 4 + r, 1)], scale=-1.0)
                    e.then_inc(hot_dist, 1)
                    act.wait_ge(hot_dist, l * HOT_B + i * 3 + (q + 1))
                    nc.scalar.activation(onehot_b[:, slot:slot + 4, :], onehot_b[:, slot:slot + 4, :].bitcast(f32),
                                         ACT.Relu, bias=1.0, scale=-1.0).then_inc(hot_b, 1)

                def copy_g(group, j):
                    act.wait_ge(g_times, l * (SEQ // 4) + group + 1)
                    nc.scalar.activation(
                        arena[:, EARLY:NKEYS, bass.ds(group * 4, 4)].rearrange("p i t -> p t i"),
                        wk[:, 2 + j, :].rearrange("p (t i) -> p t i", t=4)[:, :, EARLY:NKEYS],
                        ACT.Copy).then_inc(g_free, 1)

                one_hot(l * 0, 0, l * 0)
                one_hot(l * 0 + 1, 1, l * 0)
                with act.Fori(0, SEQ // 16 - 1) as i:
                    for q in range(4):
                        if q != 1:
                            one_hot(i * 4 + (q + 2), (q + 2) % 4, i + (q + 2) // 4)
                        copy_g(i * 4 + q, q)
                for q in range(4):
                    if q == 0:
                        one_hot(l * 0 + (SEQ // 4 - 2), 2, l * 0 + (SEQ // 16 - 1))
                    copy_g(l * 0 + (SEQ // 4 - 4 + q), q)

                def w_heads(n, s):
                    nc.scalar.activation(w_hi[:, s, :], group_of(n), ACT.Copy).then_inc(w_head, 1)

                act.wait_ge(g_free, l * (SEQ // 4) + (SEQ // 4 + 4))
                for n in range(3):
                    w_heads(n, n)
                with act.Fori(0, BOTH // 4) as i:
                    for j in range(4):
                        t = L0 + i * 8 + (T_BOTH + 2 * j)
                        head(t + 2, 2 * j + 2)
                        act.wait_ge(tile_done, t + 3)
                        nc.scalar.activation(act_g[:, j % 2, :], pj[j % 2][:, 0:SEQ], ACT.Gelu_apprx_tanh)\
                            .then_inc(out_free, 1)
                        w_heads(i * 4 + (j + 3), (j + 3) % 4)
                        head(t + 3, 2 * j + 3)
                act.wait_ge(w_made, (l + 1) * BOTH)
                with act.Fori(0, EARLY // 4 - 1) as i:
                    for j in range(4):
                        t = L0 + i * 4 + (T_DOWN + j)
                        head(t + 2, j + 2)
                        act.wait_ge(tile_done, t + 3)
                        w_heads(i * 4 + (BOTH + j + 3), (j + 3) % 4)
                t = L0 + TILES - 4
                head(t + 2, 2)
                act.wait_ge(tile_done, t + 3)
                w_heads(NKEYS - 1, 3)
                head(t + 3, 3)
                act.wait_ge(tile_done, L0 + TILES + 2)
                for e in range(2):
                    nc.scalar.activation(ftok[:, 1, e * 512:(e + 1) * 512], wk[:, 4 + e, :], ACT.Copy)\
                        .then_inc(f_tok2, 1)

        @block.vector
        def _(dve):
            setup = [0]

            def slink(ins):
                ins.then_inc(setup_step, 1)
                setup[0] += 1
                dve.wait_ge(setup_step, setup[0])

            def rest_of(t, j):
                dve.wait_ge(hi_done, t + 1)
                nc.vector.tensor_tensor(lo[j % SPLIT][:, :], raw[j % RAW][:, :], hi[j % SPLIT][:, :].bitcast(f32),
                                        ALU.subtract).then_inc(lo_done, 1)

            dve.wait_ge(setup_loaded, 64)
            dve.wait_ge(c_exp, 1)
            slink(nc.vector.tensor_scalar(c_tmp[:, :], c_tmp[:, :], 1.0, None, ALU.add))
            slink(nc.vector.reciprocal(c_tmp[:, :], c_tmp[:, :]))
            nc.vector.tensor_tensor(c_tmp[:, :], c_tmp[:, :], c_in[:, :], ALU.mult).then_inc(c_ready, 1)
            dve.sem_inc(x_ready, KC)
            dve.sem_inc(arena_free, 1)

            def own_columns(own, src, cols, count):
                n = cols.shape[-1]
                nc.vector.tensor_tensor(own.rearrange("p (a b) -> p a b", a=n), src.rearrange("p (a b) -> p a b", a=n),
                                        ident.unsqueeze(1).to_broadcast([P, n, P]), ALU.mult).then_inc(mod_own, 1)
                dve.wait_ge(mod_own, count)
                nc.vector.tensor_reduce(cols, own.rearrange("p (a b) -> p a b", a=n), AX.X, ALU.add)\
                    .then_inc(mod_read, 1)

            for n in range(4):
                dve.wait_ge(front_used, n + 1)
                own_columns(gated[:, n % 2, :], wk[:, n, :], mod[:, MS1 + 4 * n:MS1 + 4 * n + 4], n + 1)

            with dve.Fori(0, DEPTH) as l:
                dve.sem_clear(dve_step)
                n_link = [0]
                L0 = l * TILES

                def link(ins):
                    ins.then_inc(dve_step, 1)
                    n_link[0] += 1
                    dve.wait_ge(dve_step, n_link[0])

                def norm(n, sq):
                    def scaled(k):
                        nc.vector.scalar_tensor_tensor(sq[:, k, :], x[:, k, :], amp[:, n, k:k + 1], rstd, ALU.mult,
                                                       ALU.mult).then_inc(h_ready, 1)

                    dve.wait_ge(rstd_ready, 2 * l + n + 1)
                    scaled(0)
                    for k in range(KC):
                        if k + 1 < KC:
                            scaled(k + 1)
                        shift = (MS1, MS2)[n] + k
                        dve.wait_ge(h_hi, l * HI_READY + ((0, HI_2)[n] + k + 1))
                        nc.vector.scalar_tensor_tensor(mov_lo[:, k, :], sq[:, k, :], mod[:, shift:shift + 1],
                                                       mov_hi[:, k, :].bitcast(f32), ALU.add,
                                                       ALU.subtract).then_inc(mov_ready, 1)

                link(nc.vector.tensor_copy(par[:, :], par_all[:, bass.ds(l, 1), :].squeeze(1)))
                def modulation(used, count, group, cols):
                    dve.wait_ge(used, count)
                    own_columns(wk[:, 1, 256:512], wk[:, 1, 0:256], cols, l * ADA_GROUPS + group + 5)

                rest_of(L0, 0)
                rest_of(L0 + 1, 1)
                dve.wait_ge(mod_read, l * ADA_GROUPS + 4)
                link(nc.vector.tensor_tensor(mod[:, MS1:N_ADA], mod[:, MS1:N_ADA], par[:, MS1:N_ADA], ALU.add))
                nc.vector.scalar_tensor_tensor(amp[:, 0, :], mod[:, MC1:MC1 + KC], 1.0, par[:, PG1:PG1 + KC],
                                               ALU.add, ALU.mult)
                for n, g in ((0, PQA), (1, PQB)):
                    link(nc.vector.tensor_scalar(gain[:, n:n + 1], par[:, g:g + 1], HD ** -0.5, None, ALU.mult))
                norm(0, sq)
                with dve.Fori(0, N_QKV // 8) as i:
                    for j in range(8):
                        rest_of(L0 + i * 8 + (j + 2), j + 2)
                        if j in (1, 4, 6):
                            g = (1, 4, 6).index(j)
                            modulation(ada_used, l * ADA_QKV + i * 6 + (2 * g + 4), i * 3 + g,
                                       mod[:, bass.ds(i * 6 + (MG1 + 2 * g), 2)])

                def gate(n):
                    rest_of(L0 + (T_GATE + 2 + n), n + 2)

                dve.wait_ge(mod_read, l * ADA_GROUPS + (ADA_QKV // 2 + 4))
                link(nc.vector.tensor_tensor(mod[:, MG1:MG2], mod[:, MG1:MG2], par[:, MG1:MG2], ALU.add))
                nc.vector.scalar_tensor_tensor(amp[:, 1, :], mod[:, MC2:MC2 + KC], 1.0, par[:, PG2:PG2 + KC],
                                               ALU.add, ALU.mult)
                dve.wait_ge(out_free, l * OUTS + (O_GATE + 2))
                nc.vector.tensor_scalar(projT[:, QC:QC + 4, :], projT[:, QC:QC + 4, :], HD ** -0.5, None, ALU.mult)
                nc.vector.tensor_tensor(merged, projT[:, QB:QB + 8, :], projT[:, QB:QB + 8, :],
                                        ALU.mult).then_inc(qk_sq2, 1)
                for g, (q0, k0, nk, gk) in enumerate(((QA, KA, 1, PKA), (QB, KB, 4, PKB))):
                    if g == 0:
                        gate(0)
                    dve.wait_ge(qk_rr, 2 * l + g + 1)
                    nc.vector.scalar_tensor_tensor(projT[:, q0:q0 + 4, :], projT[:, q0:q0 + 4, :], gain[:, g:g + 1],
                                                   (sq, merged)[g][:, 0:4, :], ALU.mult, ALU.mult)
                    nc.vector.scalar_tensor_tensor(projT[:, k0:k0 + nk, :], projT[:, k0:k0 + nk, :],
                                                   par[:, gk:gk + 1], (sq, merged)[g][:, 4:4 + nk, :], ALU.mult,
                                                   ALU.mult).then_inc(qk_done, 1)
                    if g == 0:
                        gate(1)
                dve.wait_ge(qk_done, 2 * l + 2)
                nc.vector.tensor_scalar(fl[:, 0, :], projT[0:HEADS, FG, :], par[0:HEADS, PBF:PBF + 1], None,
                                        ALU.add).then_inc(f_sum, 1)
                gate(2)
                gate(3)
                dve.wait_ge(tables, 32 * l + 32)
                for br in range(2):
                    if br:
                        dve.wait_ge(ptr_ready, 16 * l + 8)
                    for h in range(HEADS):
                        wait_alone(dve, score_ready, 16 * l + 8 * br + h + 1)
                        for b, (c0, c1) in enumerate(((0, 128), (128, 384))):
                            tab = taba[:, h, c0:c1] if br == 0 else btab[:, c0:c1]
                            e = nc.vector.tensor_tensor_reduce(
                                out=prob[:, h, c0:c1], in0=wk[:, 2 + h % 2, c0:c1], in1=tab, scale=1.0,
                                scalar=-3e38, op0=ALU.add, op1=ALU.max, accum_out=mx[:, b * 8 + h:b * 8 + h + 1])
                        e.then_inc(score_read, 1)
                        if h == 3:
                            gate(4 + 4 * br)
                    dve.wait_ge(score_read, 16 * l + 8 * br + 8)
                    if br == 0:
                        sink = par[:, PSINK:PSINK + 8].unsqueeze(1).to_broadcast([P, 2, 8])
                        mx2, sk2 = mx.rearrange("p (b h) -> p b h", b=2), sinkd.rearrange("p (b h) -> p b h", b=2)
                        link(nc.vector.tensor_tensor(mx2, mx2, sink, ALU.max))
                        link(nc.vector.tensor_tensor(sk2, sink, mx2, ALU.subtract))
                    nc.vector.tensor_scalar(negm, mx, -1.0, None, ALU.mult).then_inc(negmax, 1)
                    for g in ((5,), (9, 10))[br]:
                        gate(g)
                    if br == 0:
                        dve.wait_ge(f_log, l + 1)
                        link(nc.vector.scalar_tensor_tensor(fl[:, 0, :], fl[:, 0, :], 0.0, fl[:, 1, :], ALU.min,
                                                            ALU.subtract))
                        link(nc.vector.tensor_tensor_scan(fl[:, 2, :], const[0:HEADS, C_ONE:C_ONE + 1].to_broadcast([HEADS, SEQ]),
                                                          fl[:, 0, :], 0.0, ALU.mult, ALU.add))
                        nc.vector.tensor_scalar(fl[:, 3, :], fl[:, 2, :], -1.0, None, ALU.mult).then_inc(f_ready, 1)
                    for h in range(HEADS):
                        n = 8 * br + h
                        dve.wait_ge(ptr_ready, 16 * l + n + 1)
                        if n >= 2:
                            dve.wait_ge(pv_done, 24 * l + n - 1)
                        nc.vector.tensor_copy(probT[:, h % 2, :], wk[:, h % 2, 0:384]).then_inc(pt_copied, 1)
                        if h in (2, 5):
                            gate((6, 11)[br] + h // 3)
                    dve.wait_ge(prob_ready, 16 * l + 8 * br + 8)
                    if br == 0:
                        dve.wait_ge(sinkd_exp, l + 1)
                        link(nc.vector.tensor_tensor(den, den, sinkd, ALU.add))
                    link(nc.vector.reciprocal(rden, den))
                    dve.wait_ge(pv_done, 24 * l + 8 * br + 8)
                    for b in range(2):
                        e = nc.vector.tensor_tensor(
                            ytok[:, b, br, :].rearrange("p (h c) -> p h c", h=8),
                            wk[:, 4 + b, :].rearrange("p (h c) -> p h c", h=8),
                            rden[:, b * 8:b * 8 + 8].unsqueeze(2).to_broadcast([P, 8, HD]), ALU.mult)
                    e.then_inc(y_read, 1)
                    if br:
                        gate(13)
                def stick_tail(h):
                    s = h % 2
                    dve.wait_ge(tail_ready, 8 * l + h + 1)
                    nc.vector.tensor_tensor(stick[:, s, 2, :], stick[:, s, 2, :], wk[:, s, 0:384],
                                            ALU.subtract).then_inc(stick_arg, 1)
                    dve.wait_ge(stick_exp, 8 * l + h + 1)
                    if h >= 2:
                        dve.wait_ge(pv_done, 24 * l + 16 + h - 1)
                    nc.vector.tensor_tensor(stick[:, s, 3, :], stick[:, s, 2, :], cmask,
                                            ALU.mult).then_inc(stick_ready, 1)

                for h in range(HEADS):
                    s = h % 2
                    z = wk[:, 2 + s, 0:384]
                    dve.wait_ge(z_log, 8 * l + h + 1)
                    link(nc.vector.scalar_tensor_tensor(stick[:, s, 1, :], z, 0.0, stick[:, s, 0, :], ALU.max,
                                                        ALU.add))
                    nc.vector.tensor_tensor(stick[:, s, 1, :], stick[:, s, 1, :], cmask, ALU.mult)
                    nc.vector.scalar_tensor_tensor(stick[:, s, 2, :], z, 0.0, stick[:, s, 0, :], ALU.min,
                                                   ALU.subtract).then_inc(z_read, 1)
                    if h:
                        stick_tail(h - 1)
                        gate(13 + h)
                    else:
                        dve.wait_ge(z_read, 8 * l + 1)
                stick_tail(HEADS - 1)
                gate(21)
                gate(22)
                dve.wait_ge(pv_done, 24 * l + 24)
                for b in range(2):
                    e = nc.vector.tensor_copy(ytok[:, b, 2, :], wk[:, 4 + b, :])
                e.then_inc(y_read, 1)
                gate(23)
                for n in range(6):
                    br, b = n // 2, n % 2
                    dve.wait_ge(y_hi, 6 * l + n + 1)
                    nc.vector.tensor_tensor(mov_lo[:, 4 * br:4 * br + 4, b * P:(b + 1) * P],
                                            wk[:, n, :].rearrange("p (c t) -> p c t", c=4),
                                            mov_hi[:, 4 * br:4 * br + 4, b * P:(b + 1) * P].bitcast(f32),
                                            ALU.subtract).then_inc(mov_ready, 1)
                wait_alone(dve, merged_zero, l + 1)
                with dve.Fori(0, 3) as br:
                    dve.wait_ge(sigmoids, 3 * l + br + 1)
                    for j in range(4):
                        t = L0 + br * 4 + (T_BR + j)
                        rest_of(t + 2, j + 2)
                        dve.wait_ge(tile_done, t + 3)
                        n = l * N_BR + br * 4 + j
                        nc.vector.tensor_tensor(
                            gated[:, j % 2, :].rearrange("p (o s) -> p o s", o=2),
                            pj[j % 2][:, :].rearrange("p (o s) -> p o s", o=2),
                            projT[:, bass.ds(br * 8 + (N_QKV + 2 * j), 2), :], ALU.mult).then_inc(out_free, 1)
                        dve.wait_ge(out_free, l * OUTS + br * 4 + (O_BR + j + 3))
                        nc.vector.tensor_tensor(merged[:, 2 * j:2 * j + 2, :], merged[:, 2 * j:2 * j + 2, :],
                                                gated[:, j % 2, :].rearrange("p (o s) -> p o s", o=2),
                                                ALU.add).then_inc(br_add, 1)
                        dve.wait_ge(br_add, n + 1)
                for k in range(KC):
                    dve.wait_ge(h_hi, l * HI_READY + (HI_MERGED + k + 1))
                    nc.vector.tensor_tensor(mov_lo[:, k, :], merged[:, k, :], mov_hi[:, k, :].bitcast(f32),
                                            ALU.subtract).then_inc(mov_ready, 1)
                dve.wait_ge(mov_ready, l * M_READY + M_2)
                dve.sem_inc(keys_free, 1)
                with dve.Fori(0, N_OUT // 4) as i:
                    for j in range(4):
                        t = L0 + i * 4 + (T_OUT + j)
                        rest_of(t + 2, j + 2)
                        dve.wait_ge(tile_done, t + 3)
                        xk = x[:, bass.ds(i * 4 + j, 1), :].squeeze(1)
                        nc.vector.scalar_tensor_tensor(xk, pj[j % 2][:, 0:SEQ], mod[:, bass.ds(i * 4 + (MG1 + j), 1)],
                                                       xk, ALU.mult, ALU.add).then_inc(out_free, 1)
                norm(1, sq2)
                with dve.Fori(0, N_QUERY // 4) as i:
                    for j in range(4):
                        rest_of(L0 + i * 4 + (T_QUERY + 2 + j), j + 2)
                early = [0]

                def split_early(n):
                    for _ in range(min(n, EARLY - early[0])):
                        j = early[0]
                        rest_of(L0 + (T_PEER + 2 + j), j + 2)
                        early[0] += 1

                split_early(1)
                dve.wait_ge(q_rr, l + 1)
                nc.vector.scalar_tensor_tensor(queryT, queryT, par[:, PQP:PQP + 1], sq2, ALU.mult,
                                               ALU.mult).then_inc(q_norm, 1)
                split_early(1)

                def step(ins):
                    ins.then_inc(dve_step, 1)
                    n_link[0] += 1
                    return n_link[0]

                done = None
                for u in range(17):
                    halves = []
                    if u < 16:
                        if u % 2 == 0:
                            wait_alone(dve, s_copied, 8 * l + u // 2 + 1)
                        for n in range(2):
                            halves.append((score[:, u, n * 128:(n + 1) * 128], rest[:, n, 0:128],
                                           sel_v[:, u % 2, n, :], sel_i[:, u, n, :]))
                    if done is not None:
                        v, ts, tp_ = sel_v[:, (u - 1) % 2], top_s[:, u - 1, :], top_p[:, u - 1, :]
                        dve.wait_ge(dve_step, done)
                        add = step(nc.vector.tensor_tensor(cand.rearrange("p (a b) -> p a b", a=16),
                                                           v[:, 0, :].unsqueeze(2).to_broadcast([P, 16, 16]),
                                                           v[:, 1, :].unsqueeze(1).to_broadcast([P, 16, 16]), ALU.add))
                    first = [step(nc.vector.max(v8[:, 0:8], sc)) for sc, _, v8, _ in halves]
                    split_early(1)
                    if done is not None:
                        dve.wait_ge(dve_step, add)
                        top = step(nc.vector.max(ts[:, 0:8], cand))
                    if halves:
                        dve.wait_ge(dve_step, first[1])
                        removed = [step(nc.vector.match_replace(r, v8[:, 0:8], sc, -3e38)) for sc, r, v8, _ in halves]
                    split_early(1)
                    if done is not None:
                        dve.wait_ge(dve_step, top)
                        top = step(nc.vector.match_replace(candr, ts[:, 0:8], cand, -3e38))
                        nc.vector.max_index(tp_[:, 0:8], ts[:, 0:8], cand)
                    split_early(u % 2)
                    if halves:
                        dve.wait_ge(dve_step, removed[1])
                        second = [step(nc.vector.max(v8[:, 8:16], r)) for _, r, v8, _ in halves]
                    if done is not None:
                        dve.wait_ge(dve_step, top)
                        top = step(nc.vector.max(ts[:, 8:16], candr))
                    for sc, _, v8, i8 in halves:
                        nc.vector.max_index(i8[:, 0:8], v8[:, 0:8], sc)
                    split_early(1)
                    if halves:
                        dve.wait_ge(dve_step, second[1])
                        for _, r, v8, i8 in halves:
                            done = step(nc.vector.max_index(i8[:, 8:16], v8[:, 8:16], r))
                    if u:
                        dve.wait_ge(dve_step, top)
                        top = step(nc.vector.max_index(tp_[:, 8:16], ts[:, 8:16], candr))
                dve.wait_ge(dve_step, top)
                gs, gr = gsum[:, 0, :], gsum[:, 1, :]
                link(nc.vector.tensor_copy(gs, top_s[:, :, 0:1].squeeze(2)))
                nc.vector.tensor_tensor(top_s, top_s, gs.unsqueeze(2).to_broadcast([P, 16, 16]),
                                        ALU.subtract).then_inc(g_arg, 1)
                tp = top_p.rearrange("p u k -> p (u k)")
                nc.vector.tensor_scalar(pos_i[:, 0, :], tp, 4, None, ALU.logical_shift_right)
                link(nc.vector.tensor_scalar(pos_i[:, 1, :], tp, 15, None, ALU.bitwise_and))
                nc.vector.tensor_copy(sel_if, sel_i)
                link(nc.vector.tensor_copy(pos_f, pos_i))
                split_early(1)
                for n in range(2):
                    for b in range(2):
                        hot = pick.rearrange("p (c j) -> p c j", j=16)
                        pf = pos_f[:, n, b * 128:(b + 1) * 128]
                        one_hots = step(nc.vector.tensor_tensor(
                            hot, pf.unsqueeze(2).to_broadcast([P, 128, 16]),
                            iota[:, 0:16].unsqueeze(1).to_broadcast([P, 128, 16]), ALU.is_equal))
                        split_early(2 if n + b else 1)
                        dve.wait_ge(dve_step, one_hots)
                        hot4 = pick.rearrange("p (u k j) -> p u k j", u=8, k=16)
                        picked = step(nc.vector.tensor_tensor(
                            hot4, hot4, sel_if[:, b * 8:b * 8 + 8, n, :].unsqueeze(2).to_broadcast([P, 8, 16, 16]),
                            ALU.mult))
                        split_early(1)
                        dve.wait_ge(dve_step, picked)
                        link(nc.vector.tensor_reduce(idx_tok[:, n, b * 128:(b + 1) * 128], hot, AX.X, ALU.add))
                        split_early(2 if n and b else 1)
                assert early[0] <= EXP_AT
                split_early(EXP_AT - early[0])
                dve.wait_ge(g_exp, l + 1)
                link(nc.vector.tensor_reduce(gs, top_s, AX.X, ALU.add))
                link(nc.vector.reciprocal(gr, gs))
                nc.vector.tensor_tensor(top_s, top_s, gr.unsqueeze(2).to_broadcast([P, 16, 16]),
                                        ALU.mult).then_inc(route_ready, 1)
                split_early(ROUTE_AT - early[0])
                for n, dst in enumerate((idx1T, idx2T, gateT)):
                    for b in range(2):
                        dve.wait_ge(route_tr, 6 * l + 2 * n + b + 1)
                        nc.vector.tensor_copy(dst[:, b * P:(b + 1) * P], wk[:, 2 * n + b, 0:P]).then_inc(route_in, 1)
                split_early(EARLY)
                wait_alone(dve, route_in, 6 * l + 6)

                def one_hot(group, q):
                    dve.wait_ge(hot_used, l * SEQ + group * 4 + 4)
                    j = q % 2
                    if q == 3:
                        nc.vector.tensor_tensor(
                            onehot_b[:, 4:8, :], iota.unsqueeze(1).to_broadcast([P, 4, NKEYS]),
                            idx2T[:, bass.ds(group * 4, 4)].unsqueeze(2).to_broadcast([P, 4, NKEYS]),
                            ALU.is_equal)
                    for r in range(4):
                        nc.vector.tensor_scalar(onehot_a[:, 4 * j + r, :], iota, idx1T[:, bass.ds(group * 4 + r, 1)],
                                                gateT[:, bass.ds(group * 4 + r, 1)], ALU.is_equal,
                                                ALU.mult).then_inc(hot_a, 1)

                def times_g(group, j):
                    dve.wait_ge(hot_used, l * SEQ + group * 4 + 12)
                    a = arena[:, 0:EARLY, bass.ds(group * 4, 4)].rearrange("p i t -> p t i")
                    nc.vector.tensor_tensor(a, wk[:, 2 + j, :].rearrange("p (t i) -> p t i", t=4)[:, :, 0:EARLY], a,
                                            ALU.mult).then_inc(g_times, 1)

                dve.wait_ge(out_free, l * OUTS + (O_PEER + EARLY + 2))
                one_hot(l * 0, 0)
                one_hot(l * 0 + 1, 1)
                with dve.Fori(0, ADA_LATE // 2) as i:
                    for q in range(4):
                        one_hot(i * 4 + (q + 2), (q + 2) % 4)
                        times_g(i * 4 + q, q)
                    modulation(late_used, l * (2 * ADA_LATE) + i * 4 + 6, i + ADA_QKV // 2,
                               mod[:, bass.ds(i * 2 + MG2, 2)])
                with dve.Fori(ADA_LATE // 2, SEQ // 16 - 1) as i:
                    for q in range(4):
                        one_hot(i * 4 + (q + 2), (q + 2) % 4)
                        times_g(i * 4 + q, q)
                for q in range(4):
                    if q < 2:
                        one_hot(l * 0 + (SEQ // 4 - 2 + q), q + 2)
                    times_g(l * 0 + (SEQ // 4 - 4 + q), q)
                dve.wait_ge(mod_read, (l + 1) * ADA_GROUPS + 4)
                nc.vector.tensor_tensor(mod[:, MG2:MS1], mod[:, MG2:MS1], par[:, MG2:MS1], ALU.add)

                def w_rests(n, s, done):
                    dve.wait_ge(w_head, l * NKEYS + done)
                    nc.vector.tensor_tensor(w_lo[:, s, :], group_of(n), w_hi[:, s, :].bitcast(f32),
                                            ALU.subtract).then_inc(w_rest, 1)

                dve.wait_ge(g_free, l * (SEQ // 4) + (SEQ // 4 + 4))
                for n in range(3):
                    w_rests(n, n, n + 1)
                with dve.Fori(0, BOTH // 4) as i:
                    for j in range(4):
                        t = L0 + i * 8 + (T_BOTH + 2 * j)
                        rest_of(t + 2, 2 * j + 2)
                        dve.wait_ge(out_free, l * OUTS + i * 4 + (O_PEER + EARLY + j + 3))
                        g = group_of(i * 4 + (EARLY + j))
                        nc.vector.tensor_tensor(g, act_g[:, j % 2, :], g, ALU.mult).then_inc(w_made, 1)
                        w_rests(i * 4 + (j + 3), (j + 3) % 4, i * 4 + (j + 4))
                        rest_of(t + 3, 2 * j + 3)
                wait_alone(dve, w_made, (l + 1) * BOTH)
                with dve.Fori(0, EARLY // 4 - 1) as i:
                    for j in range(4):
                        t = L0 + i * 4 + (T_DOWN + j)
                        rest_of(t + 2, j + 2)
                        w_rests(i * 4 + (BOTH + j + 3), (j + 3) % 4, i * 4 + (BOTH + j + 4))
                t = L0 + TILES - 4
                rest_of(t + 2, 2)
                w_rests(NKEYS - 1, 3, NKEYS)
                rest_of(t + 3, 3)
                dve.wait_ge(tile_done, L0 + TILES + 2)
                for e in range(2):
                    nc.vector.tensor_copy(ftok[:, 0, e * 512:(e + 1) * 512], wk[:, 2 + e, :]).then_inc(f_tok, 1)
                for k in range(KC):
                    if k % 2 == 0:
                        dve.wait_ge(f_tr, 4 * l + k // 2 + 1)
                    nc.vector.scalar_tensor_tensor(
                        x[:, k, :], wk[:, F_BANK[k // 2], (k % 2) * SEQ:(k % 2 + 1) * SEQ],
                        mod[:, MG2 + k:MG2 + k + 1], x[:, k, :], ALU.mult, ALU.add).then_inc(x_ready, 1)
                dve.wait_ge(x_ready, l * KC + 2 * KC)
                dve.sem_inc(arena_free, 1)

        @block.tensor
        def _(pe):
            def product(out, w_h, w_l, m_h, m_l, first, last):
                pe.matmul(out, w_h, m_h, start=first, stop=False)
                pe.matmul(out, w_h, m_l, start=False, stop=False)
                return pe.matmul(out, w_l, m_h, start=False, stop=last)

            def chunk(j, k):
                return hi[j % SPLIT][:, k * P:(k + 1) * P], lo[j % SPLIT][:, k * P:(k + 1) * P]

            pe.sem_inc(tile_done, 2)
            pe.sem_inc(out_free, 2)
            pe.sem_inc(hot_used, 8)
            pe.sem_inc(g_free, 4)
            pe.sem_inc(ada_used, 2)
            pe.sem_inc(late_used, 2)

            def columns(out, tile, first_chunk, chunks):
                for k in range(chunks):
                    c = first_chunk + k
                    last = pe.matmul(out, c_tmp[:, c:c + 1].to_broadcast([P, P]), tile[:, k * 256:(k + 1) * 256],
                                     start=c == 0, stop=c == KC - 1)
                return last

            pe.wait_ge(c_ready, 1)
            for n in range(ADA_FIRST):
                if n % 4 == 0:
                    pe.wait_ge(front_loaded[n // 4], 16)
                last = columns(wk[:, n // 4, n // 2 % 2 * 256:n // 2 % 2 * 256 + 256], ada_front[:, n, :],
                               n % 2 * 4, 4)
                if n % 4 == 3:
                    last.then_inc(front_used, 1)
            with pe.Fori(0, DEPTH) as l:
                L0 = l * TILES

                def squares(n, sq, k):
                    pe.wait_ge(sq_ready, 2 * KC * l + (n * KC + k + 1))
                    last = pe.matmul(wk[:, 0, 0:SEQ], ones, sq[:, k, :], start=k == 0, stop=k == KC - 1)
                    if k == KC - 1:
                        last.then_inc(ss_ready, 1)

                def project(t, j, o, bank, chunks=None):
                    pe.wait_ge(lo_done, t + 1)
                    pe.wait_ge(out_free, l * OUTS + o + 1)
                    for k in range(KC):
                        if chunks is not None:
                            pe.wait_ge(mov_ready, l * M_READY + (chunks + k + 1))
                        last = product(pj[bank][:, 0:SEQ], *chunk(j, k), mov_hi[:, k, :], mov_lo[:, k, :],
                                       k == 0, k == KC - 1)
                    return last

                pe.wait_ge(mod_read, l * ADA_GROUPS + 4)
                for k in range(KC):
                    squares(0, sq, k)
                wait_alone(pe, rstd_ready, 2 * l + 1)
                with pe.Fori(0, N_QKV // 8) as i:
                    for j in range(8):
                        project(L0 + i * 8 + j, j, i * 8 + j, j % 2, None if j else 0).then_inc(tile_done, 1)
                        if j % 4 == 3:
                            continue
                        n = 3 * (j // 4) + j % 4
                        pe.wait_ge(ada_loaded[n % 2], l * (ADA_QKV * 8) + i * 48 + 16 * (n // 2 + 1))
                        if n % 2 == 0:
                            pe.wait_ge(mod_read, l * ADA_GROUPS + i * 3 + (n // 2 + 4))
                        columns(wk[:, 1, 0:256], ada_slot[:, n % 2, :], n % 2 * 4, 4).then_inc(ada_used, 1)

                def gate(n):
                    project(L0 + (T_GATE + n), n, O_GATE + n, n % 2).then_inc(tile_done, 1)

                pe.wait_ge(out_free, l * OUTS + (O_GATE + 2))
                pe.wait_ge(mod_read, l * ADA_GROUPS + (ADA_QKV // 2 + 4))
                for b in range(2):
                    for n, t in enumerate(V_TILES):
                        c = b * 1536 + n * P
                        last = pe.transpose(wkf[:, c:c + P], projT[:, t, b * P:(b + 1) * P], ident)
                    last.then_inc(vtr, 1)
                pe.wait_ge(tables, 32 * l + 32)
                for g, (t0, n) in enumerate(((QA, 5), (QB, 8))):
                    gate(g)
                    pe.wait_ge((qk_sq, qk_sq2)[g], l + 1)
                    if g == 0:
                        pe.wait_ge(vtok_in, 2 * l + 2)
                    else:
                        pe.wait_ge(qk_rr, 2 * l + 1)
                    for k in range(n):
                        last = pe.matmul(wkf[:, k * SEQ:(k + 1) * SEQ], blk, (sq, merged)[g][:, k, :], start=True, stop=True)
                    last.then_inc(qk_ss, 1)
                gate(2)
                gate(3)
                pe.wait_ge(qk_rr, 2 * l + 2)
                for br in range(2):
                    pe.wait_ge(qk_done, 2 * l + br + 1)
                    if br:
                        pe.wait_ge(f_ready, l + 1)

                    def scores(h):
                        n = 8 * br + h
                        if n >= 2:
                            pe.wait_ge(score_read, 16 * l + n - 1)
                        if br == 0:
                            o = (h // 4) * HD
                            q, k = projT[o:o + HD, QA + h % 4, :], projT[o:o + HD, KA, :]
                        else:
                            o = (h % 2) * HD
                            q, k = projT[o:o + HD, QB + h // 2, :], projT[o:o + HD, KB + h // 2, :]
                        s = wk[:, 2 + h % 2, :]
                        hot = ident[0:HEADS, h:h + 1].to_broadcast([HEADS, P])
                        for q0, nk, c0 in ((0, P, 0), (P, 2 * P, P)):
                            last = pe.matmul(s[:, c0:c0 + nk], q[:, q0:q0 + P], k[:, 0:nk], start=True, stop=br == 0)
                            if br:
                                last = pe.matmul(s[:, c0:c0 + nk], hot, fl[:, 3, 0:nk], start=False, stop=True)
                        last.then_inc(score_ready, 1)

                    def turn(h):
                        n = 8 * br + h
                        pe.wait_ge(prob_ready, 16 * l + n + 1)
                        if n >= 2:
                            pe.wait_ge(pt_copied, 16 * l + n - 1)
                        for c in range(3):
                            last = pe.transpose(wk[:, h % 2, c * P:(c + 1) * P], prob[:, h, c * P:(c + 1) * P], ident)
                        last.then_inc(ptr_ready, 1)

                    def values(h):
                        n = 8 * br + h
                        pe.wait_ge(pt_copied, 16 * l + n + 1)
                        if h == 0 and br:
                            pe.wait_ge(y_read, 3 * l + 1)
                        v = (h // 4) * HD if br == 0 else P + h * HD
                        o = slice(h * HD, (h + 1) * HD)
                        pt = probT[:, h % 2, :]
                        pe.matmul(wk[:, 4, o], pt[:, 0:P], vtok[:, 0, v:v + HD], start=True, stop=True)
                        pe.matmul(wk[:, 5, o], pt[:, P:2 * P], vtok[:, 0, v:v + HD], start=True, stop=False)
                        pe.matmul(wk[:, 5, o], pt[:, 2 * P:3 * P], vtok[:, 1, v:v + HD], start=False,
                                  stop=True).then_inc(pv_done, 1)

                    for h in range(HEADS):
                        scores(h)
                        if h == 3:
                            gate(4 + 4 * br)
                    for g in ((5,), (9, 10))[br]:
                        gate(g)
                    turn(0)
                    for h in range(HEADS):
                        if h + 1 < HEADS:
                            turn(h + 1)
                        values(h)
                        if h in (1, 4):
                            gate((6, 11)[br] + h // 3)
                gate(13)
                def logits(h):
                    if h >= 2:
                        pe.wait_ge(z_read, 8 * l + h - 1)
                    else:
                        pe.wait_ge(score_read, 16 * l + 16)
                        pe.wait_ge(pt_copied, 16 * l + 16)
                    o = (h % 2) * HD
                    q, k = projT[o:o + HD, QC + h // 2, :], projT[o:o + HD, KCT + h // 2, :]
                    z = wk[:, 2 + h % 2, :]
                    pe.matmul(z[:, 0:SEQ], k[:, 0:P], q, start=True, stop=True)
                    pe.matmul(z[:, SEQ:SEQ + P], k[:, P:2 * P], q[:, P:2 * P], start=True,
                              stop=True).then_inc(z_ready, 1)

                def tails(h):
                    pe.wait_ge(z_read, 8 * l + h + 1)
                    if h >= 2:
                        pe.wait_ge(stick_arg, 8 * l + h - 1)
                    t = wk[:, h % 2, :]
                    sp_ = stick[:, h % 2, 1, :]
                    pe.matmul(t[:, 0:P], tri, sp_[:, 0:P], start=True, stop=True)
                    pe.matmul(t[:, P:2 * P], tri, sp_[:, P:2 * P], start=True, stop=False)
                    pe.matmul(t[:, P:2 * P], ones, sp_[:, 2 * P:3 * P], start=False, stop=True)
                    pe.matmul(t[:, 2 * P:3 * P], tri, sp_[:, 2 * P:3 * P], start=True,
                              stop=True).then_inc(tail_ready, 1)

                def stick_values(h):
                    pe.wait_ge(stick_ready, 8 * l + h + 1)
                    if h == 0:
                        pe.wait_ge(y_read, 3 * l + 2)
                    v = P + 512 + h * HD
                    o = slice(h * HD, (h + 1) * HD)
                    a = stick[:, h % 2, 3, :]
                    pe.matmul(wk[:, 4, o], a[:, 0:P], vtok[:, 0, v:v + HD], start=True, stop=True)
                    pe.matmul(wk[:, 5, o], a[:, P:2 * P], vtok[:, 0, v:v + HD], start=True, stop=False)
                    pe.matmul(wk[:, 5, o], a[:, 2 * P:3 * P], vtok[:, 1, v:v + HD], start=False,
                              stop=True).then_inc(pv_done, 1)

                logits(0)
                for h in range(HEADS):
                    if h + 1 < HEADS:
                        logits(h + 1)
                    tails(h)
                    gate(14 + h)
                    if h:
                        stick_values(h - 1)
                gate(22)
                stick_values(HEADS - 1)
                gate(23)
                pe.wait_ge(y_read, 3 * l + 3)
                for n in range(6):
                    br, b = n // 2, n % 2
                    for c in range(4):
                        last = pe.transpose(wk[:, n, c * P:(c + 1) * P], ytok[:, b, br, c * P:(c + 1) * P], ident)
                    last.then_inc(ytr, 1)
                for n in range(N_BR):
                    br, j = n // 4, n % 4
                    pe.wait_ge(mov_ready, l * M_READY + (M_MIX + 2 * br + 2))
                    pe.wait_ge(lo_done, L0 + (T_BR + n + 1))
                    pe.wait_ge(out_free, l * OUTS + (O_BR + n + 1))
                    for o in range(2):
                        for k in range(4):
                            last = product(pj[j % 2][:, o * SEQ:(o + 1) * SEQ], *chunk(j, 4 * o + k),
                                           mov_hi[:, br * 4 + k, :], mov_lo[:, br * 4 + k, :], k == 0, k == 3)
                    last.then_inc(tile_done, 1)
                for k in range(N_OUT):
                    project(L0 + (T_OUT + k), k, O_OUT + k, k % 2, None if k else M_MERGED).then_inc(tile_done, 1)
                    if k:
                        squares(1, sq2, k - 1)
                squares(1, sq2, KC - 1)
                wait_alone(pe, rstd_ready, 2 * l + 2)
                with pe.Fori(0, N_QUERY // 4) as i:
                    for j in range(4):
                        project(L0 + i * 4 + (T_QUERY + j), j, i * 4 + (O_QUERY + j), j % 2,
                                None if j else M_2).then_inc(tile_done, 1)
                pe.wait_ge(rstd_ready, 2 * l + 2)
                def early_tile(j):
                    project(L0 + (T_PEER + j), j, O_PEER + j, j % 2).then_inc(tile_done, 1)

                early_tile(0)
                pe.wait_ge(q_sq, l + 1)
                for k in range(KC):
                    last = pe.matmul(wkf[:, k * SEQ:(k + 1) * SEQ], ones, sq2[:, k, :], start=True, stop=True)
                last.then_inc(q_ss, 1)
                early_tile(1)
                pe.wait_ge(q_norm, l + 1)
                pe.wait_ge(keys_in, 16 * l + 16)
                for u in range(16):
                    b, h = u // 8, u % 8
                    if u >= 12 and u % 2 == 0:
                        pe.wait_ge(s_copied, 8 * l + u // 2 - 5)
                    pe.matmul(wk[:, (u // 2) % 6, (u % 2) * 256:(u % 2 + 1) * 256], queryT[:, h, b * P:(b + 1) * P],
                              skeys[:, h, :], start=True, stop=True).then_inc(s_ready, 1)
                early_tile(2)
                early_tile(3)
                with pe.Fori(1, ROUTE_AT // 4) as i:
                    for j in range(4):
                        project(L0 + i * 4 + (T_PEER + j), j, i * 4 + (O_PEER + j), j % 2).then_inc(tile_done, 1)
                pe.wait_ge(route_ready, l + 1)
                pe.wait_ge(s_copied, 8 * l + 8)
                tsf = top_s.rearrange("p u k -> p (u k)")
                for n, src in enumerate((idx_tok[:, 0, :], idx_tok[:, 1, :], tsf)):
                    for b in range(2):
                        pe.transpose(wk[:, 2 * n + b, 0:P], src[:, b * P:(b + 1) * P], ident).then_inc(route_tr, 1)
                for j in range(EARLY - ROUTE_AT):
                    project(L0 + (T_PEER + ROUTE_AT + j), j, O_PEER + ROUTE_AT + j, j % 2).then_inc(tile_done, 1)
                wait_alone(pe, route_in, 6 * l + 6)
                def tokens(i, modulate):
                    for r in range(16):
                        pe.wait_ge(hot_a, l * SEQ + i * 16 + (r + 1))
                        if r % 4 == 0 and r < 12:
                            pe.wait_ge(hot_b, l * HOT_B + i * 3 + (r // 4 + 1))
                        if r % 4 == 0:
                            pe.wait_ge(g_free, l * (SEQ // 4) + i * 4 + (r // 4 + 1))
                        pe.matmul(wk[:, 2 + r // 4, (r % 4) * P:(r % 4 + 1) * P], onehot_a[:, r % 8, :],
                                  onehot_b[:, r % 8, :].bitcast(f32), start=True, stop=True).then_inc(hot_used, 1)
                        if modulate and r % 4 == 3:
                            q = r // 4
                            pe.wait_ge(late_loaded[q % 2], l * (ADA_LATE * 16) + i * 32 + 16 * (q // 2 + 1))
                            if q == 0:
                                pe.wait_ge(mod_read, l * ADA_GROUPS + i + (ADA_QKV // 2 + 4))
                            columns(wk[:, 1, 0:256], ada_late[:, q % 2, :], 2 * q, 2).then_inc(late_used, 1)

                with pe.Fori(0, ADA_LATE // 2) as i:
                    tokens(i, True)
                with pe.Fori(ADA_LATE // 2, SEQ // 16) as i:
                    tokens(i, False)

                def down(t, j, n, s, last_group=False):
                    pe.wait_ge(lo_done, t + 1)
                    pe.wait_ge(w_rest, l * NKEYS + n + 1)
                    vh, vl = hi[j % SPLIT], lo[j % SPLIT]
                    for b in range(2):
                        wh, wl = w_hi[:, s, b * P:(b + 1) * P], w_lo[:, s, b * P:(b + 1) * P]
                        for e in range(2):
                            last = product(wk[:, 2 + 2 * b + e, :], wh, wl, vh[:, e * 512:(e + 1) * 512],
                                           vl[:, e * 512:(e + 1) * 512], False, last_group)
                    last.then_inc(tile_done, 1)

                pe.wait_ge(g_free, l * (SEQ // 4) + (SEQ // 4 + 4))
                for c in range(4):
                    pe.matmul(wk[:, 2 + c, :], zero, const[:, 0:512], start=True, stop=False)
                with pe.Fori(0, BOTH // 4) as i:
                    for j in range(4):
                        t = L0 + i * 8 + (T_BOTH + 2 * j)
                        project(t, 2 * j, i * 4 + (O_PEER + EARLY + j), j % 2).then_inc(tile_done, 1)
                        down(t + 1, 2 * j + 1, i * 4 + j, j)
                with pe.Fori(0, EARLY // 4 - 1) as i:
                    for j in range(4):
                        down(L0 + i * 4 + (T_DOWN + j), j, i * 4 + (BOTH + j), j)
                for j in range(4):
                    down(L0 + (TILES - 4 + j), j, NKEYS - 4 + j, j, j == 3)
                for k in range(KC):
                    if k % 4 == 0:
                        pe.wait_ge(f_tok, 2 * l + (k // 4 + 1))
                        pe.wait_ge(f_tok2, 2 * l + (k // 4 + 1))
                    for b in range(2):
                        c = (k % 2) * SEQ + b * P
                        last = pe.transpose(wk[:, F_BANK[k // 2], c:c + P], ftok[:, b, k * P:(k + 1) * P], ident)
                    if k % 2:
                        last.then_inc(f_tr, 1)


def _rows(w):
    k, n = w.shape[0] // P, w.shape[1] // P
    return w.reshape(k, P, n, P).transpose(2, 1, 0, 3).reshape(n, P, k * P)


def _lay_out(np, i):
    qh = [h for t in range(4) for h in (t, t + 4)]
    tiles = []
    for l in range(DEPTH):
        w = i["w_in"][l]
        cut = np.split(w, [512, 640, 768, 1280, 1792, 2304, 2312, 2824, 3336, 3848], axis=1)
        qa, ka, va, qb, kb, vb, fb, qc, kc, vc, gates = cut
        qa = qa.reshape(D, 8, HD)[:, qh].reshape(D, 512)
        fb = np.concatenate([fb, np.zeros((D, P - 8), fb.dtype)], 1)
        blank = np.zeros((D, P), w.dtype)
        tiles.append(_rows(np.concatenate([qa, ka, va, qb, kb, vb, fb, qc, kc, vc, blank], 1)))
        tiles.append(_rows(gates))
        for b in "abc":
            wo = i["w_out_" + b][l]
            t = wo.reshape(4, P, 4, 2, P).transpose(2, 1, 3, 0, 4)
            tiles.append(t.reshape(4, P, 1024))
        tiles.append(_rows(i["w_out"][l]))
        tiles.append(_rows(i["w_query"][l]))
        u = i["expert_u"][l].reshape(NKEYS, NKEYS, KC, P).transpose(1, 3, 2, 0).reshape(NKEYS, P, 1024)
        v = i["expert_v"][l].reshape(NKEYS, NKEYS, D).transpose(1, 0, 2)
        mix = np.empty((2 * BOTH, P, 1024), u.dtype)
        mix[0::2] = u[EARLY:]
        mix[1::2] = v[:BOTH]
        tiles += [u[:EARLY], mix, v[BOTH:]]
    stream = np.concatenate(tiles)
    ada = i["w_ada"].reshape(DEPTH, 2, 4, P, ADA_GROUPS, 256).transpose(0, 4, 1, 3, 2, 5)
    ada = ada.reshape(DEPTH * N_ADA, P, 1024)
    front = ada[:ADA_FIRST].transpose(1, 0, 2)
    ada = np.concatenate([ada[ADA_FIRST:], np.zeros((ADA_FIRST, P, 1024), ada.dtype)])
    par = np.zeros((P, DEPTH, NPAR), np.float32)
    for l in range(DEPTH):
        q = par[:, l]
        q[:, PB_ADA:PB_ADA + 48] = np.roll(i["b_ada"][l].reshape(48, P).T, -ADA_FIRST, axis=1)
        q[:, PG1:PG1 + 8] = i["norm1_g"][l].reshape(8, P).T
        q[:, PG2:PG2 + 8] = i["norm2_g"][l].reshape(8, P).T
        q[:, PBG:PBG + 24] = i["b_gate"][l].reshape(24, P).T
        for c, n in ((PQA, "q_norm_a"), (PKA, "k_norm_a"), (PQB, "q_norm_b"), (PKB, "k_norm_b")):
            q[:, c] = np.concatenate([i[n][l], i[n][l]])
        q[:, PQP] = i["q_norm_peer"][l]
        q[:, PSINK:PSINK + 8] = i["sinks"][l]
        q[0:8, PBF] = i["b_forget"][l]
    r = np.arange(P)
    const = np.zeros((P, NCONST), np.float32)
    const[:, C_ID:C_ID + P] = np.eye(P)
    const[:, C_ONE:C_ONE + P] = 1
    mix = np.zeros((P, NMIX), np.float32)
    mix[:, X_BLK:X_BLK + P] = (r[:, None] // HD) == (r[None] // HD)
    mix[:, X_TRI:X_TRI + P] = r[:, None] > r[None]
    const[:, C_IOTA:C_IOTA + P] = r[None]
    before = (r[:, None] < r[None]).astype(np.float32)
    mix[:, X_CM:X_CM + 384] = np.concatenate([before, np.ones((P, P)), before], 1)
    late = np.where(r[None] <= r[:, None], 0, NEG)
    mix[:, X_BT:X_BT + 384] = np.concatenate([late, np.zeros((P, P)), late], 1)
    const[:, C_EPS] = EPS
    chunk = r // 64
    own = np.where(chunk[:, None] >= chunk[None], 0, NEG)
    prev = np.where((chunk[:, None] + 2 - chunk[None]) < 2, 0, NEG)
    d_own, d_prev = np.abs(r[:, None] - r[None]), r[:, None] - (r[None] - P)
    taba = np.zeros((P, HEADS, 384), np.float32)
    for h in range(HEADS):
        s = 2.0 ** -(h + 1)
        a, b = own - s * d_own, prev - s * d_prev
        taba[:, h] = np.concatenate([a, b, a], 1)
    keys = np.zeros((DEPTH, P, PEER_HEADS, 256), np.float32)
    keys[:, 0:64, :, 0:128] = i["sub_keys_1"].transpose(0, 3, 1, 2)
    keys[:, 64:128, :, 128:256] = i["sub_keys_2"].transpose(0, 3, 1, 2)
    xT = i["x"][0].reshape(SEQ, KC, P).transpose(2, 1, 0)
    cT = i["c"][0].reshape(KC, P).T
    return {"stream": stream, "par": par, "const": const, "mix": mix, "taba": taba, "keys": keys, "front": front, "ada": ada,
            "xT": xT, "cT": cT}


def kernel(**inputs):
    import numpy as np
    import concourse.bacc as bacc
    from concourse.bass_utils import run_bass_kernel_spmd

    arrays = {k: np.ascontiguousarray(v) for k, v in _lay_out(np, {k: np.asarray(v) for k, v in inputs.items()}).items()}
    nc = bacc.Bacc("TRN2", target_bir_lowering=False, num_devices=1)
    args = [nc.dram_tensor("in_" + n, a.shape, mybir.dt.float32, kind="ExternalInput").ap() for n, a in arrays.items()]
    out = nc.dram_tensor("out", (P, KC, SEQ), mybir.dt.float32, kind="ExternalOutput").ap()
    trunk(nc, *args, out)
    r = run_bass_kernel_spmd(nc, [{"in_" + n: a for n, a in arrays.items()}], core_ids=[0])
    got = r.results[0]["out"]
    return got.transpose(2, 1, 0).reshape(1, SEQ, D)
```
